# Optimizing a Trainium2 kernel written in Bass

```python
import jax
import jax.numpy as jnp
from jax import lax
import numpy as np
import math
import jax, jax.numpy as jnp

D_MODEL = 2048
BATCH = 1
SEQ = 256
DEPTH = 1

CHUNK = 64
MLSTM_HEADS = 8
MLSTM_WIDTH = D_MODEL
MLSTM_HEAD_DIM = MLSTM_WIDTH // MLSTM_HEADS
QK_CONV_WIDTH = 4
POOL_GROUPS = 4
POOL_WIDTH = D_MODEL // 2
POOL_GROUP_DIM = POOL_WIDTH // POOL_GROUPS
POOL_WINDOWS = (2, 4, 8, 16)
RMS_EPS = 1e-6
IN_SPLITS = (MLSTM_WIDTH, MLSTM_WIDTH, MLSTM_WIDTH, MLSTM_WIDTH, MLSTM_WIDTH,
             MLSTM_HEADS, MLSTM_HEADS, POOL_WIDTH, POOL_WIDTH, D_MODEL, D_MODEL)
IN_WIDTH = 5 * MLSTM_WIDTH + 2 * MLSTM_HEADS + 2 * POOL_WIDTH + 2 * D_MODEL


def _rmsnorm(x, w):
    xf = x.astype(jnp.float32)
    y = xf * lax.rsqrt(jnp.mean(xf * xf, axis=-1, keepdims=True) + RMS_EPS)
    return (y * w.astype(jnp.float32)).astype(x.dtype)

def _partition(t):
    parts, start = [], 0
    for width in IN_SPLITS:
        parts.append(t[..., start:start + width])
        start += width
    return parts

def _causal_depthwise_conv(x, w, b):
    c = x.shape[-1]
    y = lax.conv_general_dilated(
        x, w[:, None, :].astype(x.dtype), window_strides=(1,),
        padding=[(w.shape[0] - 1, 0)], dimension_numbers=('NWC', 'WIO', 'NWC'),
        feature_group_count=c)
    return y + b.astype(x.dtype)

def _to_chunks(t, nc):
    b = t.shape[0]
    t = t.reshape((b, nc, CHUNK) + t.shape[2:])
    t = jnp.moveaxis(t, 1, 0)
    return jnp.swapaxes(t, 2, 3)

def _mlstm_chunkwise(q, k, v, ig, lf):
    bsz, s, nh, d = q.shape
    nc = s // CHUNK
    causal = jnp.tril(jnp.ones((CHUNK, CHUNK), dtype=bool))
    xs = (_to_chunks(q, nc), _to_chunks(k, nc), _to_chunks(v, nc),
          _to_chunks(ig, nc), _to_chunks(lf, nc))

    def step(carry, inp):
        c_st, n_st, m_st = carry
        qc, kc, vc, ic, fc = inp
        b = jnp.cumsum(fc, axis=-1)
        log_d = b[..., :, None] - b[..., None, :] + ic[..., None, :]
        log_d = jnp.where(causal, log_d, -jnp.inf)
        log_inter = b + m_st[..., None]
        m_row = jnp.maximum(jnp.max(log_d, axis=-1), log_inter)
        p = jnp.exp(log_d - m_row[..., None]) * jnp.einsum('bhld,bhsd->bhls', qc, kc)
        w_inter = jnp.exp(log_inter - m_row)
        num = (jnp.einsum('bhls,bhsd->bhld', p, vc)
               + w_inter[..., None] * jnp.einsum('bhlk,bhkv->bhlv', qc, c_st))
        den = jnp.sum(p, axis=-1) + w_inter * jnp.einsum('bhlk,bhk->bhl', qc, n_st)
        h = num / jnp.maximum(jnp.abs(den), jnp.exp(-m_row))[..., None]
        g = b[..., -1]
        log_w = g[..., None] - b + ic
        m_new = jnp.maximum(g + m_st, jnp.max(log_w, axis=-1))
        decay = jnp.exp(g + m_st - m_new)
        w = jnp.exp(log_w - m_new[..., None])
        c_new = decay[..., None, None] * c_st + jnp.einsum('bhs,bhsk,bhsv->bhkv', w, kc, vc)
        n_new = decay[..., None] * n_st + jnp.einsum('bhs,bhsk->bhk', w, kc)
        return (c_new, n_new, m_new), h

    init = (jnp.zeros((bsz, nh, d, d), jnp.float32),
            jnp.zeros((bsz, nh, d), jnp.float32),
            jnp.zeros((bsz, nh), jnp.float32))
    _, hs = lax.scan(step, init, xs)
    hs = jnp.moveaxis(jnp.swapaxes(hs, 2, 3), 0, 1)
    return hs.reshape(bsz, s, nh, d)

def _multiscale_pool(u):
    bsz, s, _ = u.shape
    uf = u.astype(jnp.float32).reshape(bsz, s, POOL_GROUPS, POOL_GROUP_DIM)
    cs = jnp.concatenate(
        [jnp.zeros((bsz, 1, POOL_GROUPS, POOL_GROUP_DIM), jnp.float32),
         jnp.cumsum(uf, axis=1)], axis=1)
    t = jnp.arange(1, s + 1)[:, None]
    win = jnp.array(POOL_WINDOWS, dtype=jnp.int32)[None, :]
    lo = jnp.maximum(t - win, 0)
    grp = jnp.arange(POOL_GROUPS)[None, :]
    window_sum = cs[:, 1:] - cs[:, lo, grp]
    count = (t - lo).astype(jnp.float32)
    return window_sum / count[..., None] - uf

def first_inputs(seed: int = 0) -> dict:
    key = jax.random.key(seed)
    ks = jax.random.split(key, 16)
    f32 = jnp.float32
    nrm = lambda k, shape, scale: (jax.random.normal(k, shape, f32) * scale)
    x = jax.random.normal(ks[0], (BATCH, SEQ, D_MODEL), f32)
    norm_pre_w = 1.0 + nrm(ks[1], (DEPTH, D_MODEL), 0.05)
    w_in = nrm(ks[2], (DEPTH, D_MODEL, IN_WIDTH), D_MODEL ** -0.5)
    mlstm_i_bias = nrm(ks[3], (DEPTH, MLSTM_HEADS), 0.1)
    mlstm_f_bias = (jnp.linspace(3.0, 6.0, MLSTM_HEADS, dtype=f32)[None, :]
                    + nrm(ks[4], (DEPTH, MLSTM_HEADS), 0.1))
    qk_conv_w = nrm(ks[5], (DEPTH, QK_CONV_WIDTH, 2 * MLSTM_WIDTH), QK_CONV_WIDTH ** -0.5)
    qk_conv_b = nrm(ks[6], (DEPTH, 2 * MLSTM_WIDTH), 0.01)
    mlstm_norm_w = 1.0 + nrm(ks[7], (DEPTH, MLSTM_WIDTH), 0.05)
    pool_w = nrm(ks[8], (DEPTH, POOL_GROUPS, POOL_GROUP_DIM, POOL_GROUP_DIM), POOL_GROUP_DIM ** -0.5)
    pool_scale = 1.0 + nrm(ks[9], (DEPTH, POOL_WIDTH), 0.1)
    w_proj_mlstm = nrm(ks[10], (DEPTH, MLSTM_WIDTH, D_MODEL), MLSTM_WIDTH ** -0.5)
    w_proj_pool = nrm(ks[11], (DEPTH, POOL_WIDTH, D_MODEL), POOL_WIDTH ** -0.5)
    w_out = nrm(ks[12], (DEPTH, D_MODEL, D_MODEL), D_MODEL ** -0.5)
    norm_post_w = 1.0 + nrm(ks[13], (DEPTH, D_MODEL), 0.05)
    return {'x': x, 'norm_pre_w': norm_pre_w, 'w_in': w_in,
            'mlstm_i_bias': mlstm_i_bias, 'mlstm_f_bias': mlstm_f_bias,
            'qk_conv_w': qk_conv_w, 'qk_conv_b': qk_conv_b,
            'mlstm_norm_w': mlstm_norm_w, 'pool_w': pool_w, 'pool_scale': pool_scale,
            'w_proj_mlstm': w_proj_mlstm, 'w_proj_pool': w_proj_pool,
            'w_out': w_out, 'norm_post_w': norm_post_w}

def first_block(x, norm_pre_w, w_in, mlstm_i_bias, mlstm_f_bias, qk_conv_w, qk_conv_b,
              mlstm_norm_w, pool_w, pool_scale, w_proj_mlstm, w_proj_pool, w_out,
              norm_post_w):
    bsz, s, _ = x.shape
    f32 = jnp.float32
    for l in range(DEPTH):
        h = _rmsnorm(x, norm_pre_w[l])
        proj = jnp.einsum('bsd,de->bse', h, w_in[l])
        (q, k, v, o_g, z_a, i_pre, f_pre, u_b, z_b, g_a, g_b) = _partition(proj)

        qk = jax.nn.silu(_causal_depthwise_conv(jnp.concatenate([q, k], axis=-1),
                                                qk_conv_w[l], qk_conv_b[l]))
        q = qk[..., :MLSTM_WIDTH].astype(f32).reshape(bsz, s, MLSTM_HEADS, MLSTM_HEAD_DIM)
        k = qk[..., MLSTM_WIDTH:].astype(f32).reshape(bsz, s, MLSTM_HEADS, MLSTM_HEAD_DIM)
        v = v.astype(f32).reshape(bsz, s, MLSTM_HEADS, MLSTM_HEAD_DIM)
        q = q * (MLSTM_HEAD_DIM ** -0.5)
        log_i = i_pre.astype(f32) + mlstm_i_bias[l].astype(f32)
        log_f = jax.nn.log_sigmoid(f_pre.astype(f32) + mlstm_f_bias[l].astype(f32))
        h_t = _mlstm_chunkwise(q, k, v, log_i, log_f)
        h_t = h_t * lax.rsqrt(jnp.mean(h_t * h_t, axis=-1, keepdims=True) + RMS_EPS)
        h_t = h_t * mlstm_norm_w[l].astype(f32).reshape(MLSTM_HEADS, MLSTM_HEAD_DIM)
        h_a = jax.nn.sigmoid(o_g.astype(f32)) * h_t.reshape(bsz, s, MLSTM_WIDTH)
        y_a = (h_a * jax.nn.silu(z_a.astype(f32))).astype(x.dtype)

        pooled = _multiscale_pool(u_b)
        mixed = jnp.einsum('bsgc,gcd->bsgd', pooled, pool_w[l].astype(f32))
        mixed = mixed.reshape(bsz, s, POOL_WIDTH) * pool_scale[l].astype(f32)
        y_b = (mixed * jax.nn.silu(z_b.astype(f32))).astype(x.dtype)

        br_a = jnp.einsum('bsc,cd->bsd', y_a, w_proj_mlstm[l])
        br_b = jnp.einsum('bsc,cd->bsd', y_b, w_proj_pool[l])
        merged = jax.nn.sigmoid(g_a) * br_a + jax.nn.sigmoid(g_b) * br_b
        out = jnp.einsum('bsd,de->bse', merged, w_out[l])
        x = x + _rmsnorm(out, norm_post_w[l])
    return x


N_META = 16
D_MIX = D_MODEL
Q_BLOCK = 128
ROPE_THETA = 10000.0

A_HEADS = 8
A_QK_DIM = 64
A_V_DIM = 2 * A_QK_DIM
A_WIDTH = A_HEADS * A_V_DIM
B_HEADS = 8
B_Q_LORA = 512
B_KV_LORA = 256
B_NOPE = 128
B_ROPE = 64
B_V_DIM = 128
B_WIDTH = B_HEADS * B_V_DIM

A_Q_COLS = A_HEADS * 2 * A_QK_DIM
A_K_COLS = A_HEADS * 2 * A_QK_DIM
A_V_COLS = A_WIDTH
A_G_COLS = A_WIDTH
B_CQ_COLS = B_Q_LORA
B_CKV_COLS = B_KV_LORA
B_KR_COLS = B_ROPE
B_G_COLS = B_WIDTH
IN_COLS = A_Q_COLS + A_K_COLS + A_V_COLS + A_G_COLS + B_CQ_COLS + B_CKV_COLS + B_KR_COLS + B_G_COLS
UQ_COLS = B_HEADS * (B_NOPE + B_ROPE)
UKV_COLS = B_HEADS * (B_NOPE + B_V_DIM)


def _rmsnorm_2(x, w):
    xf = x.astype(jnp.float32)
    xf = xf * lax.rsqrt(jnp.mean(xf * xf, axis=-1, keepdims=True) + RMS_EPS)
    return xf.astype(x.dtype) * w

def _rope(x, pos):
    half = x.shape[-1] // 2
    inv = ROPE_THETA ** (-jnp.arange(half, dtype=jnp.float32) / half)
    ang = pos.astype(jnp.float32)[:, None] * inv[None, :]
    cos, sin = jnp.cos(ang), jnp.sin(ang)
    xf = x.astype(jnp.float32)
    x1, x2 = xf[..., :half], xf[..., half:]
    return jnp.concatenate([x1 * cos - x2 * sin, x1 * sin + x2 * cos], axis=-1).astype(x.dtype)

def _sweep(block_fn, n_blocks):
    out = lax.map(block_fn, jnp.arange(n_blocks, dtype=jnp.int32) * Q_BLOCK)
    nb, b, h, qb, dv = out.shape
    return jnp.moveaxis(out, 0, 2).reshape(b, h, nb * qb, dv)

def _diff_attention(q, k, v, lam, slopes):
    L = k.shape[3]
    scale = A_QK_DIM ** -0.5
    k_pos = jnp.arange(L, dtype=jnp.int32)

    def block(start):
        qb = lax.dynamic_slice_in_dim(q, start, Q_BLOCK, axis=3)
        rel = (start + jnp.arange(Q_BLOCK, dtype=jnp.int32))[:, None] - k_pos[None, :]
        s = jnp.einsum('bhcqd,bhckd->bhcqk', qb, k).astype(jnp.float32) * scale
        s = s - slopes[:, None, None, None] * rel.astype(jnp.float32)
        s = jnp.where(rel >= 0, s, -jnp.inf)
        p = jax.nn.softmax(s, axis=-1)
        w = p[:, :, 0] - lam * p[:, :, 1]
        return jnp.einsum('bhqk,bhkd->bhqd', w.astype(v.dtype), v)

    return _sweep(block, L // Q_BLOCK)

def _mla_attention(q_nope, q_pe, k_nope, k_pe, v):
    L = k_nope.shape[2]
    scale = (B_NOPE + B_ROPE) ** -0.5
    k_pos = jnp.arange(L, dtype=jnp.int32)

    def block(start):
        qn = lax.dynamic_slice_in_dim(q_nope, start, Q_BLOCK, axis=2)
        qp = lax.dynamic_slice_in_dim(q_pe, start, Q_BLOCK, axis=2)
        rel = (start + jnp.arange(Q_BLOCK, dtype=jnp.int32))[:, None] - k_pos[None, :]
        s = (jnp.einsum('bhqd,bhkd->bhqk', qn, k_nope) + jnp.einsum('bhqd,bkd->bhqk', qp, k_pe)).astype(jnp.float32) * scale
        s = jnp.where(rel >= 0, s, -jnp.inf)
        p = jax.nn.softmax(s, axis=-1)
        return jnp.einsum('bhqk,bhkd->bhqd', p.astype(v.dtype), v)

    return _sweep(block, L // Q_BLOCK)

def second_inputs(seed: int = 0) -> dict:
    key = jax.random.key(seed)
    ks = jax.random.split(key, 13)
    f32 = jnp.float32
    n = lambda k, shp: jax.random.normal(k, shp, dtype=f32)
    return {
        "x": n(ks[0], (BATCH, SEQ, D_MODEL)),
        "meta_tokens": n(ks[1], (N_META, D_MODEL)),
        "attn_norm_w": 1.0 + 0.02 * n(ks[2], (DEPTH, D_MODEL)),
        "w_in": n(ks[3], (DEPTH, D_MODEL, IN_COLS)) * D_MODEL ** -0.5,
        "diff_lambda": 0.1 * n(ks[4], (DEPTH, 4, A_QK_DIM)),
        "diff_subln_w": 1.0 + 0.02 * n(ks[5], (DEPTH, A_V_DIM)),
        "mla_q_norm_w": 1.0 + 0.02 * n(ks[6], (DEPTH, B_Q_LORA)),
        "w_uq": n(ks[7], (DEPTH, B_Q_LORA, UQ_COLS)) * B_Q_LORA ** -0.5,
        "mla_kv_norm_w": 1.0 + 0.02 * n(ks[8], (DEPTH, B_KV_LORA)),
        "w_ukv": n(ks[9], (DEPTH, B_KV_LORA, UKV_COLS)) * B_KV_LORA ** -0.5,
        "w_out": n(ks[10], (DEPTH, D_MIX, D_MODEL)) * D_MIX ** -0.5,
        "final_norm_w": 1.0 + 0.02 * n(ks[11], (D_MODEL,)),
    }

def second_block(x, meta_tokens, attn_norm_w, w_in, diff_lambda, diff_subln_w,
              mla_q_norm_w, w_uq, mla_kv_norm_w, w_ukv, w_out, final_norm_w):
    B, S, D = x.shape
    L = S + N_META
    L_pad = -(-L // Q_BLOCK) * Q_BLOCK
    meta = jnp.broadcast_to(meta_tokens[None].astype(x.dtype), (B, N_META, D))
    h = jnp.concatenate([meta, x], axis=1)
    h = jnp.pad(h, ((0, 0), (0, L_pad - L), (0, 0)))
    pos = jnp.arange(L_pad, dtype=jnp.int32)
    slopes = jnp.exp2(-8.0 * jnp.arange(1, A_HEADS + 1, dtype=jnp.float32) / A_HEADS)
    splits = np.cumsum([A_Q_COLS, A_K_COLS, A_V_COLS, A_G_COLS, B_CQ_COLS, B_CKV_COLS, B_KR_COLS])

    for l in range(DEPTH):
        hn = _rmsnorm_2(h, attn_norm_w[l])
        proj = hn @ w_in[l]
        a_q, a_k, a_v, a_g, b_cq, b_ckv, b_kr, b_g = jnp.split(proj, list(splits), axis=-1)

        qA = a_q.reshape(B, L_pad, A_HEADS, 2, A_QK_DIM).transpose(0, 2, 3, 1, 4)
        kA = a_k.reshape(B, L_pad, A_HEADS, 2, A_QK_DIM).transpose(0, 2, 3, 1, 4)
        vA = a_v.reshape(B, L_pad, A_HEADS, A_V_DIM).transpose(0, 2, 1, 3)
        lam_init = 0.8 - 0.6 * math.exp(-0.3 * l)
        lp = diff_lambda[l].astype(jnp.float32)
        lam = jnp.exp(jnp.sum(lp[0] * lp[1])) - jnp.exp(jnp.sum(lp[2] * lp[3])) + lam_init
        oA = _diff_attention(qA, kA, vA, lam, slopes)
        oA = _rmsnorm_2(oA, diff_subln_w[l]) * (1.0 - lam_init)
        oA = oA.transpose(0, 2, 1, 3).reshape(B, L_pad, A_WIDTH) * jax.nn.silu(a_g)

        qB = (_rmsnorm_2(b_cq, mla_q_norm_w[l]) @ w_uq[l]).reshape(B, L_pad, B_HEADS, B_NOPE + B_ROPE).transpose(0, 2, 1, 3)
        q_nope, q_pe = qB[..., :B_NOPE], _rope(qB[..., B_NOPE:], pos)
        kvB = (_rmsnorm_2(b_ckv, mla_kv_norm_w[l]) @ w_ukv[l]).reshape(B, L_pad, B_HEADS, B_NOPE + B_V_DIM).transpose(0, 2, 1, 3)
        k_nope, vB = kvB[..., :B_NOPE], kvB[..., B_NOPE:]
        k_pe = _rope(b_kr, pos)
        oB = _mla_attention(q_nope, q_pe, k_nope, k_pe, vB)
        oB = oB.transpose(0, 2, 1, 3).reshape(B, L_pad, B_WIDTH) * jax.nn.silu(b_g)

        h = h + jnp.concatenate([oA, oB], axis=-1) @ w_out[l]

    y = _rmsnorm_2(h, final_norm_w)
    return y[:, N_META:N_META + S]


def setup_inputs(seed=0):
    out = dict(first_inputs(seed))
    for name, value in second_inputs(seed + 1).items():
        if name != "x":
            out[name + "_2"] = value
    return out


def reference(
    x, norm_pre_w, w_in, mlstm_i_bias, mlstm_f_bias, qk_conv_w, qk_conv_b, mlstm_norm_w, pool_w,
    pool_scale, w_proj_mlstm, w_proj_pool, w_out, norm_post_w, meta_tokens_2, attn_norm_w_2,
    w_in_2, diff_lambda_2, diff_subln_w_2, mla_q_norm_w_2, w_uq_2, mla_kv_norm_w_2, w_ukv_2,
    w_out_2, final_norm_w_2,
):
    x = first_block(
        x, norm_pre_w, w_in, mlstm_i_bias, mlstm_f_bias, qk_conv_w, qk_conv_b, mlstm_norm_w,
        pool_w, pool_scale, w_proj_mlstm, w_proj_pool, w_out, norm_post_w,
    )
    return second_block(
        x, meta_tokens_2, attn_norm_w_2, w_in_2, diff_lambda_2, diff_subln_w_2, mla_q_norm_w_2,
        w_uq_2, mla_kv_norm_w_2, w_ukv_2, w_out_2, final_norm_w_2,
    )


_drawn_inputs = setup_inputs


def setup_inputs(seed=0):
    import zlib

    import numpy as np

    out = dict(_drawn_inputs(seed))
    spreads = {}
    factors = {'mlstm_i_bias': 64.0,
     'qk_conv_b': 8.0,
     'mlstm_norm_w': 2.725,
     'attn_norm_w_2': 6.274,
     'diff_lambda_2': 2.871,
     'diff_subln_w_2': 32.357,
     'mla_q_norm_w_2': 8.0,
     'mla_kv_norm_w_2': 8.0,
     'final_norm_w_2': 8.195}
    for name, (base, spread) in spreads.items():
        noise = np.random.default_rng([zlib.crc32(name.encode()), seed]).standard_normal(out[name].shape)
        drawn = base * np.exp(spread * noise) if base else spread * noise
        out[name] = jnp.asarray(drawn.astype(out[name].dtype))
    for name, factor in factors.items():
        out[name] = (out[name] * factor).astype(out[name].dtype)
    return out
```

```python
import math

import numpy as np

import concourse.bass as bass
from concourse import mybir

F32 = mybir.dt.float32
F32R = mybir.dt.float32r
ACT = mybir.ActivationFunctionType
ALU = mybir.AluOpType
AX = mybir.AxisListType

P = 128
D = 2048
S = 256
META = 16
L2 = S + META
KC = D // P
TOK = S // P
H = 8
HD = D // H
VW = HD + 1
EPS = 1e-6
LAM0 = 0.8 - 0.6 * math.exp(-0.3 * 0)
MLA_SCALE = (128 + 64) ** -0.5
COLS = 512
SLOT_KC = 2
SLOT = SLOT_KC * COLS
RING = 4
LEAD = 3
GROUP = KC // SLOT_KC

STAGES = (
    ("QK", ("qk", "qk"), 4),
    ("V", ("v", "v"), 2),
    ("OZ", ("o", "z"), 4),
    ("UZ", ("u", "zb"), 2),
    ("MG", ("ga", "pa", "gb", "pb"), 4),
    ("WO", ("wo", "wo"), 2),
    ("CKQ", ("ckv", "cq"), 1),
    ("AK", ("ak", "ak"), 1),
    ("AV", ("av", "av"), 1),
    ("AQ", ("aq", "aq"), 1),
    ("UQ", ("uq", "uq", "ur"), 1),
    ("UKV", ("uk", "uk", "uv", "uv"), 1),
    ("G", ("g",), 4),
    ("W2", ("w2", "w2"), 2),
)
N_SLOTS = {"pb": 4, "uq": 2, "ur": 2, "uk": 1, "uv": 1}


def slots_of(kind):
    return N_SLOTS.get(kind, GROUP)


def first_slots():
    at, out = 0, {}
    for name, kinds, times in STAGES:
        out[name] = at
        at += times * sum(map(slots_of, kinds))
    return out, at


FIRST, SLOTS = first_slots()
OUT_ORDER = (0, 2, 1, 3)
HIGH_AT = (("g", 4, 3, 0), ("g", 5, 3, 0), ("w2", 2, 0, 0), ("w2", 3, 0, 0))


def slot_turn(n, r):
    return n // RING if isinstance(n, int) else (n - r) // RING


def align(n):
    return n + -n % 32


def packed(parts):
    at, out = 0, {}
    for name, n in parts:
        out[name] = (at, at + n)
        at += n
    return out, at


SMALL, SMALL_W = packed((
    ("norm_pre", 16), ("conv_w", 128), ("conv_b", 32), ("mnorm", 16), ("pscale", 8), ("attn_norm", 16),
    ("qnorm", 4), ("kvnorm", 2), ("subln", 1), ("ibias", 1), ("fbias", 1), ("lambda", 256)))
K0 = 144
KEYS = K0 + L2
CONST, CONST_W = packed((
    ("ident", 128), ("ones", 128), ("dmask", 384), ("inv", 64), ("rel", KEYS), ("cmask", KEYS),
    ("slope", 8), ("cos", L2), ("sin", L2), ("rot", 128), ("half", 4)))


def build_program(nc, ctx, x, meta, w_stream, w_gates, pool_w, small_in, const_in, post_w, final_w, out):
    x1_dram = nc.dram_tensor("x1_kept", (P, TOK, D), F32, kind="Internal").ap()

    BASE = 16512
    R_X, R_C, R_Y, R_Z, R_V, R_T = 49152, 83968, 116736, 149504, 165888, 182336
    KB4 = 4096

    def sb(name, shape, dt, offset):
        return nc.alloc_sbuf_tensor_at(name, shape, dt, offset=BASE + offset)

    raw = [sb(f"raw{r}", [P, SLOT_KC, COLS], F32, r * KB4) for r in range(RING)]
    wh = [sb(f"wh{r}", [P, SLOT_KC, COLS], F32R, (RING + r) * KB4) for r in range(RING)]
    wl = [sb(f"wl{r}", [P, SLOT_KC, COLS], F32R, (2 * RING + r) * KB4) for r in range(RING)]
    xh = sb("xh", [P, KC, S], F32R, R_X)
    xl = sb("xl", [P, KC, S], F32R, R_X + 16384)
    qk = sb("qk", [P, 2 * KC, S], F32, R_C)
    yh = sb("yh", [P, KC, S], F32R, R_Y)
    yl = sb("yl", [P, KC, S], F32R, R_Y + 16384)
    xn = sb("xn", [P, TOK, D], F32, R_Y)
    xsq = sb("xsq", [P, TOK, D], F32, R_C)
    xf = [sb(f"xf{b}", [P, 4, S], F32, R_Y + 16384 + b * KB4) for b in range(2)]
    zh = sb("zh", [P, KC // 2, S], F32R, R_Z)
    zl = sb("zl", [P, KC // 2, S], F32R, R_Z + 8192)
    vn = sb("vn", [P, TOK, H * VW], F32, R_V)
    kst = sb("kst", [P, 2, S], F32, R_Z)
    darg = sb("darg", [P, 384], F32, R_Z + 2048)
    dmat = sb("dmat", [P, 384], F32, R_Z + 3584)
    pt = sb("pt", [P, 384], F32, R_Z + 5120)
    hn = sb("hn", [P, TOK, HD], F32, R_Z + 6656)
    mrow = sb("mrow", [H, S], F32, R_Z + 8704)
    rows = sb("rows", [H, 6, S], F32, R_Z + 9728)
    wg = sb("wg", [P, KC, 2 * H], F32, R_Z)
    wgh = sb("wgh", [P, KC, 2 * H], F32R, R_Z + 1024)
    wgl = sb("wgl", [P, KC, 2 * H], F32R, R_Z + 2048)
    gsb = sb("gsb", [P, TOK, 2 * H], F32, R_Z + 3072)
    mh = sb("mh", [P, KC, S], F32R, R_C)
    ml = sb("ml", [P, KC, S], F32R, R_C + 16384)
    upad = sb("upad", [P, 4, META + S], F32, R_C)
    wa = sb("wa", [P, 4, META + S], F32, R_C + 4352)
    wb = sb("wb", [P, 4, META + S], F32, R_C + 8704)
    pooled = sb("pooled", [P, 4, S], F32, R_C + 13056)
    poolw = sb("poolw", [P, 8, HD], F32, R_C + 17152)
    work = [sb(f"work{b}", [P, 4, S], F32, R_T + b * 4352) for b in range(4)]
    T2 = R_T + 4 * 4352
    small = sb("small", [P, SMALL_W], F32, T2)
    T3 = T2 + align(4 * SMALL_W)
    const = sb("const", [P, CONST_W], F32, T3)
    T4 = T3 + align(4 * CONST_W)
    cqn = sb("cqn", [P, TOK, COLS], F32, R_T)
    sqs = sb("sqs", [P, COLS], F32, R_T + 4352)
    stat = sb("stat", [P, 144], F32, T4)

    x2h = sb("x2h", [P, KC, L2], F32R, R_X)
    x2l = sb("x2l", [P, KC, L2], F32R, R_X + 17408)
    x2f = [sb(f"x2f{b}", [P, 4, S], F32, R_C + 16384 + b * KB4) for b in range(2)]
    metan = sb("metan", [META, D], F32, R_V)
    metasq = sb("metasq", [META, D], F32, R_T)
    metat = sb("metat", [P, KC, META], F32, R_V + 8192)
    aq = sb("aq", [P, H, S], F32, R_C)
    ak = sb("ak", [P, H, L2], F32, R_C + 8192)
    kn = sb("kn", [P, H, L2], F32, R_C + 16896)
    qp = sb("qp", [P, H // 2, S], F32, R_C + 25600)
    qst = [sb(f"qst{b}", [P, S], F32, R_C + 29696 + 1024 * b) for b in range(3)]
    kpe = sb("kpe", [P, L2], F32, T4 + 576)
    qhalf = [qst[0], small[:, slice(*SMALL["lambda"])]]
    avn = sb("avn", [P, 3, H * P], F32, R_Y)
    vbn = sb("vbn", [P, 3, H * P], F32, R_Y + 12288)
    qn = sb("qn", [P, H, S], F32, R_Y + 24576)
    ckvn = sb("ckvn", [P, 3, 384], F32, R_Z)
    avt = sb("avt", [P, H, L2], F32, R_Z + 4608)
    krs = sb("krs", [P, L2], F32, R_Z + 13312)
    gates = sb("gates", [P, KC, S], F32, R_Z)
    cqh = sb("cqh", [P, 4, S], F32R, R_V)
    cql = sb("cql", [P, 4, S], F32R, R_V + 4096)
    KVP = 3 * P
    ckh = sb("ckh", [P, 2, KVP], F32R, R_V + 8192)
    ckl = sb("ckl", [P, 2, KVP], F32R, R_V + 8192 + 3072)
    oall = sb("oall", [P, KC, S], F32, R_V)
    W1, W2_, W3 = R_T + 4352, R_T + 2 * 4352, R_T + 3 * 4352
    sbd = sb("sbd", [P, 2, KEYS], F32, W1)
    ond = sb("ond", [P, TOK, P], F32, W1 + 3328)
    wmix = sb("wmix", [P, KEYS], F32, W2_)
    wt = sb("wt", [P, 384], F32, W2_ + 1664)
    wts = sb("wts", [META, S], F32, W2_ + 3200)
    pm = [sb(f"pm{b}", [P, KEYS], F32, W3 + 1664 * b) for b in range(2)]
    onm = sb("onm", [P, TOK, P], F32, W3 + 3328)
    oh = sb("oh", [P, KC, S], F32R, R_V)
    ol = sb("ol", [P, KC, S], F32R, R_Z)
    yn = sb("yn", [P, TOK, D], F32, R_C)
    finalw = sb("finalw", [P, D], F32, R_C + 16384)
    x1r = sb("x1r", [P, TOK, D], F32, R_Y)

    ps = nc.alloc_psum_tensor("ps", [P, 8, 512], F32)

    def sm(name, a=0, n=None):
        lo, hi = SMALL[name]
        return small[:, lo + a:lo + a + (n or hi - lo - a)]

    def cn(name, a=0, n=None, p=P):
        lo, hi = CONST[name]
        return const[0:p, lo + a:lo + a + (n or hi - lo - a)]

    ident = cn("ident")

    def spread(ap, n):
        return ap.unsqueeze(2).to_broadcast([ap.shape[0], ap.shape[1], n])

    on = sb("on", [P, TOK, D], F32, R_Z)
    postw = sb("postw", [P, D], F32, R_X)
    xr = sb("xr", [P, TOK, D], F32, R_Y)

    sems = {}

    def sem(name):
        if name not in sems:
            sems[name] = ctx.enter_context(nc.semaphore(name))
        return sems[name]

    raw_in = [sem(f"raw_in{r}") for r in range(RING)]
    wh_done = sem("wh_done")
    split_done = sem("split_done")
    slots_done = sem("slots_done")
    psum_free = [sem("psum_free0"), sem("psum_free1")]

    def wait(eng, s, v):
        if not isinstance(v, int) or v > 0:
            eng.wait_ge(s, v)

    def group_numbers():
        at, outp = 0, {}
        for name, kinds, times in STAGES:
            outp[name] = at
            at += times * len(kinds)
        return outp

    FIRST_G = group_numbers()

    def pe_group(pe, n, frees, out_at, moving, tiles, tokens, ring=0, kcs=KC, cols=COLS, before=None,
                 chunk=lambda kc: kc):
        hi, lo = moving
        for k in range(kcs // SLOT_KC):
            if before:
                before(k)
            wait(pe, split_done, n + k + 1)
            if k == 0:
                for s, v in frees:
                    wait(pe, s, v)
            r = (ring + k) % RING
            for c in range(SLOT_KC):
                kc = k * SLOT_KC + c
                a, z = kc == 0, kc == kcs - 1
                kc = chunk(kc)
                if tiles:
                    for m, t in enumerate(tiles):
                        o = out_at(m)
                        pe.matmul(o, hi[:, kc, t], wh[r][:, c, 0:cols], start=a, stop=False)
                        pe.matmul(o, hi[:, kc, t], wl[r][:, c, 0:cols], start=False, stop=False)
                        last = pe.matmul(o, lo[:, kc, t], wh[r][:, c, 0:cols], start=False, stop=z)
                else:
                    two = tokens.stop - tokens.start <= S
                    for j in range(4):
                        f = slice(j * P, (j + 1) * P)
                        st = a and (j % 2 == 0 or not two)
                        pe.matmul(out_at(j), wh[r][:, c, f], hi[:, kc, tokens], start=st, stop=False,
                                  skip_group_check=True)
                        pe.matmul(out_at(j), wh[r][:, c, f], lo[:, kc, tokens], start=False, stop=False,
                                  skip_group_check=True)
                        last = pe.matmul(out_at(j), wl[r][:, c, f], hi[:, kc, tokens], start=False, stop=z,
                                         skip_group_check=True)
            last.then_inc(slots_done, 1)

    def half_bank(parity):
        return lambda j: ps[:, 2 * parity + j // 2, (j % 2) * S:(j % 2) * S + S]

    def whole_bank(first, width=COLS):
        return lambda m: ps[:, first + m, 0:width]

    def banks(parity):
        return ps[:, 2 * parity:2 * parity + 2, :].rearrange("p b (j s) -> p (b j) s", j=2)

    s_x, s_small, s_const, s_wg = [sem("x_in0"), sem("x_in1")], sem("small_in"), sem("const_in"), sem("wg_in")
    s_ss, s_ms, s_rstd, s_xn = sem("x_squares"), sem("x_mean"), sem("x_rstd"), sem("x_normed")
    s_xt, s_xf, s_xh, s_xl = sem("x_turned"), sem("x_scaled"), sem("x_high"), sem("x_low")
    s_wgh, s_wgl, s_gmm, s_gsb, s_grow = (sem("gate_w_high"), sem("gate_w_low"), sem("gate_sums"),
                                          sem("gate_copied"), sem("gate_rows"))
    s_gact, s_gB, s_gthr, s_gT, s_gcol = (sem("gate_log"), sem("gate_scanned"), sem("gate_bound"),
                                          sem("gate_turned"), sem("gate_columns"))
    s_acc, s_conv, s_sg, s_qk, s_v = (sem("conv_first"), sem("conv_done"), sem("conv_sigmoid"), sem("qk_done"),
                                      sem("v_done"))
    s_kst, s_sc, s_arg, s_dm, s_pt, s_num = (sem("head_keys"), sem("head_scores"), sem("head_exponent"),
                                             sem("head_decay"), sem("head_weights"), sem("head_sums"))
    s_den, s_hsq, s_hms, s_hrs, s_hn, s_ht, s_htc = (sem("head_denominator"), sem("head_squares"), sem("head_mean"),
                                                     sem("head_rstd"), sem("head_normed"), sem("head_turned"),
                                                     sem("head_kept"))
    s_sgo, s_sgz, s_y = sem("o_sigmoid"), sem("z_sigmoid"), sem("y_done")
    s_u, s_pool, s_pmm, s_pw, s_zsg, s_zd = (sem("u_kept"), sem("pooled"), sem("pool_mixed"), sem("pool_w_in"),
                                             sem("zb_sigmoid"), sem("yb_done"))
    s_ga, s_gb, s_m = sem("ga_sigmoid"), sem("gb_sigmoid"), sem("merged")
    s_wosq, s_on, s_post, s_xr = sem("out_squares"), sem("out_scaled"), sem("post_w_in"), sem("x_again")
    s_t1, s_t2, s_x1, s_t3 = sem("tail_mean"), sem("tail_rstd"), sem("x1_done"), sem("tail")
    s_out = sem("stored")
    s_meta, s_mss, s_mms, s_mrs, s_mn, s_mt, s_mtc = (sem("meta_in"), sem("meta_squares"), sem("meta_mean"),
                                                      sem("meta_rstd"), sem("meta_normed"), sem("meta_turned"),
                                                      sem("meta_kept"))
    s_xkept, s_ss2, s_ms2, s_rs2, s_xs, s_xt2, s_xf2, s_xh2, s_xl2 = (
        sem("x1_kept"), sem("x1_squares"), sem("x1_mean"), sem("x1_rstd"), sem("x1_normed"), sem("x2_turned"),
        sem("x2_scaled"), sem("x2_high"), sem("x2_low"))
    s_ckc, s_cks, s_ckm, s_ckr, s_ckn, s_ckt, s_krs, s_krm, s_ckl, s_kpe = (
        sem("ckv_copied"), sem("ckv_squares"), sem("ckv_mean"), sem("ckv_rstd"), sem("ckv_normed"),
        sem("ckv_turned"), sem("kr_kept"), sem("kr_rotated"), sem("ckv_low"), sem("kpe_done"))
    s_cqs, s_cqm, s_cqr, s_cqn, s_cqt, s_cql = (sem("cq_squares"), sem("cq_mean"), sem("cq_rstd"),
                                                sem("cq_normed"), sem("cq_turned"), sem("cq_low"))
    s_avt, s_avm, s_avn = sem("av_kept"), sem("av_turned"), sem("av_done")
    s_qpr, s_qpm, s_qp, s_k2, s_l1, s_l2, s_lam = (sem("qp_raw"), sem("qp_rotated"), sem("qp_done"),
                                                   sem("second_kept"), sem("lambda_sums"), sem("lambda_exp"),
                                                   sem("lambda_done"))
    s_gsum, s_gs, s_gate = sem("gate_summed"), sem("gate_sigmoid"), sem("gate_done")
    pair = {name: sem("pair_" + name) for name in (
        "queries", "scores_d", "scores_m", "max_d", "exp_d", "mix", "max_m", "exp_m", "turned_d", "kept_d",
        "sums_d", "squares", "mean", "rstd", "scale", "normed_d", "back_d", "out_d", "turned_m", "kept_m",
        "sums_m", "inverse_m", "normed_m", "back_m", "out_m")}
    s_og, s_oh, s_ol, s_fin, s_x1r, s_yn, s_ysq, s_t4, s_t5, s_t6 = (
        sem("out_gated"), sem("out_high"), sem("out_low"), sem("final_w_in"), sem("x1_back"), sem("y_summed"),
        sem("y_squares"), sem("y_mean"), sem("y_rstd"), sem("y_scaled"))
    s_one, s_pad = sem("vn_ones"), sem("pad_zeroed")

    block = ctx.enter_context(nc.Block())

    @block.sync
    def _(sp):
        for m in range(TOK):
            sp.dma_start(xn[:, m, :], x[m * P:(m + 1) * P, :]).then_inc(s_x[m], 16)
            if m == 0:
                sp.dma_start(small[:, :], small_in).then_inc(s_small, 16)
                sp.dma_start(const[:, :], const_in).then_inc(s_const, 16)
        for n in range(RING):
            sp.dma_start(raw[n][:, :, :], w_stream[n]).then_inc(raw_in[n], 16)
        sp.dma_start(wg[:, :, :], w_gates).then_inc(s_wg, 16)
        with sp.Fori(1, SLOTS // RING) as i:
            for r in range(RING):
                sp.wait_ge(split_done, i * RING + (r - RING + 1))
                sp.dma_start(raw[r][:, :, :], w_stream[bass.ds(i * RING + r, 1), :, :, :].rearrange(
                    "o p c n -> p (o c) n")).then_inc(raw_in[r], 16)
        for n in range(SLOTS - SLOTS % RING, SLOTS):
            sp.wait_ge(split_done, n - RING + 1)
            sp.dma_start(raw[n % RING][:, :, :], w_stream[n]).then_inc(raw_in[n % RING], 16)

        for c in range(4):
            m, q = c // 2, c % 2
            sp.wait_ge(s_t6, c + 1)
            sp.dma_start(out[m * P:(m + 1) * P, q * 1024:(q + 1) * 1024], yn[:, m, q * 1024:(q + 1) * 1024]).then_inc(
                s_out, 16)
        sp.wait_ge(s_xkept, 16)
        sp.wait_ge(s_out, 4 * 16)

    @block.tensor
    def _(pe):
        def turn(o, i, n=P):
            return pe.transpose(o, i, ident[0:n, 0:n])

        wait(pe, s_const, 16)
        for b in range(4):
            for j in range(4):
                for m in range(TOK):
                    if b == 0 and j == 0:
                        pe.wait_ge(s_xn, m + 1)
                    f = (4 * b + j) * P
                    last = turn(ps[:, 2 * b + j // 2, (j % 2) * S + m * P:(j % 2) * S + (m + 1) * P],
                                xn[:, m, f:f + P])
            last.then_inc(s_xt, 1)

        def groups(name, i, moving, token_kinds=(), before=None):
            kinds = dict((a, b) for a, b, _ in STAGES)[name]
            per = sum(map(slots_of, kinds))
            off = 0
            for j, kind in enumerate(kinds):
                by_token = kind in token_kinds
                pe_group(pe, FIRST[name] + i * per + off,
                         [(psum_free[j % 2], FIRST_G[name] // 2 + i * (len(kinds) // 2) + j // 2)],
                         whole_bank(2 * (j % 2)) if by_token else half_bank(j % 2), moving[kind],
                         [slice(m * P, (m + 1) * P) for m in range(TOK)] if by_token else None, slice(0, S),
                         kcs=slots_of(kind) * SLOT_KC, before=before and (lambda k, j=j, kind=kind: before(j, kind, k)))
                off += slots_of(kind)

        X, Y, Z = (xh, xl), (yh, yl), (zh, zl)

        def x_there(j, kind, k):
            pe.wait_ge(s_xl, (k * SLOT_KC + SLOT_KC - 1) // 4 + 1)

        with pe.Fori(0, 4) as i:
            groups("QK", i, {"qk": X}, before=x_there)

        pe.wait_ge(s_wgl, 1)
        for m in range(TOK):
            t = slice(m * P, (m + 1) * P)
            for kc in range(KC):
                o = ps[:, 4, m * 16:m * 16 + 16]
                pe.matmul(o, xh[:, kc, t], wgh[:, kc, :], start=kc == 0, stop=False)
                pe.matmul(o, xh[:, kc, t], wgl[:, kc, :], start=False, stop=False)
                last = pe.matmul(o, xl[:, kc, t], wgh[:, kc, :], start=False, stop=kc == KC - 1)
        last.then_inc(s_gmm, 1)

        groups("V", 0, {"v": X}, token_kinds=("v",))
        pe.wait_ge(s_gsb, 1)
        for w in range(2):
            for m in range(TOK):
                last = turn(ps[0:H, 5, w * S + m * P:w * S + (m + 1) * P], gsb[:, m, w * H:(w + 1) * H])
        last.then_inc(s_grow, 1)
        groups("V", 1, {"v": X}, token_kinds=("v",))
        pe.wait_ge(s_gthr, 1)
        for w, row in enumerate((4, 2)):
            for m in range(TOK):
                last = turn(ps[:, 6, 16 * w + 8 * m:16 * w + 8 * m + 8], rows[:, row, m * P:(m + 1) * P], H)
        last.then_inc(s_gT, 1)

        def head(i, j, k):
            h = i * 2 + j
            if k == 0:
                pe.wait_ge(s_kst, h * 2 + 2)
                pe.wait_ge(s_htc, h + 1)
                pe.matmul(ps[:, 4, 0:S], cn("ones", p=H), mrow[:, :], start=True, stop=True)
                for st in range(TOK):
                    w = S - st * P
                    for dt in range(2):
                        last = pe.matmul(ps[:, 5, st * S:st * S + w], kst[:, dt, st * P:(st + 1) * P],
                                         qk[:, bass.ds(h * 2 + dt, 1), st * P:S].rearrange("p o s -> p (o s)"),
                                         start=dt == 0, stop=dt == 1)
                last.then_inc(s_sc, 1)
            if k == 3:
                pe.wait_ge(s_pt, h + 1)
                for t, st in ((0, 0), (1, 0), (1, 1)):
                    lhs = pt[:, t * P:(t + 1) * P] if st == 0 else pt[:, S:S + P]
                    last = pe.matmul(ps[:, 6 + t, 0:VW], lhs, vn[:, st, bass.ds(h * VW, VW)],
                                     start=st == 0, stop=st == t)
                last.then_inc(s_num, 1)
            if k == 7:
                pe.wait_ge(s_hn, h + 1)
                for dt in range(2):
                    for m in range(TOK):
                        last = turn(ps[:, 4, dt * S + m * P:dt * S + (m + 1) * P], hn[:, m, dt * P:(dt + 1) * P])
                last.then_inc(s_ht, 1)

        pe.wait_ge(s_one, 1)
        with pe.Fori(0, 4) as i:
            groups("OZ", i, {"o": X, "z": X}, before=lambda j, kind, k: head(i, j, k))

        def mix(i, j, k):
            if j == 1 and k == 6:
                pe.wait_ge(s_pool, i + 1)
                pe.wait_ge(s_pw, 16)
                wait(pe, s_zd, i)
                for jj in range(4):
                    for cc in range(2):
                        g = jj // 2
                        last = pe.matmul(ps[:, 4 + g, (jj % 2) * S:(jj % 2) * S + S],
                                         poolw[:, (2 * i + g) * 2 + cc, (jj % 2) * P:(jj % 2) * P + P],
                                         pooled[:, 2 * g + cc, :], start=cc == 0, stop=cc == 1)
                last.then_inc(s_pmm, 1)

        for i in range(2):
            groups("UZ", i, {"u": X, "zb": X}, before=lambda j, kind, k: mix(i, j, k))

        def projected(j, kind, k):
            if kind == "pa" and k == 0:
                pe.wait_ge(s_y, 4)
            if kind == "pb" and k == 0:
                pe.wait_ge(s_zd, 2)

        with pe.Fori(0, 4) as i:
            groups("MG", i, {"ga": X, "pa": Y, "gb": X, "pb": Z}, before=projected)

        def merged_there(i, j, k):
            pe.wait_ge(s_m, (k * SLOT_KC + SLOT_KC - 1) // 4 + 1)
            if i == 1 and j == 0 and k == 2:
                pe.wait_ge(s_mn, 1)
                for c in range(KC):
                    last = turn(ps[:, 6, c * META:(c + 1) * META], metan[:, c * P:(c + 1) * P], META)
                last.then_inc(s_mt, 1)

        for i in range(2):
            groups("WO", i, {"wo": (mh, ml)}, token_kinds=("wo",),
                   before=lambda j, kind, k: merged_there(i, j, k))

        uses = [FIRST_G["CKQ"] // 2, FIRST_G["CKQ"] // 2]
        X2 = (x2h, x2l)
        xtok = [slice(META, META + P), slice(META + P, L2)]
        pe.wait_ge(psum_free[0], uses[0])
        pe.wait_ge(psum_free[1], uses[1])
        pe.wait_ge(s_mtc, 1)
        pe.wait_ge(s_wosq, 4)
        for m in range(TOK):
            pe.wait_ge(s_xs, m + 1)
            for c in range(KC):
                last = turn(ps[:, c // 2, (c % 2) * S + m * P:(c % 2) * S + (m + 1) * P], on[:, m, c * P:(c + 1) * P])
                if m == TOK - 1 and c % 4 == 3:
                    last.then_inc(s_xt2, 1)

        def x2_there(k):
            pe.wait_ge(s_xl2, (k * SLOT_KC + SLOT_KC - 1) // 4 + 1)

        def both():
            return [(psum_free[0], uses[0]), (psum_free[1], uses[1])]

        def used(*parities):
            for parity in parities:
                uses[parity] += 1

        n = FIRST["CKQ"]
        pe.wait_ge(s_xl2, 4)
        pe_group(pe, n, [(psum_free[0], uses[0])], lambda m: ps[:, (0, 1, 4)[m], 0:384], X2,
                 [slice(0, P), slice(P, 2 * P), slice(L2 - P, L2)], None, cols=384)
        used(0)
        pe_group(pe, n + GROUP, [(psum_free[1], uses[1])], whole_bank(2), X2, xtok, None)
        used(1)

        def second(stage, j, k):
            if stage == "AK" and j == 1 and k == 2:
                pe.wait_ge(s_ckn, 1)
                for c in range(3):
                    for t in (0, P, L2 - P):
                        m = min(t // P + (t % P > 0), 2)
                        last = turn(ps[:, 5 + c, t:t + P], ckvn[:, m, c * P:(c + 1) * P])
                last.then_inc(s_ckt, 1)
            if stage == "AV" and j == 0 and k == 2:
                pe.wait_ge(s_krs, 1)
                pe.wait_ge(s_ckl, 1)
                pe.matmul(ps[:, 7, 0:L2], cn("rot"), krs[:, :], start=True, stop=True).then_inc(s_krm, 1)
                pe.wait_ge(s_cqn, 1)
                for c in range(4):
                    for m in range(TOK):
                        last = turn(ps[:, 5 + c // 2, (c % 2) * S + m * P:(c % 2) * S + (m + 1) * P],
                                    cqn[:, m, c * P:(c + 1) * P])
                last.then_inc(s_cqt, 1)
            if stage == "AQ" and k == 3:
                pe.wait_ge(s_avt, j + 1)
                pe.wait_ge(s_cql, 1)
                pe.wait_ge(s_kpe, 1)
                wait(pe, s_avn, j)
                for kt in range(3):
                    w = min(P, L2 - kt * P)
                    for h in range(4):
                        last = turn(ps[0:w, 4 + kt, h * P:(h + 1) * P], avt[:, 4 * j + h, kt * P:kt * P + w])
                last.then_inc(s_avm, 1)

        for stage in ("AK", "AV"):
            for j in range(2):
                pe_group(pe, FIRST[stage] + j * GROUP, both(), whole_bank(0, L2), X2, None, slice(0, L2),
                         before=lambda k: second(stage, j, k))
                used(0, 1)
        for j in range(2):
            pe_group(pe, FIRST["AQ"] + j * GROUP, [(psum_free[j], uses[j])], half_bank(j), X2, None,
                     slice(META, L2), before=lambda k: second("AQ", j, k))
            used(j)
        n = FIRST["UQ"]
        for j in range(3):
            pe_group(pe, n, [(psum_free[j % 2], uses[j % 2])], half_bank(j % 2), (cqh, cql), None, slice(0, S),
                     kcs=4, ring=n % RING)
            used(j % 2)
            n += 2
        n = FIRST["UKV"]
        for j in range(2):
            pe_group(pe, n, both(), whole_bank(0, L2), (ckh, ckl), None, slice(0, L2), kcs=2, ring=n % RING)
            used(0, 1)
            n += 1
            if j == 0:
                pe.wait_ge(s_qpr, 1)
                pe.wait_ge(s_avn, 2)
                for t in range(4):
                    last = pe.matmul(ps[:, 4 + t // 2, (t % 2) * S:(t % 2) * S + S], cn("rot"), work[1][:, t, :],
                                     start=True, stop=True)
                last.then_inc(s_qpm, 1)
        for j in range(2):
            pe_group(pe, n, both(), whole_bank(0), (ckh, ckl), [slice(t * P, (t + 1) * P) for t in range(3)], None,
                     kcs=2, ring=n % RING)
            used(0, 1)
            n += 1

        def scores(p, odd):
            pe.wait_ge(pair["queries"], p * 4 + 4)
            for c in range(2):
                for t, (lo, w) in enumerate(((0, K0), (K0, L2))):
                    last = pe.matmul(ps[:, 2 + c, lo:lo + w], qhalf[c][:, t * P:(t + 1) * P],
                                     ak[:, bass.ds(p, 1), 0:w].rearrange("p o s -> p (o s)"), start=True, stop=True)
            last.then_inc(pair["scores_d"], 1)
            r = slice(64 * odd, 64 * odd + 64)
            for t, (lo, w) in enumerate(((0, K0), (K0, L2))):
                pe.matmul(ps[:, 4, lo:lo + w], qst[1][:, t * P:(t + 1) * P],
                          kn[:, bass.ds(p, 1), 0:w].rearrange("p o s -> p (o s)"), start=True, stop=False)
                last = pe.matmul(ps[:, 4, lo:lo + w], qst[2][r, t * P:(t + 1) * P], kpe[r, 0:w],
                                 start=False, stop=True)
            last.then_inc(pair["scores_m"], 1)

        def turned(w, s):
            for at, lo in ((0, 0), (P, K0), (2 * P, K0 + P)):
                turn(ps[:, 5, at:at + P], w[:, lo:lo + P])
            for at, lo in ((0, P), (P, K0 + 2 * P)):
                last = turn(ps[0:META, 6, at:at + P], w[:, lo:lo + META])
            last.then_inc(s, 1)

        def weighted(bank, v, h, s):
            hc = bass.ds(h * P, P)
            pe.matmul(ps[:, bank, 0:P], wt[:, 0:P], v[:, 0, hc], start=True, stop=False)
            pe.matmul(ps[:, bank, 0:P], wts[:, 0:P], v[0:META, 1, hc], start=False, stop=True)
            pe.matmul(ps[:, bank, P:2 * P], wt[:, P:2 * P], v[:, 0, hc], start=True, stop=False)
            pe.matmul(ps[:, bank, P:2 * P], wt[:, 2 * P:3 * P], v[:, 1, hc], start=False, stop=False)
            pe.matmul(ps[:, bank, P:2 * P], wts[:, P:2 * P], v[0:META, 2, hc], start=False, stop=True).then_inc(s, 1)

        def back(bank, o, s):
            for m in range(TOK):
                last = turn(ps[:, bank, m * P:(m + 1) * P], o[:, m, :])
            last.then_inc(s, 1)

        def quarter(p, k, odd):
            first = p if isinstance(p, int) else 2
            here = not isinstance(p, int) or p < H
            if k == 0:
                if first >= 1:
                    pe.wait_ge(pair["kept_m"], p)
                    weighted(6, vbn, p - 1, pair["sums_m"])
                if here:
                    if first < 1:
                        pe.wait_ge(s_qp, 1)
                    else:
                        pe.wait_ge(pair["max_m"], p)
                    scores(p, odd)
            if k == 1 and first >= 1:
                pe.wait_ge(pair["normed_m"], p)
                back(6, onm, pair["back_m"])
                pe.wait_ge(pair["normed_d"], p)
                back(7, ond, pair["back_d"])
            if k == 2 and here:
                pe.wait_ge(pair["mix"], p + 1)
                if first >= 1:
                    pe.wait_ge(pair["out_m"], p)
                turned(wmix, pair["turned_d"])
            if k == 3 and here:
                pe.wait_ge(pair["kept_d"], p + 1)
                if first >= 1:
                    pe.wait_ge(pair["out_d"], p)
                weighted(7, avn, p, pair["sums_d"])
                pe.wait_ge(pair["exp_m"], p + 1)
                turned(pm[odd], pair["turned_m"])

        def gate_group(q):
            pe_group(pe, FIRST["G"] + q * GROUP, [(s_gsum, q)] if not isinstance(q, int) or q else both(),
                     half_bank(0), X2, None, slice(META, L2), ring=FIRST["G"] % RING,
                     before=lambda k: quarter(q * 2 + k // 4, k % 4, k // 4))

        gate_group(0)
        with pe.Fori(1, 3) as q:
            gate_group(q)
        gate_group(3)

        for j in range(4):
            def out_there(k):
                if j == 0:
                    if k < 2:
                        quarter(H, k, 0)
                    pe.wait_ge(s_ol, k // 2 + 1)
            pe_group(pe, FIRST["W2"] + j * GROUP, [(s_yn, j - 1)] if j >= 2 else [(s_gsum, 4)],
                     whole_bank(2 * (j % 2)), (oh, ol), [slice(0, P), slice(P, S)], None,
                     ring=FIRST["W2"] % RING, before=out_there, chunk=lambda kc: OUT_ORDER[kc // 4] * 4 + kc % 4)

    def run(eng, split, evac, attend, breaks):
        prev = None
        for name, kinds, times in STAGES:
            if name in breaks:
                for k in range(GROUP):
                    evac(prev[0], k, prev[1], prev[2], FIRST[name])
                breaks[name]()
                prev = None
            per = sum(map(slots_of, kinds))
            n0 = FIRST[name]

            def body(i, prev):
                off = 0
                for j, kind in enumerate(kinds):
                    here = n0 + i * per + off
                    for k in range(slots_of(kind)):
                        if prev:
                            evac(prev[0], k, prev[1], prev[2], here)
                        attend(kind, k, i, j)
                        if not isinstance(i, int) or here + k + LEAD < SLOTS:
                            split(here + k + LEAD, (n0 + off + k + LEAD) % RING)
                    prev = (kind, i, j)
                    off += slots_of(kind)
                return prev

            prev = body(0, prev)
            if times > 2:
                last = times - (name == "G")
                with eng.Fori(1, last) as i:
                    body(i, (kinds[-1], i - 1, len(kinds) - 1))
                if last < times:
                    body(last, (kinds[-1], last - 1, len(kinds) - 1))
            elif times == 2:
                body(1, prev)
            prev = (kinds[-1], times - 1, len(kinds) - 1)
        for k in range(GROUP):
            evac(prev[0], k, prev[1], prev[2], SLOTS)

    @block.scalar
    def _(act):
        def drain():
            act.drain()

        def split(n, r):
            act.wait_ge(raw_in[r], 16 * slot_turn(n, r) + 16)
            wait(act, slots_done, n - RING + 1)
            act.activation(wh[r][:, :, :], raw[r][:, :, :], ACT.Copy).then_inc(wh_done, 1)

        act.sem_inc(s_htc, 1)
        for m in range(TOK):
            act.wait_ge(s_x[m], 16)
            act.activation(xsq[:, m, :], xn[:, m, :], ACT.Square, accum_out=stat[:, m:m + 1]).then_inc(s_ss, 1)
        for n in range(LEAD):
            split(n, n)
        for b in range(4):
            act.wait_ge(s_xf, b + 1)
            act.activation(xh[:, 4 * b:4 * b + 4, :], xf[b % 2][:, :, :], ACT.Copy).then_inc(s_xh, 1)
        act.wait_ge(s_wg, 16)
        act.activation(wgh[:, :, :], wg[:, :, :], ACT.Copy).then_inc(s_wgh, 1)

        def evac(kind, k, i, j, done):
            if kind == "qk":
                q = i * 2 + j
                if k == 0:
                    act.wait_ge(slots_done, done)
                    wait(act, s_qk, q)
                    for jj in range(4):
                        last = act.activation(
                            work[0][:, jj, :], banks(j)[:, jj, :], ACT.Identity,
                            bias=small[:, bass.ds(SMALL["conv_b"][0] + q * 4 + jj, 1)],
                            scale=small[:, bass.ds(SMALL["conv_w"][0] + q * 16 + 4 * jj + 3, 1)])
                    last.then_inc(s_acc, 1)
                if k == 3:
                    act.wait_ge(s_conv, q + 1)
                    act.activation(work[1][:, :, :], work[0][:, :, :], ACT.Sigmoid).then_inc(s_sg, 1)
            if kind == "v" and k == 0:
                act.wait_ge(slots_done, done)
                q = i * 2 + j
                for m in range(TOK):
                    last = act.activation(
                        vn[:, m, 2 * q * VW:2 * (q + 1) * VW].rearrange("p (h d) -> p h d", h=2)[:, :, 0:HD],
                        ps[:, 2 * j + m, :].rearrange("p (h d) -> p h d", h=2), ACT.Copy)
                last.then_inc(psum_free[j], 1)
            if kind == "o" and k == 0:
                act.wait_ge(slots_done, done)
                wait(act, s_y, i)
                if isinstance(i, int):
                    act.wait_ge(s_qk, 8)
                act.activation(work[0][:, :, :], banks(0), ACT.Sigmoid).then_inc(psum_free[0], 1)
            if kind == "z" and k == 0:
                act.wait_ge(slots_done, done)
                act.activation(work[1][:, :, :], banks(1), ACT.Sigmoid).then_inc(s_sgz, 1)
            if kind == "u" and k == 0:
                act.wait_ge(slots_done, done)
                wait(act, s_pool, i)
                act.wait_ge(s_pad, 1)
                act.activation(upad[:, :, META:META + S], banks(0), ACT.Copy).then_inc(s_u, 1)
                act.drain().then_inc(psum_free[0], 1)
            if kind == "zb" and k == 0:
                act.wait_ge(slots_done, done)
                act.wait_ge(s_y, 4)
                wait(act, s_zd, i)
                act.activation(work[1][:, :, :], banks(1), ACT.Sigmoid).then_inc(s_zsg, 1)
            if kind == "ga" and k == 0:
                act.wait_ge(slots_done, done)
                wait(act, s_m, i)
                if isinstance(i, int):
                    act.wait_ge(s_zd, 2)
                act.activation(work[0][:, :, :], banks(0), ACT.Sigmoid).then_inc(s_ga, 1)
                act.drain().then_inc(psum_free[0], 1)
            if kind == "gb" and k == 0:
                act.wait_ge(slots_done, done)
                act.activation(work[1][:, :, :], banks(0), ACT.Sigmoid).then_inc(s_gb, 1)
                act.drain().then_inc(psum_free[0], 1)
            if kind == "wo" and k == 0:
                act.wait_ge(slots_done, done)
                act.wait_ge(s_m, 4)
                q = i * 2 + j
                for m in range(TOK):
                    last = act.activation(ps[:, 4 + m, :], ps[:, 2 * j + m, :], ACT.Square,
                                          accum_out=stat[:, 12 + 4 * m + q:13 + 4 * m + q])
                    drain()
                act.drain().then_inc(s_wosq, 1)

            if kind == "ckv" and k == 0:
                act.wait_ge(slots_done, done)
                act.activation(ckvn[:, 0:2, :], ps[:, 0:2, 0:384], ACT.Copy)
                act.activation(ckvn[:, 2, :], ps[:, 4, 0:384], ACT.Copy)
                act.drain().then_inc(psum_free[0], 1)
                for m in range(3):
                    act.activation(sqs[:, 0:S], ckvn[:, m, 0:S], ACT.Square, accum_out=stat[:, 30 + m:31 + m])
                    drain()
                act.drain().then_inc(s_cks, 1)
            if kind == "cq" and k == 0:
                act.wait_ge(slots_done, done)
                act.activation(cqn[:, :, :], ps[:, 2:4, :], ACT.Copy)
                act.drain().then_inc(psum_free[1], 1)
                for m in range(TOK):
                    act.activation(sqs[:, :], cqn[:, m, :], ACT.Square, accum_out=stat[:, 36 + m:37 + m])
                    drain()
                act.drain().then_inc(s_cqs, 1)
            if kind in ("ak", "av", "uk") and k == 0:
                act.wait_ge(slots_done, done)
                to = {"ak": ak, "av": avt, "uk": kn}[kind]
                act.activation(to[:, 4 * j:4 * j + 4, :], ps[:, 0:4, 0:L2], ACT.Copy)
                act.drain().then_inc(psum_free[0], 1)
                act.sem_inc(psum_free[1], 1)
                if kind == "av":
                    act.sem_inc(s_avt, 1)
            if kind in ("aq", "uq") and k == 0:
                act.wait_ge(slots_done, done)
                to = aq if kind == "aq" else qn
                act.activation(to[:, 4 * j:4 * j + 4, :], banks(j), ACT.Copy).then_inc(psum_free[j], 1)
            if kind == "ur" and k == 0:
                act.wait_ge(slots_done, done)
                act.activation(work[1][:, :, :], banks(0), ACT.Copy)
                act.drain().then_inc(psum_free[0], 1)
                act.sem_inc(s_qpr, 1)
            if kind == "uv" and k == 0:
                act.wait_ge(slots_done, done)
                c = slice((j - 2) * COLS, (j - 1) * COLS)
                act.activation(vbn[:, 0:2, c], ps[:, 0:2, :], ACT.Copy)
                act.activation(vbn[0:META, 2, c], ps[0:META, 2, :], ACT.Copy)
                act.drain().then_inc(psum_free[0], 1)
                act.sem_inc(psum_free[1], 1)
                act.sem_inc(s_k2, 1)
            if kind == "g" and k == 2:
                act.wait_ge(s_gsum, i + 1)
                wait(act, s_gate, i)
                act.activation(work[0][:, :, :], gates[:, bass.ds(i * 4, 4), :], ACT.Sigmoid).then_inc(s_gs, 1)
            if kind == "w2" and k == 1:
                q = i * 2 + j
                act.wait_ge(s_yn, q + 1)
                for m in range(TOK):
                    act.activation(sqs[:, :], yn[:, m, q * COLS:(q + 1) * COLS], ACT.Square,
                                   accum_out=stat[:, 12 + 4 * m + q:13 + 4 * m + q])
                    drain()
                act.drain().then_inc(s_ysq, 1)

        def exps(parts, p, s):
            for x_, bias, total, scale in parts:
                act.activation(x_, x_, ACT.Exp, bias=bias, scale=scale, accum_out=total)
            act.drain().then_inc(s, 1)

        def quarter(p, k, odd):
            first = p if isinstance(p, int) else 2
            here = not isinstance(p, int) or p < H
            b, b1 = 64 + 40 * odd, 64 + 40 * (1 - odd)

            def keep(s, t):
                act.wait_ge(t, p + 1)
                act.activation(wt[:, :], ps[:, 5, 0:384], ACT.Copy)
                act.activation(wts[:, :], ps[0:META, 6, 0:S], ACT.Copy)
                act.drain().then_inc(s, 1)

            if k == 0:
                if first >= 1:
                    act.wait_ge(pair["scale"], p)
                    for m in range(TOK):
                        act.activation(ond[:, m, :], ps[:, 7, m * P:(m + 1) * P], ACT.Copy,
                                       scale=stat[:, b1 + 24 + m:b1 + 25 + m])
                    act.drain().then_inc(pair["normed_d"], 1)
                    act.wait_ge(pair["sums_m"], p)
                    act.wait_ge(pair["inverse_m"], p)
                    for m in range(TOK):
                        act.activation(onm[:, m, :], ps[:, 6, m * P:(m + 1) * P], ACT.Copy,
                                       scale=stat[:, b1 + 32 + m:b1 + 33 + m])
                    act.drain().then_inc(pair["normed_m"], 1)
                if here:
                    act.wait_ge(pair["max_d"], p + 1)
                    exps([(sbd[:, c, lo:lo + w], stat[:, b + 4 + 2 * t + c:b + 5 + 2 * t + c],
                           stat[:, b + 8 + 2 * t + c:b + 9 + 2 * t + c], 0.125)
                          for t, (lo, w) in enumerate(((0, K0), (K0, L2))) for c in range(2)], p, pair["exp_d"])
            if k == 1 and here:
                act.wait_ge(pair["max_m"], p + 1)
                exps([(pm[odd][:, lo:lo + w], stat[:, b + 28 + t:b + 29 + t], stat[:, b + 30 + t:b + 31 + t],
                       MLA_SCALE) for t, (lo, w) in enumerate(((0, K0), (K0, L2)))], p, pair["exp_m"])
            if k == 2 and here:
                if first >= 1:
                    act.wait_ge(pair["sums_m"], p)
                keep(pair["kept_d"], pair["turned_d"])
            if k == 3 and here:
                act.wait_ge(pair["sums_d"], p + 1)
                if first >= 1:
                    act.wait_ge(pair["back_d"], p)
                for m in range(TOK):
                    act.activation(ond[:, m, :], ps[:, 7, m * P:(m + 1) * P], ACT.Square,
                                   scale=stat[:, b + 12 + 2 * m:b + 13 + 2 * m],
                                   accum_out=stat[:, b + 18 + m:b + 19 + m])
                act.drain().then_inc(pair["squares"], 1)
                keep(pair["kept_m"], pair["turned_m"])

        def attend(kind, k, i, j):
            if kind == "wo" and i == 0 and j == 0 and k == 4:
                act.wait_ge(s_meta, 16)
                act.wait_ge(s_m, 4)
                act.activation(metasq[:, :], metan[:, :], ACT.Square, accum_out=stat[0:META, 24:25])
                act.drain().then_inc(s_mss, 1)
            if kind == "ak" and j == 0 and k == 3:
                act.wait_ge(s_l1, 1)
                act.activation(stat[:, 40:42], stat[:, 40:42], ACT.Exp).then_inc(s_l2, 1)
            if kind == "g":
                quarter(i * 2 + k // 4, k % 4, k // 4)
            if kind == "w2" and i == 0 and j == 0 and k < 2:
                quarter(H, k, 0)
            for turn, b in enumerate(OUT_ORDER):
                if isinstance(i, int) and (kind, k, i, j) == HIGH_AT[turn]:
                    act.wait_ge(s_og, turn + 1)
                    act.activation(oh[:, 4 * b:4 * b + 4, :], gates[:, 4 * b:4 * b + 4, :], ACT.Copy).then_inc(s_oh, 1)
            if kind == "v" and i == 1 and j == 0 and k == 2:
                act.wait_ge(s_grow, 1)
                act.activation(rows[:, 0, :], ps[0:H, 5, 0:S], ACT.Identity, bias=sm("ibias")[0:H, :])
                act.activation(rows[:, 1, :], ps[0:H, 5, S:2 * S], ACT.Abs, bias=sm("fbias")[0:H, :])
                drain()
                act.activation(rows[:, 1, :], rows[:, 1, :], ACT.Exp, scale=-1.0)
                drain()
                act.activation(rows[:, 1, :], rows[:, 1, :], ACT.Ln, bias=1.0).then_inc(s_gact, 1)
            if kind == "v" and i == 1 and j == 0 and k == 5:
                act.wait_ge(s_gB, 1)
                act.activation(rows[:, 2, :], rows[:, 2, :], ACT.Exp, scale=-1.0).then_inc(s_gthr, 1)
            if kind in ("o", "z"):
                h = i * 2 + j
                if k == 1:
                    act.wait_ge(s_arg, h + 1)
                    act.activation(dmat[:, :], darg[:, :], ACT.Exp).then_inc(s_dm, 1)
                if k == 4:
                    act.wait_ge(s_den, h + 1)
                    for m in range(TOK):
                        last = act.activation(ps[:, 5, m * S:m * S + S], ps[:, 6 + m, 0:HD], ACT.Square,
                                              scale=stat[:, 2 + m:3 + m], accum_out=stat[:, 4 + m:5 + m])
                    act.drain().then_inc(s_hsq, 1)
                if k == 7:
                    act.wait_ge(s_ht, h + 1)
                    wait(act, s_y, i)
                    act.activation(work[3][:, 2 * j:2 * j + 2, :],
                                   ps[:, 4, :].rearrange("p (a s) -> p a s", a=2), ACT.Copy).then_inc(s_htc, 1)

        def between():
            for m in range(TOK):
                act.wait_ge(s_x1, m + 1)
                act.activation(xsq[:, 0, :], xr[:, m, :], ACT.Square, accum_out=stat[:, 26 + m:27 + m])
                act.drain().then_inc(s_ss2, 1)
            for b in range(4):
                act.wait_ge(s_xf2, b + 1)
                act.activation(x2h[:, 4 * b:4 * b + 4, META:L2], x2f[b % 2][:, :, :], ACT.Copy).then_inc(s_xh2, 1)

        run(act, split, evac, attend, {"CKQ": between})

    @block.vector
    def _(dve):
        tt, ts, stt = dve.tensor_tensor, dve.tensor_scalar, dve.scalar_tensor_tensor

        def drain():
            dve.drain()

        def split(n, r):
            dve.wait_ge(wh_done, n + 1)
            tt(wl[r][:, :, :], raw[r][:, :, :], wh[r][:, :, :].bitcast(F32), ALU.subtract).then_inc(split_done, 1)

        dve.wait_ge(s_ss, 1)
        for m in range(TOK):
            dve.wait_ge(s_ss, m + 1)
            ts(stat[:, m:m + 1], stat[:, m:m + 1], 1.0 / D, EPS, ALU.mult, ALU.add).then_inc(s_ms, 1)
        for m in range(TOK):
            dve.wait_ge(s_rstd, m + 1)
            ts(xn[:, m, :], xn[:, m, :], stat[:, 2 + m:3 + m], None, ALU.mult).then_inc(s_xn, 1)
        for n in range(LEAD):
            split(n, n)
        dve.wait_ge(s_small, 16)

        def x_low(b):
            dve.wait_ge(s_xh, b + 1)
            tt(xl[:, 4 * b:4 * b + 4, :], xf[b % 2][:, :, :], xh[:, 4 * b:4 * b + 4, :].bitcast(F32),
               ALU.subtract).then_inc(s_xl, 1)

        for b in range(4):
            dve.wait_ge(s_xt, b + 1)
            if b >= 2:
                dve.wait_ge(s_xl, b - 1)
            w = sm("norm_pre", 4 * b, 4)
            tt(xf[b % 2][:, :, :], ps[:, 2 * b:2 * b + 2, :].rearrange("p b (j s) -> p (b j) s", j=2), spread(w, S),
               ALU.mult).then_inc(s_xf, 1)
            if b >= 1:
                x_low(b - 1)
        x_low(3)
        dve.wait_ge(s_wgh, 1)
        tt(wgl[:, :, :], wg[:, :, :], wgh[:, :, :].bitcast(F32), ALU.subtract).then_inc(s_wgl, 1)

        def split_high_low(hi, lo, src, s):
            dve.tensor_copy(hi, src)
            drain()
            tt(lo, src, hi.bitcast(F32), ALU.subtract).then_inc(s, 1)

        def evac(kind, k, i, j, done):
            if kind == "qk":
                q = i * 2 + j
                if k < 3:
                    if k == 0:
                        dve.wait_ge(s_acc, q + 1)
                    sh = k + 1
                    for jj in range(4):
                        last = stt(out=work[0][:, jj, sh:S], in0=banks(j)[:, jj, 0:S - sh],
                                   scalar=small[:, bass.ds(SMALL["conv_w"][0] + q * 16 + 4 * jj + 3 - sh, 1)],
                                   in1=work[0][:, jj, sh:S], op0=ALU.mult, op1=ALU.add)
                    if k == 2:
                        last.then_inc(psum_free[j], 1)
                        dve.drain().then_inc(s_conv, 1)
                    else:
                        drain()
                if k == 4:
                    dve.wait_ge(s_sg, q + 1)
                    tt(qk[:, bass.ds(q * 4, 4), :], work[0][:, :, :], work[1][:, :, :], ALU.mult).then_inc(s_qk, 1)
            if kind == "z":
                t = work[2]
                if k == 1:
                    dve.wait_ge(s_sgz, i + 1)
                    tt(t[:, :, :], banks(1), work[1][:, :, :], ALU.mult).then_inc(psum_free[1], 1)
                    drain()
                if k == 2:
                    for jj in range(4):
                        stt(out=t[:, jj, :], in0=work[0][:, jj, :],
                            scalar=small[:, bass.ds(SMALL["mnorm"][0] + i * 4 + jj, 1)],
                            in1=t[:, jj, :], op0=ALU.mult, op1=ALU.mult)
                    drain()
                if k == 3:
                    dve.wait_ge(s_htc, i * 2 + 3)
                    tt(t[:, :, :], t[:, :, :], work[3][:, :, :], ALU.mult)
                    drain()
                if k == 4:
                    split_high_low(yh[:, bass.ds(i * 4, 4), :], yl[:, bass.ds(i * 4, 4), :], t[:, :, :], s_y)
                    drain()
            if kind == "u":
                u = upad
                if k == 0:
                    dve.wait_ge(s_u, i + 1)
                    tt(wa[:, :, 1:], u[:, :, 1:], u[:, :, :-1], ALU.add)
                    drain()
                if k == 1:
                    tt(wb[:, 2 - 2 * i:, 3:], wa[:, 2 - 2 * i:, 3:], wa[:, 2 - 2 * i:, 1:-2], ALU.add)
                    drain()
                if k == 2 and i == 1:
                    tt(wa[:, :, 7:], wb[:, :, 7:], wb[:, :, 3:-4], ALU.add)
                    drain()
                    tt(wb[:, 2:, 15:], wa[:, 2:, 15:], wa[:, 2:, 7:-8], ALU.add)
                    drain()
                if k == 3:
                    for gg, win in enumerate((wa, wb)):
                        f = slice(2 * gg, 2 * gg + 2)
                        stt(out=pooled[:, f, :], in0=win[:, f, META:], scalar=1.0 / 2 ** (2 * i + gg + 1),
                            in1=u[:, f, META:], op0=ALU.mult, op1=ALU.subtract)
                        inv = cn("inv", 16 * (2 * i + gg), 16).unsqueeze(1).to_broadcast([P, 2, 16])
                        tt(work[3][:, f, 0:16], win[:, f, META:META + 16], inv, ALU.mult)
                    drain()
                    tt(pooled[:, :, 0:16], work[3][:, :, 0:16], u[:, :, META:META + 16], ALU.subtract).then_inc(
                        s_pool, 1)
                    drain()
            if kind == "zb":
                t = work[2]
                if k == 1:
                    dve.wait_ge(s_zsg, i + 1)
                    tt(t[:, :, :], banks(1), work[1][:, :, :], ALU.mult).then_inc(psum_free[1], 1)
                    drain()
                if k == 2:
                    dve.wait_ge(s_pmm, i + 1)
                    for jj in range(4):
                        stt(out=t[:, jj, :], in0=ps[:, 4 + jj // 2, (jj % 2) * S:(jj % 2) * S + S],
                            scalar=sm("pscale", 4 * i + jj, 1), in1=t[:, jj, :], op0=ALU.mult, op1=ALU.mult)
                    drain()
                if k == 3:
                    split_high_low(zh[:, 4 * i:4 * i + 4, :], zl[:, 4 * i:4 * i + 4, :], t[:, :, :], s_zd)
                    drain()
            if kind == "pa" and k == 0:
                dve.wait_ge(slots_done, done)
                dve.wait_ge(s_ga, i + 1)
                tt(work[2][:, :, :], banks(1), work[0][:, :, :], ALU.mult).then_inc(psum_free[1], 1)
            if kind == "pb":
                if k == 0:
                    dve.wait_ge(slots_done, done)
                    dve.wait_ge(s_gb, i + 1)
                    tt(work[3][:, :, :], banks(1), work[1][:, :, :], ALU.mult).then_inc(psum_free[1], 1)
                    drain()
                if k == 1:
                    tt(work[2][:, :, :], work[2][:, :, :], work[3][:, :, :], ALU.add)
                    drain()
                if k == 2:
                    split_high_low(mh[:, bass.ds(i * 4, 4), :], ml[:, bass.ds(i * 4, 4), :], work[2][:, :, :], s_m)
                    drain()
            if kind == "wo" and k == 1:
                q = i * 2 + j
                dve.wait_ge(s_wosq, q + 1)
                dve.wait_ge(s_post, 16)
                c = slice(q * COLS, (q + 1) * COLS)
                tt(on[:, :, c], ps[:, 2 * j:2 * j + 2, :],
                   postw[:, c].unsqueeze(1).to_broadcast([P, TOK, COLS]), ALU.mult).then_inc(psum_free[j], 1)

            if kind == "ckv":
                if k == 2:
                    dve.wait_ge(s_cks, 1)
                    ts(stat[:, 30:33], stat[:, 30:33], 1.0 / S, EPS, ALU.mult, ALU.add).then_inc(s_ckm, 1)
                if k == 4:
                    dve.wait_ge(s_ckr, 1)
                    for m in range(3):
                        ts(ckvn[:, m, 0:S], ckvn[:, m, 0:S], stat[:, 33 + m:34 + m], None, ALU.mult)
                    dve.drain().then_inc(s_ckn, 1)
            if kind == "cq":
                if k == 2:
                    dve.wait_ge(s_cqs, 1)
                    ts(stat[:, 36:38], stat[:, 36:38], 1.0 / COLS, EPS, ALU.mult, ALU.add).then_inc(s_cqm, 1)
                if k == 4:
                    dve.wait_ge(s_cqr, 1)
                    for m in range(TOK):
                        ts(cqn[:, m, :], cqn[:, m, :], stat[:, 38 + m:39 + m], None, ALU.mult)
                    dve.drain().then_inc(s_cqn, 1)
            if kind == "g" and k == 0:
                dve.wait_ge(slots_done, done)
                dve.tensor_copy(gates[:, bass.ds(i * 4, 4), :], banks(0)).then_inc(s_gsum, 1)
            if kind == "g" and k == 2:
                dve.wait_ge(s_gs, i + 1)
                g = gates[:, bass.ds(i * 4, 4), :]
                tt(g, g, work[0][:, :, :], ALU.mult).then_inc(s_gate, 1)
                drain()
            if kind == "w2" and k == 0:
                q = i * 2 + j
                dve.wait_ge(slots_done, done)
                dve.wait_ge(s_x1r, 16)
                c = slice(q * COLS, (q + 1) * COLS)
                tt(yn[:, :, c], ps[:, 2 * j:2 * j + 2, :], x1r[:, :, c], ALU.add).then_inc(s_yn, 1)

        def quarter(p, k, odd):
            first = p if isinstance(p, int) else 2
            here = not isinstance(p, int) or p < H
            b, b1 = 64 + 40 * odd, 64 + 40 * (1 - odd)
            segs = ((0, K0), (K0, L2))
            if k == 0:
                if first >= 1:
                    dve.wait_ge(pair["rstd"], p)
                    tt(stat[:, b1 + 24:b1 + 26], stat[:, b1 + 12:b1 + 16].rearrange("p (t c) -> p t c", c=2)[:, :, 0],
                       stat[:, b1 + 22:b1 + 24], ALU.mult).then_inc(pair["scale"], 1)
                if here:
                    dve.wait_ge(pair["scores_d"], p + 1)
                    for c in range(2):
                        stt(out=sbd[:, c, :], in0=cn("rel"), scalar=const[:, bass.ds(CONST["slope"][0] + p, 1)],
                            in1=ps[:, 2 + c, 0:KEYS], op0=ALU.mult, op1=ALU.add)
                    drain()
                    for t, (lo, w) in enumerate(segs):
                        dve.tensor_reduce(stat[:, b + 2 * t:b + 2 * t + 2], sbd[:, :, lo:lo + w], AX.X, ALU.max)
                    drain()
                    ts(stat[:, b + 4:b + 8], stat[:, b:b + 4], -0.125, None, ALU.mult).then_inc(pair["max_d"], 1)
                    dve.wait_ge(pair["scores_m"], p + 1)
                    tt(pm[odd][:, :], ps[:, 4, 0:KEYS], cn("cmask"), ALU.add)
                    drain()
                    for t, (lo, w) in enumerate(segs):
                        dve.tensor_reduce(stat[:, b + 26 + t:b + 27 + t], pm[odd][:, lo:lo + w], AX.X, ALU.max)
                    drain()
                    ts(stat[:, b + 28:b + 30], stat[:, b + 26:b + 28], -MLA_SCALE, None, ALU.mult).then_inc(
                        pair["max_m"], 1)
            if k == 1:
                if here:
                    dve.wait_ge(pair["exp_d"], p + 1)
                    dve.reciprocal(stat[:, b + 12:b + 16], stat[:, b + 8:b + 12])
                    drain()
                    pairs = stat[:, b + 8:b + 16].rearrange("p (a t c) -> p a t c", a=2, t=2)
                    stt(out=stat[:, b + 16:b + 18], in0=pairs[:, 1, :, 1], scalar=stat[:, 42:43],
                        in1=pairs[:, 0, :, 0], op0=ALU.mult, op1=ALU.mult)
                    drain()
                    for t, (lo, w) in enumerate(segs):
                        stt(out=wmix[:, lo:lo + w], in0=sbd[:, 1, lo:lo + w], scalar=stat[:, b + 16 + t:b + 17 + t],
                            in1=sbd[:, 0, lo:lo + w], op0=ALU.mult, op1=ALU.add)
                    dve.drain().then_inc(pair["mix"], 1)
                if first >= 1:
                    dve.wait_ge(pair["back_m"], p)
                    dve.tensor_copy(oall[:, bass.ds(p + H - 1, 1), :].rearrange("p o s -> p (o s)"),
                                    ps[:, 6, 0:S]).then_inc(pair["out_m"], 1)
                    dve.wait_ge(pair["back_d"], p)
                    ts(oall[:, bass.ds(p - 1, 1), :].rearrange("p o s -> p (o s)"), ps[:, 7, 0:S], sm("subln"), 0.8,
                       ALU.mult, ALU.mult).then_inc(pair["out_d"], 1)
            if k == 2 and here:
                dve.wait_ge(pair["exp_m"], p + 1)
                dve.reciprocal(stat[:, b + 32:b + 34], stat[:, b + 30:b + 32]).then_inc(pair["inverse_m"], 1)
            if k == 3 and here:
                dve.wait_ge(pair["squares"], p + 1)
                ts(stat[:, b + 20:b + 22], stat[:, b + 18:b + 20], 1.0 / P, EPS, ALU.mult, ALU.add).then_inc(
                    pair["mean"], 1)

        def attend(kind, k, i, j):
            if kind == "wo" and j == 0:
                if i == 0 and k == 6:
                    dve.wait_ge(s_mss, 1)
                    ts(stat[0:META, 24:25], stat[0:META, 24:25], 1.0 / D, EPS, ALU.mult, ALU.add).then_inc(s_mms, 1)
                if i == 1 and k == 0:
                    dve.wait_ge(s_mrs, 1)
                    ts(metan[:, :], metan[:, :], stat[0:META, 25:26], None, ALU.mult).then_inc(s_mn, 1)
                if i == 1 and k == 5:
                    dve.wait_ge(s_mt, 1)
                    tt(metat[:, :, :], ps[:, 6, 0:S].rearrange("p (c s) -> p c s", c=KC), spread(sm("attn_norm"), META),
                       ALU.mult).then_inc(s_mtc, 1)
            if kind == "ak" and j == 0 and k == 1:
                lp = sm("lambda").rearrange("p (a b d) -> p a b d", a=2, b=2)
                lt = work[3][:, 3, 0:128].rearrange("p (a d) -> p a d", a=2)
                tt(lt, lp[:, :, 0, :], lp[:, :, 1, :], ALU.mult)
                drain()
                dve.tensor_reduce(stat[:, 40:42], lt, AX.X, ALU.add).then_inc(s_l1, 1)
            if kind == "ak" and j == 0 and k == 7:
                dve.wait_ge(s_l2, 1)
                tt(stat[:, 42:43], stat[:, 41:42], stat[:, 40:41], ALU.subtract)
                drain()
                ts(stat[:, 42:43], stat[:, 42:43], -LAM0, None, ALU.add).then_inc(s_lam, 1)
            if kind == "ak" and j == 1 and k == 5:
                dve.wait_ge(s_ckt, 1)
                for c in range(2):
                    f = work[2 + c][:, 0:2, :].rearrange("p a s -> p (a s)")[:, 0:L2]
                    ts(f, ps[:, 5 + c, 0:L2], sm("kvnorm", c, 1), None, ALU.mult)
                dve.tensor_copy(krs[:, :], ps[:, 7, 0:L2])
                dve.drain().then_inc(s_krs, 1)
                for c in range(2):
                    f = work[2 + c][:, 0:2, :].rearrange("p a s -> p (a s)")[:, 0:L2]
                    dve.tensor_copy(ckh[:, c, 0:L2], f)
                    for t in (ckh, ckl):
                        ts(t[:, c, L2:KVP], ident[:, 0:KVP - L2], 0.0, None, ALU.mult)
                drain()
                for c in range(2):
                    f = work[2 + c][:, 0:2, :].rearrange("p a s -> p (a s)")[:, 0:L2]
                    tt(ckl[:, c, 0:L2], f, ckh[:, c, 0:L2].bitcast(F32), ALU.subtract)
                dve.drain().then_inc(s_ckl, 1)
            if kind == "av" and j == 0 and k == 5:
                dve.wait_ge(s_krm, 1)
                f = work[2][:, 0:2, :].rearrange("p a s -> p (a s)")[:, 0:L2]
                tt(f, ps[:, 7, 0:L2], cn("sin"), ALU.mult)
                tt(kpe[:, :], krs[:, :], cn("cos"), ALU.mult)
                drain()
                tt(kpe[:, :], kpe[:, :], f, ALU.add).then_inc(s_kpe, 1)
                drain()
            if kind == "av" and j == 0 and k == 6:
                dve.wait_ge(s_cqt, 1)
                tt(work[2][:, :, :], ps[:, 5:7, :].rearrange("p b (j s) -> p (b j) s", j=2), spread(sm("qnorm"), S),
                   ALU.mult)
                drain()
                split_high_low(cqh[:, :, :], cql[:, :, :], work[2][:, :, :], s_cql)
            if kind == "aq" and k == 5:
                dve.wait_ge(s_avm, j + 1)
                if j == 0:
                    dve.wait_ge(s_xkept, 16)
                c = slice(j * COLS, (j + 1) * COLS)
                dve.tensor_copy(avn[:, 0:2, c], ps[:, 4:6, :])
                dve.tensor_copy(avn[0:META, 2, c], ps[0:META, 6, :])
                dve.drain().then_inc(s_avn, 1)
            if kind == "uv" and j == 2 and k == 0:
                dve.wait_ge(s_qpm, 1)
                wide = [P, 4, S]
                tt(work[2][:, :, :], ps[:, 4:6, :].rearrange("p b (j s) -> p (b j) s", j=2),
                   cn("sin", META, S).unsqueeze(1).to_broadcast(wide), ALU.mult)
                tt(qp[:, :, :], work[1][:, :, :], cn("cos", META, S).unsqueeze(1).to_broadcast(wide), ALU.mult)
                drain()
                tt(qp[:, :, :], qp[:, :, :], work[2][:, :, :], ALU.add).then_inc(s_qp, 1)
            if kind == "g":
                quarter(i * 2 + k // 4, k % 4, k // 4)
            if kind == "w2" and i == 0 and j == 0 and k < 2:
                quarter(H, k, 0)
            for turn, b in enumerate(OUT_ORDER):
                c = slice(4 * b, 4 * b + 4)
                if isinstance(i, int) and (kind, k, i, j) == HIGH_AT[turn]:
                    if turn == 2:
                        drain()
                    tt(gates[:, c, :], gates[:, c, :], oall[:, c, :], ALU.mult).then_inc(s_og, 1)
                    dve.wait_ge(s_oh, turn + 1)
                    tt(ol[:, c, :], gates[:, c, :], oh[:, c, :].bitcast(F32), ALU.subtract).then_inc(s_ol, 1)
            if kind == "v" and i == 0 and j == 0 and k == 2:
                dve.wait_ge(s_gmm, 1)
                dve.tensor_copy(gsb[:, :, :], ps[:, 4, 0:32].rearrange("p (m g) -> p m g", m=2)).then_inc(s_gsb, 1)
            if kind == "v" and i == 1 and j == 0 and k == 3:
                dve.wait_ge(s_gact, 1)
                ts(rows[:, 2, :], ps[0:H, 5, S:2 * S], sm("fbias")[0:H, :], 0.0, ALU.add, ALU.min)
                dve.memset(rows[:, 5, :], 0.0)
                drain()
                tt(rows[:, 2, :], rows[:, 2, :], rows[:, 1, :], ALU.subtract)
                drain()
                dve.tensor_tensor_scan(rows[:, 3, :], rows[:, 5, :], rows[:, 2, :], 0.0, ALU.add, ALU.add)
                drain()
                tt(rows[:, 4, :], rows[:, 0, :], rows[:, 3, :], ALU.subtract)
                drain()
                dve.tensor_tensor_scan(rows[:, 1, :], rows[:, 5, :], rows[:, 4, :], 0.0, ALU.add, ALU.max)
                drain()
                tt(rows[:, 2, :], rows[:, 3, :], rows[:, 1, :], ALU.add)
                ts(rows[:, 0, :], rows[:, 1, :], -1.0, None, ALU.mult)
                dve.drain().then_inc(s_gB, 1)
            if kind == "o" and isinstance(i, int) and k == 0:
                dve.wait_ge(s_gT, 1)
                dve.tensor_copy(stat[:, 32:64], ps[:, 6, 0:32]).then_inc(s_gcol, 1)
                drain()
            if kind in ("o", "z"):
                h = i * 2 + j
                if k == 1:
                    dve.wait_ge(s_sc, h + 1)
                    for st in range(TOK):
                        w = S - st * P
                        stt(out=darg[:, st * S:st * S + w], in0=ps[:, 4, st * P:S],
                            scalar=stat[:, bass.ds(h + 32 + 8 * st, 1)], in1=cn("dmask", st * S, w),
                            op0=ALU.add, op1=ALU.min)
                    dve.drain().then_inc(s_arg, 1)
                if k == 2:
                    dve.wait_ge(s_dm, h + 1)
                    stt(out=pt[:, :], in0=ps[:, 5, 0:384], scalar=HD ** -0.5, in1=dmat[:, :],
                        op0=ALU.mult, op1=ALU.mult).then_inc(s_pt, 1)
                if k == 4:
                    dve.wait_ge(s_num, h + 1)
                    for m in range(TOK):
                        stt(out=stat[:, m:m + 1], in0=ps[:, 6 + m, HD:VW], scalar=-1.0,
                            in1=stat[:, bass.ds(h + 48 + 8 * m, 1)], op0=ALU.mult, op1=ALU.max)
                    drain()
                    tt(stat[:, 0:2].unsqueeze(2), stat[:, 0:2].unsqueeze(2), ps[:, 6:8, HD:VW], ALU.max)
                    drain()
                    dve.reciprocal(stat[:, 2:4], stat[:, 0:2]).then_inc(s_den, 1)
                if k == 5:
                    dve.wait_ge(s_hsq, h + 1)
                    ts(stat[:, 6:8], stat[:, 4:6], 1.0 / HD, EPS, ALU.mult, ALU.add).then_inc(s_hms, 1)
                if k == 6:
                    dve.wait_ge(s_hrs, h + 1)
                    tt(stat[:, 10:12], stat[:, 2:4], stat[:, 8:10], ALU.mult)
                    drain()
                    for m in range(TOK):
                        ts(hn[:, m, :], ps[:, 6 + m, 0:HD], stat[:, 10 + m:11 + m], None, ALU.mult)
                    dve.drain().then_inc(s_hn, 1)

        def between():
            drain()
            dve.wait_ge(s_wosq, 4)
            dve.tensor_reduce(stat[:, 20:22], stat[:, 12:20].rearrange("p (m q) -> p m q", m=2), AX.X, ALU.add)
            drain()
            ts(stat[:, 20:22], stat[:, 20:22], 1.0 / D, EPS, ALU.mult, ALU.add).then_inc(s_t1, 1)
            dve.wait_ge(s_t2, 1)
            dve.wait_ge(s_xr, 16)
            for m in range(TOK):
                stt(out=xr[:, m, :], in0=on[:, m, :], scalar=stat[:, 22 + m:23 + m], in1=xr[:, m, :],
                    op0=ALU.mult, op1=ALU.add).then_inc(s_x1, 1)
            dve.tensor_copy(x2h[:, :, 0:META], metat[:, :, :])
            drain()
            tt(x2l[:, :, 0:META], metat[:, :, :], x2h[:, :, 0:META].bitcast(F32), ALU.subtract)
            for m in range(TOK):
                dve.wait_ge(s_ss2, m + 1)
                ts(stat[:, 26 + m:27 + m], stat[:, 26 + m:27 + m], 1.0 / D, EPS, ALU.mult, ALU.add).then_inc(s_ms2, 1)
                dve.wait_ge(s_rs2, m + 1)
                ts(on[:, m, :], xr[:, m, :], stat[:, 28 + m:29 + m], None, ALU.mult).then_inc(s_xs, 1)

            def low(b):
                dve.wait_ge(s_xh2, b + 1)
                tt(x2l[:, 4 * b:4 * b + 4, META:L2], x2f[b % 2][:, :, :],
                   x2h[:, 4 * b:4 * b + 4, META:L2].bitcast(F32), ALU.subtract).then_inc(s_xl2, 1)

            for b in range(4):
                dve.wait_ge(s_xt2, b + 1)
                if b >= 2:
                    dve.wait_ge(s_xl2, b - 1)
                tt(x2f[b % 2][:, :, :], ps[:, 2 * b:2 * b + 2, :].rearrange("p b (j s) -> p (b j) s", j=2),
                   spread(sm("attn_norm", 4 * b, 4), S), ALU.mult).then_inc(s_xf2, 1)
                if b >= 1:
                    low(b - 1)
            low(3)

        run(dve, split, evac, attend, {"CKQ": between})

        dve.wait_ge(s_ysq, 4)
        dve.tensor_reduce(stat[:, 20:22], stat[:, 12:20].rearrange("p (m q) -> p m q", m=2), AX.X, ALU.add)
        drain()
        ts(stat[:, 20:22], stat[:, 20:22], 1.0 / D, EPS, ALU.mult, ALU.add).then_inc(s_t4, 1)
        dve.wait_ge(s_t5, 1)
        dve.wait_ge(s_fin, 16)
        for c in range(4):
            m, q = c // 2, slice(c % 2 * 1024, c % 2 * 1024 + 1024)
            stt(out=yn[:, m, q], in0=yn[:, m, q], scalar=stat[:, 22 + m:23 + m], in1=finalw[:, q],
                op0=ALU.mult, op1=ALU.mult).then_inc(s_t6, 1)

    @block.gpsimd
    def _(pool):
        pool.memset(vn[:, :, :].rearrange("p m (h d) -> p m h d", h=H)[:, :, :, HD:VW], 1.0).then_inc(s_one, 1)
        half = cn("half", 0, 2)
        pool.wait_ge(s_const, 16)
        for m in range(TOK):
            pool.wait_ge(s_ms, m + 1)
            pool.tensor_tensor(stat[:, 2 + m:3 + m], stat[:, m:m + 1], half[:, 0:1], ALU.pow).then_inc(s_rstd, 1)

        def set_down(h):
            e = const[0:H, h:h + 1] if isinstance(h, int) else const[0:H, bass.ds(h, 1)]
            pool.tensor_tensor(mrow[:, :], rows[:, 0, :], e.to_broadcast([H, S]), ALU.mult).then_inc(s_kst, 1)
            pool.tensor_copy(kst[:, :, :], qk[:, bass.ds(h * 2 + KC, 2), :]).then_inc(s_kst, 1)

        def rstd(h):
            pool.wait_ge(s_hms, h + 1)
            pool.tensor_tensor(stat[:, 8:10], stat[:, 6:8], half, ALU.pow).then_inc(s_hrs, 1)

        pool.wait_ge(s_gthr, 1)
        pool.wait_ge(s_qk, 8)
        set_down(0)
        with pool.Fori(0, H - 1) as h:
            pool.wait_ge(s_sc, h + 1)
            set_down(h + 1)
            rstd(h)
        pool.wait_ge(s_sc, H)
        pool.memset(upad[:, :, 0:META], 0.0).then_inc(s_pad, 1)
        pool.dma_start(poolw[:, :, :], pool_w).then_inc(s_pw, 16)
        rstd(H - 1)
        pool.wait_ge(slots_done, FIRST["WO"])
        pool.dma_start(postw[:, :], post_w).then_inc(s_post, 16)
        pool.dma_start(xr[:, :, :], x.rearrange("(m p) d -> p m d", p=P)).then_inc(s_xr, 16)
        pool.dma_start(metan[:, :], meta).then_inc(s_meta, 16)
        pool.wait_ge(s_mms, 1)
        pool.tensor_tensor(stat[0:META, 25:26], stat[0:META, 24:25], cn("half", 0, 1, META), ALU.pow).then_inc(s_mrs, 1)
        pool.wait_ge(s_t1, 1)
        pool.tensor_tensor(stat[:, 22:24], stat[:, 20:22], half, ALU.pow).then_inc(s_t2, 1)
        for m in range(TOK):
            pool.wait_ge(s_ms2, m + 1)
            pool.tensor_tensor(stat[:, 28 + m:29 + m], stat[:, 26 + m:27 + m], half[:, 0:1], ALU.pow).then_inc(s_rs2, 1)
        pool.wait_ge(s_x1, 2)
        pool.dma_start(x1_dram, xr[:, :, :]).then_inc(s_xkept, 16)
        const3 = cn("half", 0, 3)
        pool.wait_ge(s_ckm, 1)
        pool.tensor_tensor(stat[:, 33:36], stat[:, 30:33], const3, ALU.pow).then_inc(s_ckr, 1)
        pool.wait_ge(s_cqm, 1)
        pool.tensor_tensor(stat[:, 38:40], stat[:, 36:38], half, ALU.pow).then_inc(s_cqr, 1)

        def set_queries(p):
            pool.tensor_copy(qst[1][:, :], qn[:, bass.ds(p, 1), :].rearrange("p o s -> p (o s)")).then_inc(
                pair["queries"], 1)
            pool.drain()
            for b in range(2):
                r = slice(64 * b, 64 * b + 64)
                pool.tensor_copy(qhalf[b][r, :], aq[r, bass.ds(p, 1), :].rearrange("p o s -> p (o s)")).then_inc(
                    pair["queries"], 1)
            pool.drain()

        def set_rotated(t):
            pool.tensor_copy(qst[2][:, :], qp[:, bass.ds(t, 1), :].rearrange("p o s -> p (o s)")).then_inc(
                pair["queries"], 1)

        def pair_rstd(p, odd):
            b = 64 + 40 * odd
            pool.wait_ge(pair["mean"], p + 1)
            pool.tensor_tensor(stat[:, b + 22:b + 24], stat[:, b + 20:b + 22], half, ALU.pow).then_inc(pair["rstd"], 1)

        pool.wait_ge(s_qp, 1)
        pool.wait_ge(s_k2, 2)
        pool.memset(qhalf[0][64:P, :], 0.0)
        pool.memset(qhalf[1][0:64, :], 0.0)
        pool.drain()
        set_queries(0)
        set_rotated(0)
        with pool.Fori(0, H // 2 - 1) as q:
            pool.wait_ge(pair["scores_m"], q * 2 + 1)
            set_queries(q * 2 + 1)
            set_rotated(q)
            pair_rstd(q * 2, 0)
            pool.wait_ge(pair["scores_m"], q * 2 + 2)
            set_queries(q * 2 + 2)
            set_rotated(q + 1)
            pair_rstd(q * 2 + 1, 1)
        pool.wait_ge(pair["scores_m"], H - 1)
        set_queries(H - 1)
        set_rotated(H // 2 - 1)
        pair_rstd(H - 2, 0)
        pool.wait_ge(pair["scores_m"], H)
        pool.dma_start(finalw[:, :], final_w).then_inc(s_fin, 16)
        pair_rstd(H - 1, 1)
        pool.wait_ge(pair["sums_m"], H)
        pool.dma_start(x1r[:, :, :], x1_dram).then_inc(s_x1r, 16)
        pool.wait_ge(s_t4, 1)
        pool.tensor_tensor(stat[:, 22:24], stat[:, 20:22], half, ALU.pow).then_inc(s_t5, 1)


def small_array(v):
    a = np.zeros((P, SMALL_W), np.float32)

    def put(name, m):
        lo, hi = SMALL[name]
        a[:m.shape[0], lo:hi] = m

    put("norm_pre", v["norm_pre_w"].reshape(KC, P).T)
    put("conv_w", v["qk_conv_w"].reshape(4, 2 * KC, P).transpose(2, 1, 0).reshape(P, 128))
    put("conv_b", v["qk_conv_b"].reshape(2 * KC, P).T)
    put("mnorm", v["mlstm_norm_w"].reshape(KC, P).T)
    put("pscale", v["pool_scale"].reshape(8, P).T)
    put("attn_norm", v["attn_norm_w_2"].reshape(KC, P).T)
    put("qnorm", v["mla_q_norm_w_2"].reshape(4, P).T)
    put("kvnorm", v["mla_kv_norm_w_2"].reshape(2, P).T)
    put("subln", v["diff_subln_w_2"].reshape(1, P).T)
    put("ibias", v["mlstm_i_bias"].reshape(1, H).T)
    put("fbias", v["mlstm_f_bias"].reshape(1, H).T)
    put("lambda", np.tile(v["diff_lambda_2"].reshape(1, 256), (P, 1)))
    return a


def const_array():
    a = np.zeros((P, CONST_W), np.float32)

    def put(name, m):
        lo, hi = CONST[name]
        a[:m.shape[0], lo:hi] = m

    far = -1e30
    put("ident", np.eye(P))
    put("ones", np.ones((P, P)))
    key, tok = np.arange(S)[:, None], np.arange(S)[None, :]
    seen = np.where(key <= tok, 0.0, far)
    put("dmask", np.concatenate([seen[:P, :], seen[P:, P:]], 1))
    inv = np.stack([1.0 / np.minimum(np.arange(1, 17), w) for w in (2, 4, 8, 16)]).reshape(1, 64)
    put("inv", np.tile(inv, (P, 1)))
    pos, kpos = META + np.arange(S)[:, None], np.arange(L2)[None, :]
    rel = np.where(kpos <= pos, kpos - pos, far)
    mask = np.where(kpos <= pos, 0.0, far)
    put("rel", np.concatenate([rel[:P, :K0], rel[P:, :]], 1))
    put("cmask", np.concatenate([mask[:P, :K0], mask[P:, :]], 1))
    slopes = np.exp2(-np.arange(1, 9, dtype=np.float32)) * 8.0
    put("slope", np.tile(slopes, (P, 1)))
    half = 32
    ang = (np.arange(L2, dtype=np.float32)[None, :]
           * (np.float32(10000.0) ** (-np.arange(half, dtype=np.float32) / half))[:, None]).astype(np.float32)
    put("cos", np.tile(np.cos(ang), (4, 1)))
    put("sin", np.tile(np.sin(ang), (4, 1)))
    r = np.zeros((P, P))
    for b in (0, 64):
        for f in range(half):
            r[b + half + f, b + f] = -1.0
            r[b + f, b + half + f] = 1.0
    put("rot", r)
    put("half", np.full((P, 4), -0.5))
    return a


def stream_array(v):
    def groups(w):
        k, n = w.shape
        return w.reshape(k // (SLOT_KC * P), SLOT_KC, P, n // COLS, COLS).transpose(3, 0, 2, 1, 4)

    w_in, w2 = v["w_in"].reshape(D, -1), v["w_in_2"].reshape(D, -1)
    cuts = np.cumsum([0, D, D, D, D, D, H, H, D // 2, D // 2, D, D])
    q, k, vv, o, z, _, _, u, zb, ga, gb = (groups(w_in[:, a:b]) if b - a >= COLS else None
                                           for a, b in zip(cuts, cuts[1:]))
    pa, pb = groups(v["w_proj_mlstm"].reshape(D, D)), groups(v["w_proj_pool"].reshape(D // 2, D))
    wo = groups(v["w_out"].reshape(D, D))
    aq, ak, av, ag = (groups(w2[:, i * 1024:(i + 1) * 1024]) for i in range(4))
    cq, bg = groups(w2[:, 4096:4608]), groups(w2[:, 4928:5952])
    kr = w2[:, 4864:4928]
    ckv = groups(np.concatenate([w2[:, 4608:4864], kr, kr, np.zeros((D, 128), w2.dtype)], 1))
    uq = v["w_uq_2"].reshape(512, H, 192)
    uqn, uqr = groups(uq[:, :, :P].reshape(512, 1024)), groups(uq[:, :, P:].reshape(512, 512))
    ukv = v["w_ukv_2"].reshape(256, H, 2, P)
    uk, uv = groups(ukv[:, :, 0].reshape(256, 1024)), groups(ukv[:, :, 1].reshape(256, 1024))
    w2o = groups(v["w_out_2"].reshape(4, D // 4, D)[list(OUT_ORDER)].reshape(D, D))
    order = [*q, *k, *vv]
    for i in range(4):
        order += [o[i], z[i]]
    for i in range(2):
        order += [u[i], zb[i]]
    for i in range(4):
        order += [ga[i], pa[i], gb[i], pb[i]]
    order += [*wo, *ckv, *cq, *ak, *av, *aq, *uqn, *uqr, *uk, *uv, *ag, *bg, *w2o]
    return np.concatenate(order)


def kernel(**v):
    from contextlib import ExitStack

    import concourse.bacc as bacc
    from concourse.bass_utils import run_bass_kernel_spmd

    v = {name: np.asarray(a) for name, a in v.items()}
    w_in = v["w_in"].reshape(D, -1)
    arrays = {
        "x": v["x"].reshape(S, D),
        "meta": v["meta_tokens_2"],
        "w_stream": stream_array(v),
        "w_gates": np.ascontiguousarray(w_in[:, 5 * D:5 * D + 2 * H].reshape(KC, P, 2 * H).transpose(1, 0, 2)),
        "pool_w": np.ascontiguousarray(v["pool_w"].reshape(4, 2, P, HD).transpose(2, 0, 1, 3).reshape(P, 8, HD)),
        "small": small_array(v),
        "const": const_array(),
        "post_w": np.tile(v["norm_post_w"].reshape(1, D), (P, 1)),
        "final_w": np.tile(v["final_norm_w_2"].reshape(1, D), (P, 1)),
    }
    nc = bacc.Bacc("TRN2", target_bir_lowering=False, num_devices=1)
    args = [nc.dram_tensor(f"in_{name}", a.shape, mybir.dt.from_np(a.dtype), kind="ExternalInput").ap()
            for name, a in arrays.items()]
    out = nc.dram_tensor("out", (S, D), F32, kind="ExternalOutput").ap()
    with ExitStack() as ctx:
        build_program(nc, ctx, *args, out)
    r = run_bass_kernel_spmd(nc, [{f"in_{name}": a for name, a in arrays.items()}], core_ids=[0])
    return r.results[0]["out"].reshape(1, S, D)
```

```python
import math

import numpy as np

import concourse.bass as bass
from concourse import mybir

F32 = mybir.dt.float32
F32R = mybir.dt.float32r
ACT = mybir.ActivationFunctionType
ALU = mybir.AluOpType
AX = mybir.AxisListType

P = 128
D = 2048
S = 256
META = 16
L2 = S + META
KC = D // P
TOK = S // P
H = 8
HD = D // H
VW = HD + 1
EPS = 1e-6
LAM0 = 0.8 - 0.6 * math.exp(-0.3 * 0)
MLA_SCALE = (128 + 64) ** -0.5
COLS = 512
SLOT_KC = 2
SLOT = SLOT_KC * COLS
RING = 4
LEAD = 3
GROUP = KC // SLOT_KC

STAGES = (
    ("QK", ("qk", "qk"), 4),
    ("V", ("v", "v"), 2),
    ("OZ", ("o", "z"), 4),
    ("UZ", ("u", "zb"), 2),
    ("MG", ("ga", "pa", "gb", "pb"), 4),
    ("WO", ("wo", "wo"), 2),
    ("CKQ", ("cq", "ckv"), 1),
    ("AK", ("ak", "ak"), 1),
    ("AV", ("av", "av"), 1),
    ("AQ", ("aq", "aq"), 1),
    ("UQ", ("uq", "uq", "ur"), 1),
    ("UKV", ("uk", "uk", "uv", "uv"), 1),
    ("G", ("g",), 4),
    ("W2", ("w2", "w2"), 2),
)
N_SLOTS = {"pb": 4, "uq": 2, "ur": 2, "uk": 1, "uv": 1}


def slots_of(kind):
    return N_SLOTS.get(kind, GROUP)


def first_slots():
    at, out = 0, {}
    for name, kinds, times in STAGES:
        out[name] = at
        at += times * sum(map(slots_of, kinds))
    return out, at


FIRST, SLOTS = first_slots()
GATE_W = 32 + H
OUT_ORDER = (0, 2, 1, 3)
HIGH_AT = (("g", 1), ("g", 6), ("w2", 1), ("w2", 3))


def slot_turn(n, r):
    return n // RING if isinstance(n, int) else (n - r) // RING


def align(n):
    return n + -n % 32


def packed(parts):
    at, out = 0, {}
    for name, n in parts:
        out[name] = (at, at + n)
        at += n
    return out, at


SMALL, SMALL_W = packed((
    ("norm_pre", 16), ("conv_w", 128), ("conv_b", 32), ("mnorm", 16), ("pscale", 8), ("attn_norm", 16),
    ("qnorm", 4), ("kvnorm", 2), ("subln", 1), ("ibias", 1), ("fbias", 1), ("lambda", 256), ("half", 4), ("ident", 128)))
K0 = 144
KEYS = K0 + L2
CONST, CONST_W = packed((
    ("ones", 128), ("dmask", 384), ("inv", 64), ("rel", KEYS), ("cmask", KEYS),
    ("slope", 8), ("cos", L2), ("sin", L2), ("rot", 128)))


def build_program(nc, ctx, x, meta, w_stream, w_gates, pool_w, small_in, const_in, post_w, final_w, out):
    x1_dram = nc.dram_tensor("x1_kept", (P, TOK, D), F32, kind="Internal").ap()

    BASE = 16512
    R_X, R_C, R_Y, R_Z, R_V, R_T = 49152, 83968, 116736, 149504, 165888, 182336
    KB4 = 4096

    def sb(name, shape, dt, offset):
        return nc.alloc_sbuf_tensor_at(name, shape, dt, offset=BASE + offset)

    raw = [sb(f"raw{r}", [P, SLOT_KC, COLS], F32, r * KB4) for r in range(RING)]
    wh = [sb(f"wh{r}", [P, SLOT_KC, COLS], F32R, (RING + r) * KB4) for r in range(RING)]
    wl = [sb(f"wl{r}", [P, SLOT_KC, COLS], F32R, (2 * RING + r) * KB4) for r in range(RING)]
    xh = sb("xh", [P, KC, S], F32R, R_X)
    xl = sb("xl", [P, KC, S], F32R, R_X + 16384)
    qk = sb("qk", [P, 2 * KC, S], F32, R_C)
    yh = sb("yh", [P, KC, S], F32R, R_Y)
    yl = sb("yl", [P, KC, S], F32R, R_Y + 16384)
    xn = sb("xn", [P, TOK, D], F32, R_Y)
    xsq = sb("xsq", [P, TOK, D], F32, R_C)
    zh = sb("zh", [P, KC // 2, S], F32R, R_Z)
    zl = sb("zl", [P, KC // 2, S], F32R, R_Z + 8192)
    vn = sb("vn", [P, TOK, H * VW], F32, R_V)
    kst = sb("kst", [P, 2, S], F32, R_Z)
    darg = sb("darg", [P, 384], F32, R_Z + 2048)
    dmat = sb("dmat", [P, 384], F32, R_Z + 3584)
    pt = sb("pt", [P, 384], F32, R_Z + 5120)
    hn = sb("hn", [P, TOK, HD], F32, R_Z + 6656)
    mrow = sb("mrow", [H, S], F32, R_Z + 8704)
    rows = sb("rows", [H, 6, S], F32, R_Z + 9728)
    wg = sb("wg", [P, KC, GATE_W], F32, R_Z)
    wgh = sb("wgh", [P, KC, GATE_W], F32R, R_Z + 4 * KC * GATE_W)
    wgl = sb("wgl", [P, KC, GATE_W], F32R, R_Z + 8 * KC * GATE_W)
    mh = sb("mh", [P, KC, S], F32R, R_C)
    ml = sb("ml", [P, KC, S], F32R, R_C + 16384)
    upad = sb("upad", [P, 4, META + S], F32, R_C)
    wa = sb("wa", [P, 4, META + S], F32, R_C + 4352)
    wb = sb("wb", [P, 4, META + S], F32, R_C + 8704)
    pooled = sb("pooled", [P, 4, S], F32, R_C + 13056)
    poolw = sb("poolw", [P, 8, HD], F32, R_C + 17152)
    work = [sb(f"work{b}", [P, 4, S], F32, R_T + b * 4352) for b in range(4)]
    T2 = R_T + 4 * 4352
    small = sb("small", [P, SMALL_W], F32, T2)
    T3 = T2 + align(4 * SMALL_W)
    const = sb("const", [P, CONST_W], F32, T3)
    T4 = T3 + align(4 * CONST_W)
    cqn = sb("cqn", [P, TOK, COLS], F32, R_T)
    diag = sb("diag", [P, TOK, P], F32, R_T + 2 * 4352)
    sqs = sb("sqs", [P, COLS], F32, R_T + 4352)
    sqk = sb("sqk", [P, 2, L2], F32, R_T + 4352)
    diagk = sb("diagk", [P, L2], F32, R_T + 2 * 4352)
    stat = sb("stat", [P, 144], F32, T4)

    x2h = sb("x2h", [P, KC, L2], F32R, R_X)
    x2l = sb("x2l", [P, KC, L2], F32R, R_X + 17408)
    metan = sb("metan", [META, D], F32, R_V)
    metasq = sb("metasq", [META, D], F32, R_T)
    metat = sb("metat", [P, KC, META], F32, R_V + 8192)
    aq = sb("aq", [P, H, S], F32, R_C)
    ak = sb("ak", [P, H, L2], F32, R_C + 8192)
    kn = sb("kn", [P, H, L2], F32, R_C + 16896)
    qp = sb("qp", [P, H // 2, S], F32, R_C + 25600)
    qst = [sb(f"qst{b}", [P, S], F32, R_C + 29696 + 1024 * b) for b in range(3)]
    kpe = sb("kpe", [P, L2], F32, T4 + 576)
    qhalf = [qst[0], small[:, slice(*SMALL["lambda"])]]
    avn = sb("avn", [P, 3, H * P], F32, R_Y)
    vbn = sb("vbn", [P, 3, H * P], F32, R_Y + 12288)
    qn = sb("qn", [P, H, S], F32, R_Y + 24576)
    ckvf = sb("ckvf", [P, 3, L2], F32, R_Z)
    avt = sb("avt", [P, H, L2], F32, R_Z + 4608)
    gates = sb("gates", [P, KC, S], F32, R_Z)
    cqh = sb("cqh", [P, 4, S], F32R, R_V)
    cql = sb("cql", [P, 4, S], F32R, R_V + 4096)
    KVP = 3 * P
    ckh = sb("ckh", [P, 2, KVP], F32R, R_V + 8192)
    ckl = sb("ckl", [P, 2, KVP], F32R, R_V + 8192 + 3072)
    oall = sb("oall", [P, KC, S], F32, R_V)
    W1, W2_, W3 = R_T + 4352, R_T + 2 * 4352, R_T + 3 * 4352
    sbd = sb("sbd", [P, 2, KEYS], F32, W1)
    ond = sb("ond", [P, TOK, P], F32, W1 + 3328)
    wmix = sb("wmix", [P, KEYS], F32, W2_)
    wt = sb("wt", [P, 384], F32, W2_ + 1664)
    wts = sb("wts", [META, S], F32, W2_ + 3200)
    pm = [sb(f"pm{b}", [P, KEYS], F32, W3 + 1664 * b) for b in range(2)]
    onm = sb("onm", [P, TOK, P], F32, W3 + 3328)
    oh = sb("oh", [P, KC, S], F32R, R_V)
    ol = sb("ol", [P, KC, S], F32R, R_Z)
    yn = sb("yn", [P, TOK, D], F32, R_C)
    finalw = sb("finalw", [P, D], F32, R_C + 16384)
    x1r = sb("x1r", [P, TOK, D], F32, R_Y)

    ps = nc.alloc_psum_tensor("ps", [P, 8, 512], F32)

    def sm(name, a=0, n=None):
        lo, hi = SMALL[name]
        return small[:, lo + a:lo + a + (n or hi - lo - a)]

    def cn(name, a=0, n=None, p=P):
        lo, hi = CONST[name]
        return const[0:p, lo + a:lo + a + (n or hi - lo - a)]

    ident = sm("ident")

    def spread(ap, n):
        return ap.unsqueeze(2).to_broadcast([ap.shape[0], ap.shape[1], n])

    on = sb("on", [P, TOK, D], F32, R_Z)
    postw = sb("postw", [P, D], F32, R_X)
    xr = sb("xr", [P, TOK, D], F32, R_Y)

    sems = {}

    def sem(name):
        if name not in sems:
            sems[name] = ctx.enter_context(nc.semaphore(name))
        return sems[name]

    raw_in = [sem(f"raw_in{r}") for r in range(RING)]
    wh_done = sem("wh_done")
    split_done = sem("split_done")
    slots_done = sem("slots_done")
    psum_free = [sem("psum_free0"), sem("psum_free1")]

    def wait(eng, s, v):
        if not isinstance(v, int) or v > 0:
            eng.wait_ge(s, v)

    def group_numbers():
        at, outp = 0, {}
        for name, kinds, times in STAGES:
            outp[name] = at
            at += times * len(kinds)
        return outp

    FIRST_G = group_numbers()

    def pe_group(pe, n, frees, out_at, moving, tiles, tokens, ring=0, kcs=KC, cols=COLS, before=None,
                 chunk=lambda kc: kc):
        hi, lo = moving
        for k in range(kcs // SLOT_KC):
            if before:
                before(k)
            wait(pe, split_done, n + k + 1)
            r = (ring + k) % RING

            def free(c, at):
                if k == 0 and c == 0:
                    for s, v, o in frees:
                        if o == at:
                            wait(pe, s, v)

            for c in range(SLOT_KC):
                kc = k * SLOT_KC + c
                a, z = kc == 0, kc == kcs - 1
                kc = chunk(kc)
                if tiles:
                    for m, t in enumerate(tiles):
                        o = out_at(m)
                        free(c, m)
                        pe.matmul(o, hi[:, kc, t], wh[r][:, c, 0:cols], start=a, stop=False)
                        pe.matmul(o, hi[:, kc, t], wl[r][:, c, 0:cols], start=False, stop=False)
                        last = pe.matmul(o, lo[:, kc, t], wh[r][:, c, 0:cols], start=False, stop=z)
                else:
                    two = tokens.stop - tokens.start <= S
                    for j in range(cols // P):
                        f = slice(j * P, (j + 1) * P)
                        st = a and (j % 2 == 0 or not two)
                        free(c, j)
                        pe.matmul(out_at(j), wh[r][:, c, f], hi[:, kc, tokens], start=st, stop=False,
                                  skip_group_check=True)
                        pe.matmul(out_at(j), wh[r][:, c, f], lo[:, kc, tokens], start=False, stop=False,
                                  skip_group_check=True)
                        last = pe.matmul(out_at(j), wl[r][:, c, f], hi[:, kc, tokens], start=False, stop=z,
                                         skip_group_check=True)
            last.then_inc(slots_done, 1)

    def half_bank(parity):
        return lambda j: ps[:, 2 * parity + j // 2, (j % 2) * S:(j % 2) * S + S]

    def whole_bank(first, width=COLS):
        return lambda m: ps[:, first + m, 0:width]

    def banks(parity):
        return ps[:, 2 * parity:2 * parity + 2, :].rearrange("p b (j s) -> p (b j) s", j=2)

    s_x, s_small, s_const, s_wg = [sem("x_in0"), sem("x_in1")], sem("small_in"), sem("const_in"), sem("wg_in")
    s_ss, s_ms, s_rstd, s_xn = sem("x_squares"), sem("x_mean"), sem("x_rstd"), sem("x_normed")
    s_xt, s_xh, s_xl = sem("x_turned"), sem("x_high"), sem("x_low")
    s_wgh, s_wgl, s_gmm, s_grow = sem("gate_w_high"), sem("gate_w_low"), sem("gate_sums"), sem("gate_rows")
    s_gact, s_gB, s_gthr, s_gT, s_gcol = (sem("gate_log"), sem("gate_scanned"), sem("gate_bound"),
                                          sem("gate_turned"), sem("gate_columns"))
    s_acc, s_conv, s_sg, s_qk, s_v = (sem("conv_first"), sem("conv_done"), sem("conv_sigmoid"), sem("qk_done"),
                                      sem("v_done"))
    s_kst, s_sc, s_arg, s_dm, s_pt, s_num = (sem("head_keys"), sem("head_scores"), sem("head_exponent"),
                                             sem("head_decay"), sem("head_weights"), sem("head_sums"))
    s_den, s_hsq, s_hms, s_hrs, s_hn, s_ht, s_htc = (sem("head_denominator"), sem("head_squares"), sem("head_mean"),
                                                     sem("head_rstd"), sem("head_normed"), sem("head_turned"),
                                                     sem("head_kept"))
    s_sgo, s_sgz, s_y = sem("o_sigmoid"), sem("z_sigmoid"), sem("y_done")
    s_u, s_pool, s_pmm, s_pw, s_zsg, s_zd = (sem("u_kept"), sem("pooled"), sem("pool_mixed"), sem("pool_w_in"),
                                             sem("zb_sigmoid"), sem("yb_done"))
    s_ga, s_gb, s_m = sem("ga_sigmoid"), sem("gb_sigmoid"), sem("merged")
    s_wosq, s_on, s_post, s_xr = sem("out_squares"), sem("out_scaled"), sem("post_w_in"), sem("x_again")
    s_t1, s_t2, s_x1, s_t3 = sem("tail_mean"), sem("tail_rstd"), sem("x1_done"), sem("tail")
    s_out = sem("stored")
    s_meta, s_mss, s_mms, s_mrs, s_mn, s_mt, s_mtc = (sem("meta_in"), sem("meta_squares"), sem("meta_mean"),
                                                      sem("meta_rstd"), sem("meta_normed"), sem("meta_turned"),
                                                      sem("meta_kept"))
    s_xkept, s_ss2, s_ms2, s_rs2, s_xs, s_xt2, s_xh2, s_xl2 = (
        sem("x1_kept"), sem("x1_squares"), sem("x1_mean"), sem("x1_rstd"), sem("x1_normed"), sem("x2_turned"),
        sem("x2_high"), sem("x2_low"))
    s_cks, s_cksum, s_ckm, s_ckr, s_ckd, s_ckb, s_krm, s_ckl, s_kpe = (
        sem("ckv_squares"), sem("ckv_sums"), sem("ckv_mean"), sem("ckv_rstd"), sem("ckv_diagonal"),
        sem("ckv_spread"), sem("kr_rotated"), sem("ckv_low"), sem("kpe_done"))
    s_cqs, s_cqm, s_cqr, s_cqn, s_cqt, s_cql = (sem("cq_squares"), sem("cq_mean"), sem("cq_rstd"),
                                                sem("cq_normed"), sem("cq_turned"), sem("cq_low"))
    s_avt, s_avm, s_avn = sem("av_kept"), sem("av_turned"), sem("av_done")
    s_qpr, s_qpm, s_qp, s_l1, s_l2, s_lam = (sem("qp_raw"), sem("qp_rotated"), sem("qp_done"), sem("lambda_sums"), sem("lambda_exp"),
                                                   sem("lambda_done"))
    s_gsum, s_gs, s_gate = sem("gate_summed"), sem("gate_sigmoid"), sem("gate_done")
    pair = {name: sem("pair_" + name) for name in (
        "queries", "scores_d", "scores_m", "max_d", "exp_d", "mix", "max_m", "exp_m", "turned_d", "kept_d",
        "sums_d", "squares", "mean", "rstd", "scale", "normed_d", "back_d", "out_d", "turned_m", "kept_m",
        "sums_m", "inverse_m", "normed_m", "back_m", "out_m")}
    s_og, s_oh, s_ol, s_fin, s_x1r, s_yn, s_ysq, s_t4, s_t5, s_t6 = (
        sem("out_gated"), sem("out_high"), sem("out_low"), sem("final_w_in"), sem("x1_back"), sem("y_summed"),
        sem("y_squares"), sem("y_mean"), sem("y_rstd"), sem("y_scaled"))
    s_one, s_pad = sem("vn_ones"), sem("pad_zeroed")

    block = ctx.enter_context(nc.Block())

    @block.sync
    def _(sp):
        sp.dma_start(xn[:, 0, :], x[0:P, :]).then_inc(s_x[0], 16)
        sp.dma_start(small[:, :], small_in).then_inc(s_small, 16)
        sp.dma_start(xn[:, 1, :], x[P:S, :]).then_inc(s_x[1], 16)
        for n in range(RING):
            sp.dma_start(raw[n][:, :, :], w_stream[n]).then_inc(raw_in[n], 16)
        sp.dma_start(wg[:, :, :], w_gates).then_inc(s_wg, 16)
        sp.dma_start(const[:, :], const_in).then_inc(s_const, 16)
        with sp.Fori(1, SLOTS // RING) as i:
            for r in range(RING):
                sp.wait_ge(split_done, i * RING + (r - RING + 1))
                sp.dma_start(raw[r][:, :, :], w_stream[bass.ds(i * RING + r, 1), :, :, :].rearrange(
                    "o p c n -> p (o c) n")).then_inc(raw_in[r], 16)
        for n in range(SLOTS - SLOTS % RING, SLOTS):
            sp.wait_ge(split_done, n - RING + 1)
            sp.dma_start(raw[n % RING][:, :, :], w_stream[n]).then_inc(raw_in[n % RING], 16)

        for c in range(4):
            m, q = c // 2, c % 2
            sp.wait_ge(s_t6, c + 1)
            sp.dma_start(out[m * P:(m + 1) * P, q * 1024:(q + 1) * 1024], yn[:, m, q * 1024:(q + 1) * 1024]).then_inc(
                s_out, 16)
        sp.wait_ge(s_xkept, 16)
        sp.wait_ge(s_out, 4 * 16)

    @block.tensor
    def _(pe):
        def turn(o, i, n=P):
            return pe.transpose(o, i, ident[0:n, 0:n])

        def by_feature(rows_, made, s, parts):
            for m, b in parts:
                pe.wait_ge(made, m + 1)
                for c in range(4 * b, 4 * b + 4):
                    last = pe.matmul(ps[:, c // 2, (c % 2) * S + m * P:(c % 2) * S + (m + 1) * P],
                                     rows_[:, m, c * P:(c + 1) * P], diag[:, m, :], start=True, stop=True)
                if m == TOK - 1:
                    last.then_inc(s, 1)

        last_block = [(m, 3) for m in range(TOK)]
        by_feature(xn, s_xn, s_xt, [(m, b) for m in range(TOK) for b in range(3)])

        def groups(name, i, moving, token_kinds=(), before=None):
            kinds = dict((a, b) for a, b, _ in STAGES)[name]
            per = sum(map(slots_of, kinds))
            off = 0
            for j, kind in enumerate(kinds):
                by_token = kind in token_kinds
                pe_group(pe, FIRST[name] + i * per + off,
                         [(psum_free[j % 2], FIRST_G[name] // 2 + i * (len(kinds) // 2) + j // 2, 0)],
                         whole_bank(2 * (j % 2)) if by_token else half_bank(j % 2), moving[kind],
                         [slice(m * P, (m + 1) * P) for m in range(TOK)] if by_token else None, slice(0, S),
                         kcs=slots_of(kind) * SLOT_KC, before=before and (lambda k, j=j, kind=kind: before(j, kind, k)))
                off += slots_of(kind)

        X, Y, Z = (xh, xl), (yh, yl), (zh, zl)

        def x_there(j, kind, k):
            if j == 0 and k == 1:
                by_feature(xn, s_xn, s_xt, last_block)
            pe.wait_ge(s_xl, (k * SLOT_KC + SLOT_KC - 1) // 4 + 1)

        groups("QK", 0, {"qk": X}, before=x_there)
        with pe.Fori(1, 4) as i:
            groups("QK", i, {"qk": X})

        pe.wait_ge(s_wgl, 1)
        for kc in range(KC):
            o = ps[0:GATE_W, 4, 0:S]
            pe.matmul(o, wgh[:, kc, :], xh[:, kc, :], start=kc == 0, stop=False)
            pe.matmul(o, wgl[:, kc, :], xh[:, kc, :], start=False, stop=False)
            last = pe.matmul(o, wgh[:, kc, :], xl[:, kc, :], start=False, stop=kc == KC - 1)
        last.then_inc(s_gmm, 1)

        groups("V", 0, {"v": X}, token_kinds=("v",))
        groups("V", 1, {"v": X}, token_kinds=("v",))
        pe.wait_ge(s_gthr, 1)
        for w, row in enumerate((4, 2)):
            for m in range(TOK):
                last = turn(ps[:, 6, 16 * w + 8 * m:16 * w + 8 * m + 8], rows[:, row, m * P:(m + 1) * P], H)
        last.then_inc(s_gT, 1)

        def head(i, j, k):
            h = i * 2 + j
            if k == 0:
                pe.wait_ge(s_kst, h * 2 + 2)
                pe.wait_ge(s_htc, h + 1)
                pe.matmul(ps[:, 4, 0:S], cn("ones", p=H), mrow[:, :], start=True, stop=True)
                for st in range(TOK):
                    w = S - st * P
                    for dt in range(2):
                        last = pe.matmul(ps[:, 5, st * S:st * S + w], kst[:, dt, st * P:(st + 1) * P],
                                         qk[:, bass.ds(h * 2 + dt, 1), st * P:S].rearrange("p o s -> p (o s)"),
                                         start=dt == 0, stop=dt == 1)
                last.then_inc(s_sc, 1)
            if k == 3:
                pe.wait_ge(s_pt, h + 1)
                for t, st in ((0, 0), (1, 0), (1, 1)):
                    lhs = pt[:, t * P:(t + 1) * P] if st == 0 else pt[:, S:S + P]
                    last = pe.matmul(ps[:, 6 + t, 0:VW], lhs, vn[:, st, bass.ds(h * VW, VW)],
                                     start=st == 0, stop=st == t)
                last.then_inc(s_num, 1)
            if k == 7:
                pe.wait_ge(s_hn, h + 1)
                for dt in range(2):
                    for m in range(TOK):
                        last = turn(ps[:, 4, dt * S + m * P:dt * S + (m + 1) * P], hn[:, m, dt * P:(dt + 1) * P])
                last.then_inc(s_ht, 1)

        pe.wait_ge(s_one, 1)
        pe.wait_ge(s_const, 16)
        with pe.Fori(0, 4) as i:
            groups("OZ", i, {"o": X, "z": X}, before=lambda j, kind, k: head(i, j, k))

        def mix(i, j, k):
            if j == 1 and k == 6:
                pe.wait_ge(s_pool, i + 1)
                pe.wait_ge(s_pw, 16)
                wait(pe, s_zd, i)
                for jj in range(4):
                    for cc in range(2):
                        g = jj // 2
                        last = pe.matmul(ps[:, 4 + g, (jj % 2) * S:(jj % 2) * S + S],
                                         poolw[:, (2 * i + g) * 2 + cc, (jj % 2) * P:(jj % 2) * P + P],
                                         pooled[:, 2 * g + cc, :], start=cc == 0, stop=cc == 1)
                last.then_inc(s_pmm, 1)

        for i in range(2):
            groups("UZ", i, {"u": X, "zb": X}, before=lambda j, kind, k: mix(i, j, k))

        def projected(j, kind, k):
            if kind == "pa" and k == 0:
                pe.wait_ge(s_y, 4)
            if kind == "pb" and k == 0:
                pe.wait_ge(s_zd, 2)

        with pe.Fori(0, 4) as i:
            groups("MG", i, {"ga": X, "pa": Y, "gb": X, "pb": Z}, before=projected)

        def merged_there(i, j, k):
            pe.wait_ge(s_m, (k * SLOT_KC + SLOT_KC - 1) // 4 + 1)
            if i == 1 and j == 0 and k == 2:
                pe.wait_ge(s_mn, 1)
                for c in range(KC):
                    last = turn(ps[:, 6, c * META:(c + 1) * META], metan[:, c * P:(c + 1) * P], META)
                last.then_inc(s_mt, 1)

        for i in range(2):
            groups("WO", i, {"wo": (mh, ml)}, token_kinds=("wo",),
                   before=lambda j, kind, k: merged_there(i, j, k))

        uses = [FIRST_G["CKQ"] // 2, FIRST_G["CKQ"] // 2]
        X2 = (x2h, x2l)
        xtok = [slice(META, META + P), slice(META + P, L2)]
        pe.wait_ge(psum_free[0], uses[0])
        pe.wait_ge(psum_free[1], uses[1])
        pe.wait_ge(s_mtc, 1)
        pe.wait_ge(s_wosq, 4)
        by_feature(xr, s_xs, s_xt2, [(m, b) for b in range(3) for m in range(TOK)])

        def x2_there(k):
            if k == 1:
                by_feature(xr, s_xs, s_xt2, last_block)
            pe.wait_ge(s_xl2, (k * SLOT_KC + SLOT_KC - 1) // 4 + 1)

        def both():
            return [(psum_free[0], uses[0], 0), (psum_free[1], uses[1], 2)]

        def used(*parities):
            for parity in parities:
                uses[parity] += 1

        n = FIRST["CKQ"]
        pe_group(pe, n, [(psum_free[0], uses[0], 0)], whole_bank(0), X2, xtok, None, before=x2_there)
        used(0)
        pe_group(pe, n + GROUP, [(psum_free[1], uses[1], 0)], whole_bank(2, L2), X2, None, slice(0, L2), cols=384)
        used(1)

        def second(stage, j, k):
            if stage == "AK" and j == 0 and k == 2:
                pe.wait_ge(s_cks, 1)
                for m, t in enumerate((0, P, L2 - P)):
                    for c in range(2):
                        last = pe.matmul(ps[:, 5, m:m + 1], sqk[:, c, t:t + P], cn("ones", 0, 1), start=c == 0,
                                         stop=c == 1)
                last.then_inc(s_cksum, 1)
            if stage == "AK" and j == 0 and k == 7:
                pe.wait_ge(s_ckd, 1)
                pe.matmul(ps[:, 6, 0:L2], cn("ones"), diagk[:, :], start=True, stop=True).then_inc(s_ckb, 1)
            if stage == "AV" and j == 0 and k == 2:
                pe.wait_ge(s_ckl, 1)
                pe.matmul(ps[:, 7, 0:L2], cn("rot"), ckvf[:, 2, :], start=True, stop=True).then_inc(s_krm, 1)
                pe.wait_ge(s_cqn, 1)
                for c in range(4):
                    for m in range(TOK):
                        last = turn(ps[:, 5 + c // 2, (c % 2) * S + m * P:(c % 2) * S + (m + 1) * P],
                                    cqn[:, m, c * P:(c + 1) * P])
                last.then_inc(s_cqt, 1)
            if stage == "AQ" and k == 3:
                pe.wait_ge(s_avt, j + 1)
                pe.wait_ge(s_cql, 1)
                pe.wait_ge(s_kpe, 1)
                wait(pe, s_avn, j)
                for kt in range(3):
                    w = min(P, L2 - kt * P)
                    for h in range(4):
                        last = turn(ps[0:w, 4 + kt, h * P:(h + 1) * P], avt[:, 4 * j + h, kt * P:kt * P + w])
                last.then_inc(s_avm, 1)

        for stage in ("AK", "AV"):
            for j in range(2):
                pe_group(pe, FIRST[stage] + j * GROUP, both(), whole_bank(0, L2), X2, None, slice(0, L2),
                         before=lambda k: second(stage, j, k))
                used(0, 1)
        for j in range(2):
            pe_group(pe, FIRST["AQ"] + j * GROUP, [(psum_free[j], uses[j], 0)], half_bank(j), X2, None,
                     slice(META, L2), before=lambda k: second("AQ", j, k))
            used(j)
        n = FIRST["UQ"]
        for j in range(3):
            pe_group(pe, n, [(psum_free[j % 2], uses[j % 2], 0)], half_bank(j % 2), (cqh, cql), None, slice(0, S),
                     kcs=4, ring=n % RING)
            used(j % 2)
            n += 2
        n = FIRST["UKV"]
        for j in range(2):
            pe_group(pe, n, both(), whole_bank(0, L2), (ckh, ckl), None, slice(0, L2), kcs=2, ring=n % RING)
            used(0, 1)
            n += 1
            if j == 0:
                pe.wait_ge(s_qpr, 1)
                pe.wait_ge(s_avn, 2)
                for t in range(4):
                    last = pe.matmul(ps[:, 4 + t // 2, (t % 2) * S:(t % 2) * S + S], cn("rot"), work[1][:, t, :],
                                     start=True, stop=True)
                last.then_inc(s_qpm, 1)
        for j in range(2):
            pe_group(pe, n, both(), whole_bank(0), (ckh, ckl), [slice(t * P, (t + 1) * P) for t in range(3)], None,
                     kcs=2, ring=n % RING)
            used(0, 1)
            n += 1

        def scores(p, odd):
            pe.wait_ge(pair["queries"], p * 4 + 4)
            for c in range(2):
                for t, (lo, w) in enumerate(((0, K0), (K0, L2))):
                    last = pe.matmul(ps[:, 2 + c, lo:lo + w], qhalf[c][:, t * P:(t + 1) * P],
                                     ak[:, bass.ds(p, 1), 0:w].rearrange("p o s -> p (o s)"), start=True, stop=True)
            last.then_inc(pair["scores_d"], 1)
            r = slice(64 * odd, 64 * odd + 64)
            for t, (lo, w) in enumerate(((0, K0), (K0, L2))):
                pe.matmul(ps[:, 4, lo:lo + w], qst[1][:, t * P:(t + 1) * P],
                          kn[:, bass.ds(p, 1), 0:w].rearrange("p o s -> p (o s)"), start=True, stop=False)
                last = pe.matmul(ps[:, 4, lo:lo + w], qst[2][r, t * P:(t + 1) * P], kpe[r, 0:w],
                                 start=False, stop=True)
            last.then_inc(pair["scores_m"], 1)

        def turned(w, s):
            for at, lo in ((0, 0), (P, K0), (2 * P, K0 + P)):
                turn(ps[:, 5, at:at + P], w[:, lo:lo + P])
            for at, lo in ((0, P), (P, K0 + 2 * P)):
                last = turn(ps[0:META, 6, at:at + P], w[:, lo:lo + META])
            last.then_inc(s, 1)

        def weighted(bank, v, h, s):
            hc = bass.ds(h * P, P)
            pe.matmul(ps[:, bank, 0:P], wt[:, 0:P], v[:, 0, hc], start=True, stop=False)
            pe.matmul(ps[:, bank, 0:P], wts[:, 0:P], v[0:META, 1, hc], start=False, stop=True)
            pe.matmul(ps[:, bank, P:2 * P], wt[:, P:2 * P], v[:, 0, hc], start=True, stop=False)
            pe.matmul(ps[:, bank, P:2 * P], wt[:, 2 * P:3 * P], v[:, 1, hc], start=False, stop=False)
            pe.matmul(ps[:, bank, P:2 * P], wts[:, P:2 * P], v[0:META, 2, hc], start=False, stop=True).then_inc(s, 1)

        def back(bank, o, s):
            for m in range(TOK):
                last = turn(ps[:, bank, m * P:(m + 1) * P], o[:, m, :])
            last.then_inc(s, 1)

        def quarter(p, k, odd):
            first = p if isinstance(p, int) else 2
            here = not isinstance(p, int) or p < H
            if k == 0:
                if first >= 1:
                    pe.wait_ge(pair["kept_m"], p)
                    weighted(6, vbn, p - 1, pair["sums_m"])
                if here:
                    if first < 1:
                        pe.wait_ge(s_qp, 1)
                    else:
                        pe.wait_ge(pair["max_m"], p)
                    scores(p, odd)
            if k == 1 and first >= 1:
                pe.wait_ge(pair["normed_m"], p)
                back(6, onm, pair["back_m"])
                pe.wait_ge(pair["normed_d"], p)
                back(7, ond, pair["back_d"])
            if k == 2 and here:
                pe.wait_ge(pair["mix"], p + 1)
                if first >= 1:
                    pe.wait_ge(pair["out_m"], p)
                turned(wmix, pair["turned_d"])
            if k == 3 and here:
                pe.wait_ge(pair["kept_d"], p + 1)
                if first >= 1:
                    pe.wait_ge(pair["out_d"], p)
                weighted(7, avn, p, pair["sums_d"])
                pe.wait_ge(pair["exp_m"], p + 1)
                turned(pm[odd], pair["turned_m"])

        def gate_group(q):
            pe_group(pe, FIRST["G"] + q * GROUP, [(s_gsum, q, 0)] if not isinstance(q, int) or q else [],
                     half_bank(0), X2, None, slice(META, L2), ring=FIRST["G"] % RING,
                     before=lambda k: quarter(q * 2 + k // 4, k % 4, k // 4))

        pe.wait_ge(psum_free[0], uses[0])
        pe.wait_ge(psum_free[1], uses[1])
        gate_group(0)
        with pe.Fori(1, 3) as q:
            gate_group(q)
        gate_group(3)

        for j in range(4):
            def out_there(k):
                if j == 0:
                    if k < 2:
                        quarter(H, k, 0)
                    pe.wait_ge(s_ol, k // 2 + 1)
            pe_group(pe, FIRST["W2"] + j * GROUP, [(s_yn, 2 * (j - 1), 0)] if j >= 2 else [(s_gsum, 4, 0) if j else (pair["max_m"], H, 0)],
                     whole_bank(2 * (1 - j % 2)), (oh, ol), [slice(0, P), slice(P, S)], None,
                     ring=FIRST["W2"] % RING, before=out_there, chunk=lambda kc: OUT_ORDER[kc // 4] * 4 + kc % 4)

    def run(eng, split, evac, attend, attend_late, breaks):
        prev = None
        for name, kinds, times in STAGES:
            if name in breaks:
                for k in range(GROUP):
                    evac(prev[0], k, prev[1], prev[2], FIRST[name])
                breaks[name]()
                prev = None
            per = sum(map(slots_of, kinds))
            n0 = FIRST[name]

            def body(i, prev):
                off = 0
                for j, kind in enumerate(kinds):
                    here = n0 + i * per + off
                    for k in range(slots_of(kind)):
                        if prev and k == 0:
                            evac(prev[0], k, prev[1], prev[2], here)
                        attend(kind, k, i, j)
                        if prev and k > 0 and prev[0] != "g":
                            evac(prev[0], k, prev[1], prev[2], here)
                        if not isinstance(i, int) or here + k + LEAD < SLOTS:
                            split(here + k + LEAD, (n0 + off + k + LEAD) % RING)
                        if prev and k > 0 and prev[0] == "g":
                            evac(prev[0], k, prev[1], prev[2], here)
                        attend_late(kind, k, i, j)
                    prev = (kind, i, j)
                    off += slots_of(kind)
                return prev

            prev = body(0, prev)
            if times > 2:
                last = times - (name == "G")
                with eng.Fori(1, last) as i:
                    body(i, (kinds[-1], i - 1, len(kinds) - 1))
                if last < times:
                    body(last, (kinds[-1], last - 1, len(kinds) - 1))
            elif times == 2:
                body(1, prev)
            prev = (kinds[-1], times - 1, len(kinds) - 1)
        for k in range(GROUP):
            evac(prev[0], k, prev[1], prev[2], SLOTS)

    @block.scalar
    def _(act):
        def drain():
            act.drain()

        def split(n, r):
            act.wait_ge(raw_in[r], 16 * slot_turn(n, r) + 16)
            wait(act, slots_done, n - RING + 1)
            act.activation(wh[r][:, :, :], raw[r][:, :, :], ACT.Copy).then_inc(wh_done, 1)

        act.sem_inc(s_htc, 1)
        for m in range(TOK):
            act.wait_ge(s_x[m], 16)
            act.activation(xsq[:, m, :], xn[:, m, :], ACT.Square, accum_out=stat[:, m:m + 1]).then_inc(s_ss, 1)
        split(0, 0)

        def high_parts(hi, b, name, s):
            for j in range(4):
                c = 4 * b + j
                last = act.activation(hi[:, c, :], ps[:, c // 2, (c % 2) * S:(c % 2) * S + S], ACT.Copy,
                                      scale=sm(name, c, 1))
            last.then_inc(s, 1)

        for b in range(4):
            act.wait_ge(s_xt, b + 1)
            high_parts(xh, b, "norm_pre", s_xh)
            if b + 1 < LEAD:
                split(b + 1, b + 1)

        def evac(kind, k, i, j, done):
            if kind == "qk":
                q = i * 2 + j
                if k == 0:
                    act.wait_ge(slots_done, done)
                    wait(act, s_qk, q)
                    for jj in range(4):
                        last = act.activation(
                            work[0][:, jj, :], banks(j)[:, jj, :], ACT.Identity,
                            bias=small[:, bass.ds(SMALL["conv_b"][0] + q * 4 + jj, 1)],
                            scale=small[:, bass.ds(SMALL["conv_w"][0] + q * 16 + 4 * jj + 3, 1)])
                    last.then_inc(s_acc, 1)
                if k == 3:
                    act.wait_ge(s_conv, q + 1)
                    act.activation(work[1][:, :, :], work[0][:, :, :], ACT.Sigmoid).then_inc(s_sg, 1)
            if kind == "v" and k == 0:
                act.wait_ge(slots_done, done)
                q = i * 2 + j
                for m in range(TOK):
                    last = act.activation(
                        vn[:, m, 2 * q * VW:2 * (q + 1) * VW].rearrange("p (h d) -> p h d", h=2)[:, :, 0:HD],
                        ps[:, 2 * j + m, :].rearrange("p (h d) -> p h d", h=2), ACT.Copy)
                last.then_inc(psum_free[j], 1)
            if kind == "o" and k == 0:
                act.wait_ge(slots_done, done)
                wait(act, s_y, i)
                if isinstance(i, int):
                    act.wait_ge(s_qk, 8)
                act.activation(work[0][:, :, :], banks(0), ACT.Sigmoid).then_inc(psum_free[0], 1)
            if kind == "z" and k == 0:
                act.wait_ge(slots_done, done)
                act.activation(work[1][:, :, :], banks(1), ACT.Sigmoid).then_inc(s_sgz, 1)
            if kind == "u" and k == 0:
                act.wait_ge(slots_done, done)
                wait(act, s_pool, i)
                act.wait_ge(s_pad, 1)
                act.activation(upad[:, :, META:META + S], banks(0), ACT.Copy).then_inc(s_u, 1)
                act.drain().then_inc(psum_free[0], 1)
            if kind == "zb" and k == 0:
                act.wait_ge(slots_done, done)
                act.wait_ge(s_y, 4)
                wait(act, s_zd, i)
                act.activation(work[1][:, :, :], banks(1), ACT.Sigmoid).then_inc(s_zsg, 1)
            if kind == "ga" and k == 0:
                act.wait_ge(slots_done, done)
                wait(act, s_m, i)
                if isinstance(i, int):
                    act.wait_ge(s_zd, 2)
                act.activation(work[0][:, :, :], banks(0), ACT.Sigmoid).then_inc(s_ga, 1)
                act.drain().then_inc(psum_free[0], 1)
            if kind == "gb" and k == 0:
                act.wait_ge(slots_done, done)
                act.activation(work[1][:, :, :], banks(0), ACT.Sigmoid).then_inc(s_gb, 1)
                act.drain().then_inc(psum_free[0], 1)
            if kind == "wo" and k == 0:
                act.wait_ge(slots_done, done)
                act.wait_ge(s_m, 4)
                q = i * 2 + j
                for m in range(TOK):
                    last = act.activation(ps[:, 4 + m, :], ps[:, 2 * j + m, :], ACT.Square,
                                          accum_out=stat[:, 12 + 4 * m + q:13 + 4 * m + q])
                    drain()
                act.drain().then_inc(s_wosq, 1)

            if kind == "ckv" and k == 0:
                act.wait_ge(slots_done, done)
                act.activation(ckvf[:, :, :], ps[:, 2:5, 0:L2], ACT.Copy)
                act.drain().then_inc(psum_free[1], 1)
                act.activation(sqk[:, :, :], ckvf[:, 0:2, :], ACT.Square).then_inc(s_cks, 1)
            if kind == "cq" and k == 0:
                act.wait_ge(slots_done, done)
                act.activation(cqn[:, :, :], ps[:, 0:2, :], ACT.Copy)
                act.drain().then_inc(psum_free[0], 1)
                for m in range(TOK):
                    act.activation(sqs[:, :], cqn[:, m, :], ACT.Square, accum_out=stat[:, 36 + m:37 + m])
                    drain()
                act.drain().then_inc(s_cqs, 1)
            if kind in ("ak", "av", "uk") and k == 0:
                act.wait_ge(slots_done, done)
                to = {"ak": ak, "av": avt, "uk": kn}[kind]
                for b in range(2):
                    act.activation(to[:, 4 * j + 2 * b:4 * j + 2 * b + 2, :], ps[:, 2 * b:2 * b + 2, 0:L2], ACT.Copy)
                    act.drain().then_inc(psum_free[b], 1)
                if kind == "av":
                    act.sem_inc(s_avt, 1)
            if kind in ("aq", "uq") and k == 0:
                act.wait_ge(slots_done, done)
                to = aq if kind == "aq" else qn
                act.activation(to[:, 4 * j:4 * j + 4, :], banks(j), ACT.Copy).then_inc(psum_free[j], 1)
            if kind == "ur" and k == 0:
                act.wait_ge(slots_done, done)
                act.activation(work[1][:, :, :], banks(0), ACT.Copy)
                act.drain().then_inc(psum_free[0], 1)
                act.sem_inc(s_qpr, 1)
            if kind == "uv" and k == 0:
                act.wait_ge(slots_done, done)
                c = slice((j - 2) * COLS, (j - 1) * COLS)
                act.activation(vbn[:, 0:2, c], ps[:, 0:2, :], ACT.Copy)
                act.drain().then_inc(psum_free[0], 1)
                act.activation(vbn[0:META, 2, c], ps[0:META, 2, :], ACT.Copy)
                act.drain().then_inc(psum_free[1], 1)
            if kind == "g" and k == (1 if isinstance(i, int) and i == 3 else 3):
                act.wait_ge(s_gsum, i + 1)
                wait(act, s_gate, i)
                act.activation(work[0][:, :, :], gates[:, bass.ds(i * 4, 4), :], ACT.Sigmoid).then_inc(s_gs, 1)
            if kind == "w2" and k == 1:
                q = i * 2 + j
                for m in range(TOK):
                    act.wait_ge(s_yn, 2 * q + m + 1)
                    act.activation(sqs[:, :], yn[:, m, q * COLS:(q + 1) * COLS], ACT.Square,
                                   accum_out=stat[:, 12 + 4 * m + q:13 + 4 * m + q])
                    drain()
                act.drain().then_inc(s_ysq, 1)

        def exps(parts, p, s):
            for x_, bias, total, scale in parts:
                act.activation(x_, x_, ACT.Exp, bias=bias, scale=scale, accum_out=total)
            act.drain().then_inc(s, 1)

        def quarter(p, k, odd, late):
            first = p if isinstance(p, int) else 2
            here = not isinstance(p, int) or p < H
            b, b1 = 64 + 40 * odd, 64 + 40 * (1 - odd)

            def keep(s, t):
                act.wait_ge(t, p + 1)
                act.activation(wt[:, :], ps[:, 5, 0:384], ACT.Copy)
                act.activation(wts[:, :], ps[0:META, 6, 0:S], ACT.Copy)
                act.drain().then_inc(s, 1)

            if k == 0:
                if first >= 1 and not late:
                    act.wait_ge(pair["scale"], p)
                    for m in range(TOK):
                        act.activation(ond[:, m, :], ps[:, 7, m * P:(m + 1) * P], ACT.Copy,
                                       scale=stat[:, b1 + 24 + m:b1 + 25 + m])
                    act.drain().then_inc(pair["normed_d"], 1)
                    act.wait_ge(pair["sums_m"], p)
                    act.wait_ge(pair["inverse_m"], p)
                    for m in range(TOK):
                        act.activation(onm[:, m, :], ps[:, 6, m * P:(m + 1) * P], ACT.Copy,
                                       scale=stat[:, b1 + 32 + m:b1 + 33 + m])
                    act.drain().then_inc(pair["normed_m"], 1)
                if here and late:
                    act.wait_ge(pair["max_d"], p + 1)
                    exps([(sbd[:, c, lo:lo + w], stat[:, b + 4 + 2 * t + c:b + 5 + 2 * t + c],
                           stat[:, b + 8 + 2 * t + c:b + 9 + 2 * t + c], 0.125)
                          for t, (lo, w) in enumerate(((0, K0), (K0, L2))) for c in range(2)], p, pair["exp_d"])
            if k == 2 and here and late:
                act.wait_ge(pair["max_m"], p + 1)
                exps([(pm[odd][:, lo:lo + w], stat[:, b + 28 + t:b + 29 + t], stat[:, b + 30 + t:b + 31 + t],
                       MLA_SCALE) for t, (lo, w) in enumerate(((0, K0), (K0, L2)))], p, pair["exp_m"])
            if k == 2 and here and not late:
                if first >= 1:
                    act.wait_ge(pair["sums_m"], p)
                keep(pair["kept_d"], pair["turned_d"])
            if k == 3 and here and not late:
                act.wait_ge(pair["sums_d"], p + 1)
                if first >= 1:
                    act.wait_ge(pair["back_d"], p)
                for m in range(TOK):
                    act.activation(ond[:, m, :], ps[:, 7, m * P:(m + 1) * P], ACT.Square,
                                   scale=stat[:, b + 12 + 2 * m:b + 13 + 2 * m],
                                   accum_out=stat[:, b + 18 + m:b + 19 + m])
                act.drain().then_inc(pair["squares"], 1)
                keep(pair["kept_m"], pair["turned_m"])

        def attend(kind, k, i, j):
            if kind == "wo" and i == 0 and j == 0 and k == 4:
                act.wait_ge(s_meta, 16)
                act.wait_ge(s_m, 4)
                act.activation(metasq[:, :], metan[:, :], ACT.Square, accum_out=stat[0:META, 24:25])
                act.drain().then_inc(s_mss, 1)
            if kind == "ak" and j == 0 and k == 3:
                act.wait_ge(s_l1, 1)
                act.activation(stat[:, 40:42], stat[:, 40:42], ACT.Exp).then_inc(s_l2, 1)
            if kind == "g":
                quarter(i * 2 + k // 4, k % 4, k // 4, False)
            if kind == "w2" and i == 0 and j == 0 and k < 2:
                quarter(H, k, 0, False)
            if kind == "qk" and isinstance(i, int) and j == 0 and k == 4:
                act.wait_ge(s_wg, 16)
                act.activation(wgh[:, :, :], wg[:, :, :], ACT.Copy).then_inc(s_wgh, 1)
            if kind == "v" and i == 1 and j == 0 and k == 2:
                act.wait_ge(s_grow, 1)
                act.activation(rows[:, 0, :], rows[:, 0, :], ACT.Identity, bias=sm("ibias")[0:H, :])
                act.activation(rows[:, 1, :], rows[:, 5, :], ACT.Abs, bias=sm("fbias")[0:H, :])
                drain()
                act.activation(rows[:, 1, :], rows[:, 1, :], ACT.Exp, scale=-1.0)
                drain()
                act.activation(rows[:, 1, :], rows[:, 1, :], ACT.Ln, bias=1.0).then_inc(s_gact, 1)
            if kind == "v" and i == 1 and j == 0 and k == 5:
                act.wait_ge(s_gB, 1)
                act.activation(rows[:, 2, :], rows[:, 2, :], ACT.Exp, scale=-1.0).then_inc(s_gthr, 1)
            if kind in ("o", "z"):
                h = i * 2 + j
                if k == 1:
                    act.wait_ge(s_arg, h + 1)
                    act.activation(dmat[:, :], darg[:, :], ACT.Exp).then_inc(s_dm, 1)
                if k == 4:
                    act.wait_ge(s_den, h + 1)
                    for m in range(TOK):
                        last = act.activation(ps[:, 5, m * S:m * S + S], ps[:, 6 + m, 0:HD], ACT.Square,
                                              scale=stat[:, 2 + m:3 + m], accum_out=stat[:, 4 + m:5 + m])
                    act.drain().then_inc(s_hsq, 1)
                if k == 7:
                    act.wait_ge(s_ht, h + 1)
                    wait(act, s_y, i)
                    act.activation(work[3][:, 2 * j:2 * j + 2, :],
                                   ps[:, 4, :].rearrange("p (a s) -> p a s", a=2), ACT.Copy).then_inc(s_htc, 1)

        def between():
            for c in range(4):
                m, q = c // 2, slice(c % 2 * 1024, c % 2 * 1024 + 1024)
                act.wait_ge(s_x1, c + 1)
                act.activation(xsq[:, m, q], xr[:, m, q], ACT.Square, scale=D ** -0.5, accum_out=stat[:, 44 + c:45 + c])
                act.drain().then_inc(s_ss2, 1)
            for b in range(4):
                act.wait_ge(s_xt2, b + 1)
                high_parts(x2h[:, :, META:L2], b, "attn_norm", s_xh2)

        def attend_late(kind, k, i, j):
            if kind == "g":
                quarter(i * 2 + k // 4, k % 4, k // 4, True)
            if kind == "w2" and i == 0 and j == 0 and k < 2:
                quarter(H, k, 0, True)
            if kind == "g" and isinstance(i, int) and i == 3 or kind == "w2" and i == 0 and j == 0:
                for turn, b in enumerate(OUT_ORDER):
                    if (kind, k) == HIGH_AT[turn]:
                        act.wait_ge(s_og, turn + 1)
                        act.activation(oh[:, 4 * b:4 * b + 4, :], gates[:, 4 * b:4 * b + 4, :], ACT.Copy).then_inc(
                            s_oh, 1)

        run(act, split, evac, attend, attend_late, {"CKQ": between})

    @block.vector
    def _(dve):
        tt, ts, stt = dve.tensor_tensor, dve.tensor_scalar, dve.scalar_tensor_tensor

        def drain():
            dve.drain()

        def split(n, r):
            dve.wait_ge(wh_done, n + 1)
            tt(wl[r][:, :, :], raw[r][:, :, :], wh[r][:, :, :].bitcast(F32), ALU.subtract).then_inc(split_done, 1)

        for m in range(TOK):
            dve.wait_ge(s_ss, m + 1)
            ts(stat[:, m:m + 1], stat[:, m:m + 1], 1.0 / D, EPS, ALU.mult, ALU.add).then_inc(s_ms, 1)
            dve.wait_ge(s_rstd, m + 1)
            ts(diag[:, m, :], ident, stat[:, 2 + m:3 + m], None, ALU.mult).then_inc(s_xn, 1)
        split(0, 0)

        def low_parts(lo, hi, b, name, s):
            for j in range(4):
                c = 4 * b + j
                last = stt(out=lo[:, c, :], in0=ps[:, c // 2, (c % 2) * S:(c % 2) * S + S], scalar=sm(name, c, 1),
                           in1=hi[:, c, :].bitcast(F32), op0=ALU.mult, op1=ALU.subtract)
            last.then_inc(s, 1)

        for b in range(4):
            dve.wait_ge(s_xh, b + 1)
            low_parts(xl, xh, b, "norm_pre", s_xl)
            if b + 1 < LEAD:
                split(b + 1, b + 1)

        def split_high_low(hi, lo, src, s):
            dve.tensor_copy(hi, src)
            drain()
            tt(lo, src, hi.bitcast(F32), ALU.subtract).then_inc(s, 1)

        def evac(kind, k, i, j, done):
            if kind == "qk":
                q = i * 2 + j
                if k < 3:
                    if k == 0:
                        dve.wait_ge(s_acc, q + 1)
                    sh = k + 1
                    for jj in range(4):
                        last = stt(out=work[0][:, jj, sh:S], in0=banks(j)[:, jj, 0:S - sh],
                                   scalar=small[:, bass.ds(SMALL["conv_w"][0] + q * 16 + 4 * jj + 3 - sh, 1)],
                                   in1=work[0][:, jj, sh:S], op0=ALU.mult, op1=ALU.add)
                    if k == 2:
                        last.then_inc(psum_free[j], 1)
                        dve.drain().then_inc(s_conv, 1)
                    else:
                        drain()
                if k == 4:
                    dve.wait_ge(s_sg, q + 1)
                    tt(qk[:, bass.ds(q * 4, 4), :], work[0][:, :, :], work[1][:, :, :], ALU.mult).then_inc(s_qk, 1)
            if kind == "z":
                t = work[2]
                if k == 1:
                    dve.wait_ge(s_sgz, i + 1)
                    tt(t[:, :, :], banks(1), work[1][:, :, :], ALU.mult).then_inc(psum_free[1], 1)
                    drain()
                if k == 2:
                    for jj in range(4):
                        stt(out=t[:, jj, :], in0=work[0][:, jj, :],
                            scalar=small[:, bass.ds(SMALL["mnorm"][0] + i * 4 + jj, 1)],
                            in1=t[:, jj, :], op0=ALU.mult, op1=ALU.mult)
                    drain()
                if k == 3:
                    dve.wait_ge(s_htc, i * 2 + 3)
                    tt(t[:, :, :], t[:, :, :], work[3][:, :, :], ALU.mult)
                    drain()
                if k == 4:
                    split_high_low(yh[:, bass.ds(i * 4, 4), :], yl[:, bass.ds(i * 4, 4), :], t[:, :, :], s_y)
                    drain()
            if kind == "u":
                u = upad
                if k == 0:
                    dve.wait_ge(s_u, i + 1)
                    tt(wa[:, :, 1:], u[:, :, 1:], u[:, :, :-1], ALU.add)
                    drain()
                if k == 1:
                    tt(wb[:, 2 - 2 * i:, 3:], wa[:, 2 - 2 * i:, 3:], wa[:, 2 - 2 * i:, 1:-2], ALU.add)
                    drain()
                if k == 2 and i == 1:
                    tt(wa[:, :, 7:], wb[:, :, 7:], wb[:, :, 3:-4], ALU.add)
                    drain()
                    tt(wb[:, 2:, 15:], wa[:, 2:, 15:], wa[:, 2:, 7:-8], ALU.add)
                    drain()
                if k == 3:
                    for gg, win in enumerate((wa, wb)):
                        f = slice(2 * gg, 2 * gg + 2)
                        stt(out=pooled[:, f, :], in0=win[:, f, META:], scalar=1.0 / 2 ** (2 * i + gg + 1),
                            in1=u[:, f, META:], op0=ALU.mult, op1=ALU.subtract)
                        inv = cn("inv", 16 * (2 * i + gg), 16).unsqueeze(1).to_broadcast([P, 2, 16])
                        tt(work[3][:, f, 0:16], win[:, f, META:META + 16], inv, ALU.mult)
                    drain()
                    tt(pooled[:, :, 0:16], work[3][:, :, 0:16], u[:, :, META:META + 16], ALU.subtract).then_inc(
                        s_pool, 1)
                    drain()
            if kind == "zb":
                t = work[2]
                if k == 1:
                    dve.wait_ge(s_zsg, i + 1)
                    tt(t[:, :, :], banks(1), work[1][:, :, :], ALU.mult).then_inc(psum_free[1], 1)
                    drain()
                if k == 2:
                    dve.wait_ge(s_pmm, i + 1)
                    for jj in range(4):
                        stt(out=t[:, jj, :], in0=ps[:, 4 + jj // 2, (jj % 2) * S:(jj % 2) * S + S],
                            scalar=sm("pscale", 4 * i + jj, 1), in1=t[:, jj, :], op0=ALU.mult, op1=ALU.mult)
                    drain()
                if k == 3:
                    split_high_low(zh[:, 4 * i:4 * i + 4, :], zl[:, 4 * i:4 * i + 4, :], t[:, :, :], s_zd)
                    drain()
            if kind == "pa" and k == 0:
                dve.wait_ge(slots_done, done)
                dve.wait_ge(s_ga, i + 1)
                tt(work[2][:, :, :], banks(1), work[0][:, :, :], ALU.mult).then_inc(psum_free[1], 1)
            if kind == "pb":
                if k == 0:
                    dve.wait_ge(slots_done, done)
                    dve.wait_ge(s_gb, i + 1)
                    tt(work[3][:, :, :], banks(1), work[1][:, :, :], ALU.mult).then_inc(psum_free[1], 1)
                    drain()
                if k == 1:
                    tt(work[2][:, :, :], work[2][:, :, :], work[3][:, :, :], ALU.add)
                    drain()
                if k == 2:
                    split_high_low(mh[:, bass.ds(i * 4, 4), :], ml[:, bass.ds(i * 4, 4), :], work[2][:, :, :], s_m)
                    drain()
            if kind == "wo" and k == 1:
                q = i * 2 + j
                dve.wait_ge(s_wosq, q + 1)
                if q == 3:
                    dve.tensor_reduce(stat[:, 20:22], stat[:, 12:20].rearrange("p (m q) -> p m q", m=2), AX.X, ALU.add)
                    drain()
                    ts(stat[:, 20:22], stat[:, 20:22], 1.0 / D, EPS, ALU.mult, ALU.add).then_inc(s_t1, 1)
                dve.wait_ge(s_post, 16)
                c = slice(q * COLS, (q + 1) * COLS)
                tt(on[:, :, c], ps[:, 2 * j:2 * j + 2, :],
                   postw[:, c].unsqueeze(1).to_broadcast([P, TOK, COLS]), ALU.mult).then_inc(psum_free[j], 1)

            if kind == "cq":
                if k == 2:
                    dve.wait_ge(s_cqs, 1)
                    ts(stat[:, 36:38], stat[:, 36:38], 1.0 / COLS, EPS, ALU.mult, ALU.add).then_inc(s_cqm, 1)
                if k == 4:
                    dve.wait_ge(s_cqr, 1)
                    for m in range(TOK):
                        ts(cqn[:, m, :], cqn[:, m, :], stat[:, 38 + m:39 + m], None, ALU.mult)
                    dve.drain().then_inc(s_cqn, 1)
            if kind == "g" and k == 0:
                dve.wait_ge(slots_done, done)
                dve.tensor_copy(gates[:, bass.ds(i * 4, 4), :], banks(0)).then_inc(s_gsum, 1)
            if kind == "g" and k == (2 if isinstance(i, int) and i == 3 else 4):
                dve.wait_ge(s_gs, i + 1)
                g = gates[:, bass.ds(i * 4, 4), :]
                tt(g, g, work[0][:, :, :], ALU.mult).then_inc(s_gate, 1)
                drain()
            if kind == "w2" and k == 0:
                q = i * 2 + j
                dve.wait_ge(slots_done, done)
                dve.wait_ge(s_x1r, 16)
                c = slice(q * COLS, (q + 1) * COLS)
                b = 2 * (1 - j)
                for m in range(TOK):
                    tt(yn[:, m, c], ps[:, b + m, :], x1r[:, m, c], ALU.add).then_inc(s_yn, 1)

        def quarter(p, k, odd, late):
            first = p if isinstance(p, int) else 2
            here = not isinstance(p, int) or p < H
            b, b1 = 64 + 40 * odd, 64 + 40 * (1 - odd)
            segs = ((0, K0), (K0, L2))
            if k == 0 and not late:
                if first >= 1:
                    dve.wait_ge(pair["rstd"], p)
                    tt(stat[:, b1 + 24:b1 + 26], stat[:, b1 + 12:b1 + 16].rearrange("p (t c) -> p t c", c=2)[:, :, 0],
                       stat[:, b1 + 22:b1 + 24], ALU.mult).then_inc(pair["scale"], 1)
                if here:
                    dve.wait_ge(pair["scores_d"], p + 1)
                    for c in range(2):
                        stt(out=sbd[:, c, :], in0=cn("rel"), scalar=const[:, bass.ds(CONST["slope"][0] + p, 1)],
                            in1=ps[:, 2 + c, 0:KEYS], op0=ALU.mult, op1=ALU.add)
                    drain()
                    for t, (lo, w) in enumerate(segs):
                        dve.tensor_reduce(stat[:, b + 2 * t:b + 2 * t + 2], sbd[:, :, lo:lo + w], AX.X, ALU.max)
                    drain()
                    ts(stat[:, b + 4:b + 8], stat[:, b:b + 4], -0.125, None, ALU.mult).then_inc(pair["max_d"], 1)
            if k == 1 and not late:
                if here:
                    dve.wait_ge(pair["exp_d"], p + 1)
                    dve.reciprocal(stat[:, b + 12:b + 16], stat[:, b + 8:b + 12])
                    drain()
                    pairs = stat[:, b + 8:b + 16].rearrange("p (a t c) -> p a t c", a=2, t=2)
                    stt(out=stat[:, b + 16:b + 18], in0=pairs[:, 1, :, 1], scalar=stat[:, 42:43],
                        in1=pairs[:, 0, :, 0], op0=ALU.mult, op1=ALU.mult)
                    drain()
                    for t, (lo, w) in enumerate(segs):
                        stt(out=wmix[:, lo:lo + w], in0=sbd[:, 1, lo:lo + w], scalar=stat[:, b + 16 + t:b + 17 + t],
                            in1=sbd[:, 0, lo:lo + w], op0=ALU.mult, op1=ALU.add)
                    dve.drain().then_inc(pair["mix"], 1)
                if first >= 1:
                    dve.wait_ge(pair["back_m"], p)
                    dve.tensor_copy(oall[:, bass.ds(p + H - 1, 1), :].rearrange("p o s -> p (o s)"),
                                    ps[:, 6, 0:S]).then_inc(pair["out_m"], 1)
                    dve.wait_ge(pair["back_d"], p)
                    ts(oall[:, bass.ds(p - 1, 1), :].rearrange("p o s -> p (o s)"), ps[:, 7, 0:S], sm("subln"), 0.8,
                       ALU.mult, ALU.mult).then_inc(pair["out_d"], 1)
            if k == 1 and late:
                if here:
                    dve.wait_ge(pair["scores_m"], p + 1)
                    tt(pm[odd][:, :], ps[:, 4, 0:KEYS], cn("cmask"), ALU.add)
                    drain()
                    for t, (lo, w) in enumerate(segs):
                        dve.tensor_reduce(stat[:, b + 26 + t:b + 27 + t], pm[odd][:, lo:lo + w], AX.X, ALU.max)
                    drain()
                    ts(stat[:, b + 28:b + 30], stat[:, b + 26:b + 28], -MLA_SCALE, None, ALU.mult).then_inc(
                        pair["max_m"], 1)
            if k == 3 and here and not late:
                dve.wait_ge(pair["exp_m"], p + 1)
                dve.reciprocal(stat[:, b + 32:b + 34], stat[:, b + 30:b + 32]).then_inc(pair["inverse_m"], 1)
                dve.wait_ge(pair["squares"], p + 1)
                ts(stat[:, b + 20:b + 22], stat[:, b + 18:b + 20], 1.0 / P, EPS, ALU.mult, ALU.add).then_inc(
                    pair["mean"], 1)

        def attend(kind, k, i, j):
            if kind == "wo" and j == 0:
                if i == 0 and k == 6:
                    dve.wait_ge(s_mss, 1)
                    ts(stat[0:META, 24:25], stat[0:META, 24:25], 1.0 / D, EPS, ALU.mult, ALU.add).then_inc(s_mms, 1)
                if i == 1 and k == 0:
                    dve.wait_ge(s_mrs, 1)
                    ts(metan[:, :], metan[:, :], stat[0:META, 25:26], None, ALU.mult).then_inc(s_mn, 1)
                if i == 1 and k == 5:
                    dve.wait_ge(s_mt, 1)
                    tt(metat[:, :, :], ps[:, 6, 0:S].rearrange("p (c s) -> p c s", c=KC), spread(sm("attn_norm"), META),
                       ALU.mult).then_inc(s_mtc, 1)
            if kind == "ak" and j == 0 and k == 1:
                lp = sm("lambda").rearrange("p (a b d) -> p a b d", a=2, b=2)
                lt = work[3][:, 3, 0:128].rearrange("p (a d) -> p a d", a=2)
                tt(lt, lp[:, :, 0, :], lp[:, :, 1, :], ALU.mult)
                drain()
                dve.tensor_reduce(stat[:, 40:42], lt, AX.X, ALU.add).then_inc(s_l1, 1)
            if kind == "ak" and j == 0 and k == 7:
                dve.wait_ge(s_l2, 1)
                tt(stat[:, 42:43], stat[:, 41:42], stat[:, 40:41], ALU.subtract)
                drain()
                ts(stat[:, 42:43], stat[:, 42:43], -LAM0, None, ALU.add).then_inc(s_lam, 1)
            if kind == "ak" and j == 0 and k == 3:
                dve.wait_ge(s_cksum, 1)
                ts(stat[:, 30:33], ps[:, 5, 0:3], 1.0 / S, EPS, ALU.mult, ALU.add).then_inc(s_ckm, 1)
            if kind == "ak" and j == 0 and k == 5:
                dve.wait_ge(s_ckr, 1)
                for m, (t, w) in enumerate(((0, P), (P, P), (2 * P, META))):
                    ts(diagk[:, t:t + w], ident[:, P - w:P], stat[:, 33 + m:34 + m], None, ALU.mult)
                dve.drain().then_inc(s_ckd, 1)
            if kind == "ak" and j == 1 and k == 1:
                dve.wait_ge(s_ckb, 1)
                f = [work[2 + c][:, 0:2, :].rearrange("p a s -> p (a s)")[:, 0:L2] for c in range(2)]
                for c in range(2):
                    stt(out=f[c], in0=ckvf[:, c, :], scalar=sm("kvnorm", c, 1), in1=ps[:, 6, 0:L2],
                        op0=ALU.mult, op1=ALU.mult)
                drain()
                for c in range(2):
                    dve.tensor_copy(ckh[:, c, 0:L2], f[c])
                    for t in (ckh, ckl):
                        ts(t[:, c, L2:KVP], ident[:, 0:KVP - L2], 0.0, None, ALU.mult)
                drain()
                for c in range(2):
                    tt(ckl[:, c, 0:L2], f[c], ckh[:, c, 0:L2].bitcast(F32), ALU.subtract)
                dve.drain().then_inc(s_ckl, 1)
            if kind == "av" and j == 0 and k == 5:
                dve.wait_ge(s_krm, 1)
                f = work[2][:, 0:2, :].rearrange("p a s -> p (a s)")[:, 0:L2]
                tt(f, ps[:, 7, 0:L2], cn("sin"), ALU.mult)
                tt(kpe[:, :], ckvf[:, 2, :], cn("cos"), ALU.mult)
                drain()
                tt(kpe[:, :], kpe[:, :], f, ALU.add).then_inc(s_kpe, 1)
                drain()
            if kind == "av" and j == 0 and k == 6:
                dve.wait_ge(s_cqt, 1)
                tt(work[2][:, :, :], ps[:, 5:7, :].rearrange("p b (j s) -> p (b j) s", j=2), spread(sm("qnorm"), S),
                   ALU.mult)
                drain()
                split_high_low(cqh[:, :, :], cql[:, :, :], work[2][:, :, :], s_cql)
            if kind == "aq" and k == 5:
                dve.wait_ge(s_avm, j + 1)
                if j == 0:
                    dve.wait_ge(s_xkept, 16)
                c = slice(j * COLS, (j + 1) * COLS)
                dve.tensor_copy(avn[:, 0:2, c], ps[:, 4:6, :])
                dve.tensor_copy(avn[0:META, 2, c], ps[0:META, 6, :])
                dve.drain().then_inc(s_avn, 1)
            if kind == "uk" and j == 1 and k == 0:
                dve.wait_ge(s_qpm, 1)
                wide = [P, 4, S]
                tt(work[2][:, :, :], ps[:, 4:6, :].rearrange("p b (j s) -> p (b j) s", j=2),
                   cn("sin", META, S).unsqueeze(1).to_broadcast(wide), ALU.mult)
                tt(qp[:, :, :], work[1][:, :, :], cn("cos", META, S).unsqueeze(1).to_broadcast(wide), ALU.mult)
                drain()
                tt(qp[:, :, :], qp[:, :, :], work[2][:, :, :], ALU.add).then_inc(s_qp, 1)
            if kind == "g":
                quarter(i * 2 + k // 4, k % 4, k // 4, False)
            if kind == "w2" and i == 0 and j == 0 and k < 2:
                quarter(H, k, 0, False)
            if kind == "qk" and isinstance(i, int) and j == 0 and k == 5:
                dve.wait_ge(s_wgh, 1)
                tt(wgl[:, :, :], wg[:, :, :], wgh[:, :, :].bitcast(F32), ALU.subtract).then_inc(s_wgl, 1)
            if kind == "v" and i == 0 and j == 0 and k == 2:
                dve.wait_ge(s_gmm, 1)
                dve.tensor_copy(rows[:, 0, :], ps[0:H, 4, 0:S])
                dve.tensor_copy(rows[:, 5, :], ps[32:GATE_W, 4, 0:S])
                dve.drain().then_inc(s_grow, 1)
            if kind == "v" and i == 1 and j == 0 and k == 3:
                dve.wait_ge(s_gact, 1)
                ts(rows[:, 2, :], rows[:, 5, :], sm("fbias")[0:H, :], 0.0, ALU.add, ALU.min)
                drain()
                dve.memset(rows[:, 5, :], 0.0)
                drain()
                tt(rows[:, 2, :], rows[:, 2, :], rows[:, 1, :], ALU.subtract)
                drain()
                dve.tensor_tensor_scan(rows[:, 3, :], rows[:, 5, :], rows[:, 2, :], 0.0, ALU.add, ALU.add)
                drain()
                tt(rows[:, 4, :], rows[:, 0, :], rows[:, 3, :], ALU.subtract)
                drain()
                dve.tensor_tensor_scan(rows[:, 1, :], rows[:, 5, :], rows[:, 4, :], 0.0, ALU.add, ALU.max)
                drain()
                tt(rows[:, 2, :], rows[:, 3, :], rows[:, 1, :], ALU.add)
                ts(rows[:, 0, :], rows[:, 1, :], -1.0, None, ALU.mult)
                dve.drain().then_inc(s_gB, 1)
            if kind == "o" and isinstance(i, int) and k == 0:
                dve.wait_ge(s_gT, 1)
                dve.tensor_copy(stat[:, 32:64], ps[:, 6, 0:32]).then_inc(s_gcol, 1)
                drain()
            if kind in ("o", "z"):
                h = i * 2 + j
                if k == 1:
                    dve.wait_ge(s_sc, h + 1)
                    for st in range(TOK):
                        w = S - st * P
                        stt(out=darg[:, st * S:st * S + w], in0=ps[:, 4, st * P:S],
                            scalar=stat[:, bass.ds(h + 32 + 8 * st, 1)], in1=cn("dmask", st * S, w),
                            op0=ALU.add, op1=ALU.min)
                    dve.drain().then_inc(s_arg, 1)
                if k == 2:
                    dve.wait_ge(s_dm, h + 1)
                    stt(out=pt[:, :], in0=ps[:, 5, 0:384], scalar=HD ** -0.5, in1=dmat[:, :],
                        op0=ALU.mult, op1=ALU.mult).then_inc(s_pt, 1)
                if k == 4:
                    dve.wait_ge(s_num, h + 1)
                    for m in range(TOK):
                        stt(out=stat[:, m:m + 1], in0=ps[:, 6 + m, HD:VW], scalar=-1.0,
                            in1=stat[:, bass.ds(h + 48 + 8 * m, 1)], op0=ALU.mult, op1=ALU.max)
                    drain()
                    tt(stat[:, 0:2].unsqueeze(2), stat[:, 0:2].unsqueeze(2), ps[:, 6:8, HD:VW], ALU.max)
                    drain()
                    dve.reciprocal(stat[:, 2:4], stat[:, 0:2]).then_inc(s_den, 1)
                if k == 5:
                    dve.wait_ge(s_hsq, h + 1)
                    ts(stat[:, 6:8], stat[:, 4:6], 1.0 / HD, EPS, ALU.mult, ALU.add).then_inc(s_hms, 1)
                if k == 6:
                    dve.wait_ge(s_hrs, h + 1)
                    tt(stat[:, 10:12], stat[:, 2:4], stat[:, 8:10], ALU.mult)
                    drain()
                    for m in range(TOK):
                        ts(hn[:, m, :], ps[:, 6 + m, 0:HD], stat[:, 10 + m:11 + m], None, ALU.mult)
                    dve.drain().then_inc(s_hn, 1)

        def between():
            dve.wait_ge(s_xr, 16)
            dve.wait_ge(s_t2, 1)
            drain()
            for c in range(4):
                m, q = c // 2, slice(c % 2 * 1024, c % 2 * 1024 + 1024)
                stt(out=xr[:, m, q], in0=on[:, m, q], scalar=stat[:, 22 + m:23 + m], in1=xr[:, m, q],
                    op0=ALU.mult, op1=ALU.add).then_inc(s_x1, 1)
            for m in range(TOK):
                dve.wait_ge(s_ss2, 2 * m + 2)
                ts(stat[:, 26 + m:27 + m], stat[:, 44 + 2 * m:45 + 2 * m], stat[:, 45 + 2 * m:46 + 2 * m], EPS,
                   ALU.add, ALU.add).then_inc(s_ms2, 1)
                dve.wait_ge(s_rs2, m + 1)
                ts(diag[:, m, :], ident, stat[:, 28 + m:29 + m], None, ALU.mult).then_inc(s_xs, 1)

            dve.tensor_copy(x2h[:, :, 0:META], metat[:, :, :])
            drain()
            tt(x2l[:, :, 0:META], metat[:, :, :], x2h[:, :, 0:META].bitcast(F32), ALU.subtract)
            for b in range(4):
                dve.wait_ge(s_xh2, b + 1)
                low_parts(x2l[:, :, META:L2], x2h[:, :, META:L2], b, "attn_norm", s_xl2)

        def attend_late(kind, k, i, j):
            if kind == "g":
                quarter(i * 2 + k // 4, k % 4, k // 4, True)
            if kind == "w2" and i == 0 and j == 0 and k < 2:
                quarter(H, k, 0, True)
            if kind == "g" and isinstance(i, int) and i == 3 or kind == "w2" and i == 0 and j == 0:
                for turn, b in enumerate(OUT_ORDER):
                    c = slice(4 * b, 4 * b + 4)
                    if (kind, k) == HIGH_AT[turn]:
                        drain()
                        tt(gates[:, c, :], gates[:, c, :], oall[:, c, :], ALU.mult).then_inc(s_og, 1)
                    if (kind, k - 1) == HIGH_AT[turn]:
                        dve.wait_ge(s_oh, turn + 1)
                        tt(ol[:, c, :], gates[:, c, :], oh[:, c, :].bitcast(F32), ALU.subtract).then_inc(s_ol, 1)

        run(dve, split, evac, attend, attend_late, {"CKQ": between})

        dve.wait_ge(s_ysq, 4)
        dve.tensor_reduce(stat[:, 20:22], stat[:, 12:20].rearrange("p (m q) -> p m q", m=2), AX.X, ALU.add)
        drain()
        ts(stat[:, 20:22], stat[:, 20:22], 1.0 / D, EPS, ALU.mult, ALU.add).then_inc(s_t4, 1)
        dve.wait_ge(s_t5, 1)
        dve.wait_ge(s_fin, 16)
        for c in range(4):
            m, q = c // 2, slice(c % 2 * 1024, c % 2 * 1024 + 1024)
            stt(out=yn[:, m, q], in0=yn[:, m, q], scalar=stat[:, 22 + m:23 + m], in1=finalw[:, q],
                op0=ALU.mult, op1=ALU.mult).then_inc(s_t6, 1)

    @block.gpsimd
    def _(pool):
        pool.memset(vn[:, :, :].rearrange("p m (h d) -> p m h d", h=H)[:, :, :, HD:VW], 1.0).then_inc(s_one, 1)
        half = sm("half", 0, 2)
        pool.wait_ge(s_small, 16)
        for m in range(TOK):
            pool.wait_ge(s_ms, m + 1)
            pool.tensor_tensor(stat[:, 2 + m:3 + m], stat[:, m:m + 1], half[:, 0:1], ALU.pow).then_inc(s_rstd, 1)

        def set_down(h):
            e = small[0:H, bass.ds(SMALL["ident"][0] + h, 1)]
            pool.tensor_tensor(mrow[:, :], rows[:, 0, :], e.to_broadcast([H, S]), ALU.mult).then_inc(s_kst, 1)
            pool.tensor_copy(kst[:, :, :], qk[:, bass.ds(h * 2 + KC, 2), :]).then_inc(s_kst, 1)

        def rstd(h):
            pool.wait_ge(s_hms, h + 1)
            pool.tensor_tensor(stat[:, 8:10], stat[:, 6:8], half, ALU.pow).then_inc(s_hrs, 1)

        pool.wait_ge(s_gthr, 1)
        pool.wait_ge(s_qk, 8)
        pool.wait_ge(s_const, 16)
        set_down(0)
        with pool.Fori(0, H - 1) as h:
            pool.wait_ge(s_sc, h + 1)
            set_down(h + 1)
            rstd(h)
        pool.wait_ge(s_sc, H)
        pool.memset(upad[:, :, 0:META], 0.0).then_inc(s_pad, 1)
        pool.dma_start(poolw[:, :, :], pool_w).then_inc(s_pw, 16)
        rstd(H - 1)
        pool.wait_ge(slots_done, FIRST["WO"])
        pool.dma_start(postw[:, :], post_w).then_inc(s_post, 16)
        pool.dma_start(xr[:, :, :], x.rearrange("(m p) d -> p m d", p=P)).then_inc(s_xr, 16)
        pool.dma_start(metan[:, :], meta).then_inc(s_meta, 16)
        pool.wait_ge(s_mms, 1)
        pool.tensor_tensor(stat[0:META, 25:26], stat[0:META, 24:25], sm("half", 0, 1)[0:META, :], ALU.pow).then_inc(s_mrs, 1)
        pool.wait_ge(s_t1, 1)
        pool.tensor_tensor(stat[:, 22:24], stat[:, 20:22], half, ALU.pow).then_inc(s_t2, 1)
        for m in range(TOK):
            pool.wait_ge(s_ms2, m + 1)
            pool.tensor_tensor(stat[:, 28 + m:29 + m], stat[:, 26 + m:27 + m], half[:, 0:1], ALU.pow).then_inc(s_rs2, 1)
        pool.wait_ge(s_x1, 4)
        pool.dma_start(x1_dram, xr[:, :, :]).then_inc(s_xkept, 16)
        const3 = sm("half", 0, 3)
        pool.wait_ge(s_cqm, 1)
        pool.tensor_tensor(stat[:, 38:40], stat[:, 36:38], half, ALU.pow).then_inc(s_cqr, 1)
        pool.wait_ge(s_ckm, 1)
        pool.tensor_tensor(stat[:, 33:36], stat[:, 30:33], const3, ALU.pow).then_inc(s_ckr, 1)

        def set_queries(p):
            pool.tensor_copy(qst[1][:, :], qn[:, bass.ds(p, 1), :].rearrange("p o s -> p (o s)")).then_inc(
                pair["queries"], 1)
            pool.drain()
            for b in range(2):
                r = slice(64 * b, 64 * b + 64)
                pool.tensor_copy(qhalf[b][r, :], aq[r, bass.ds(p, 1), :].rearrange("p o s -> p (o s)")).then_inc(
                    pair["queries"], 1)
            pool.drain()

        def set_rotated(t):
            pool.tensor_copy(qst[2][:, :], qp[:, bass.ds(t, 1), :].rearrange("p o s -> p (o s)")).then_inc(
                pair["queries"], 1)

        def pair_rstd(p, odd):
            b = 64 + 40 * odd
            pool.wait_ge(pair["mean"], p + 1)
            pool.tensor_tensor(stat[:, b + 22:b + 24], stat[:, b + 20:b + 22], half, ALU.pow).then_inc(pair["rstd"], 1)

        pool.wait_ge(s_qp, 1)
        pool.memset(qhalf[0][64:P, :], 0.0)
        pool.memset(qhalf[1][0:64, :], 0.0)
        pool.drain()
        set_queries(0)
        set_rotated(0)
        with pool.Fori(0, H // 2 - 1) as q:
            pool.wait_ge(pair["scores_m"], q * 2 + 1)
            set_queries(q * 2 + 1)
            set_rotated(q)
            pair_rstd(q * 2, 0)
            pool.wait_ge(pair["scores_m"], q * 2 + 2)
            set_queries(q * 2 + 2)
            set_rotated(q + 1)
            pair_rstd(q * 2 + 1, 1)
        pool.wait_ge(pair["scores_m"], H - 1)
        set_queries(H - 1)
        set_rotated(H // 2 - 1)
        pair_rstd(H - 2, 0)
        pool.wait_ge(pair["scores_m"], H)
        pool.dma_start(finalw[:, :], final_w).then_inc(s_fin, 16)
        pair_rstd(H - 1, 1)
        pool.wait_ge(pair["sums_m"], H)
        pool.dma_start(x1r[:, :, :], x1_dram).then_inc(s_x1r, 16)
        pool.wait_ge(s_t4, 1)
        pool.tensor_tensor(stat[:, 22:24], stat[:, 20:22], half, ALU.pow).then_inc(s_t5, 1)


def small_array(v):
    a = np.zeros((P, SMALL_W), np.float32)

    def put(name, m):
        lo, hi = SMALL[name]
        a[:m.shape[0], lo:hi] = m

    put("norm_pre", v["norm_pre_w"].reshape(KC, P).T)
    put("conv_w", v["qk_conv_w"].reshape(4, 2 * KC, P).transpose(2, 1, 0).reshape(P, 128))
    put("conv_b", v["qk_conv_b"].reshape(2 * KC, P).T)
    put("mnorm", v["mlstm_norm_w"].reshape(KC, P).T)
    put("pscale", v["pool_scale"].reshape(8, P).T)
    put("attn_norm", v["attn_norm_w_2"].reshape(KC, P).T)
    put("qnorm", v["mla_q_norm_w_2"].reshape(4, P).T)
    put("kvnorm", v["mla_kv_norm_w_2"].reshape(2, P).T)
    put("subln", v["diff_subln_w_2"].reshape(1, P).T)
    put("ibias", v["mlstm_i_bias"].reshape(1, H).T)
    put("fbias", v["mlstm_f_bias"].reshape(1, H).T)
    put("ident", np.eye(P))
    put("half", np.full((P, 4), -0.5))
    put("lambda", np.tile(v["diff_lambda_2"].reshape(1, 256), (P, 1)))
    return a


def gates_array(w):
    a = np.zeros((P, KC, GATE_W), np.float32)
    w = w.reshape(KC, P, 2 * H).transpose(1, 0, 2)
    a[:, :, 0:H], a[:, :, 32:GATE_W] = w[:, :, 0:H], w[:, :, H:]
    return a


def const_array():
    a = np.zeros((P, CONST_W), np.float32)

    def put(name, m):
        lo, hi = CONST[name]
        a[:m.shape[0], lo:hi] = m

    far = -1e30
    put("ones", np.ones((P, P)))
    key, tok = np.arange(S)[:, None], np.arange(S)[None, :]
    seen = np.where(key <= tok, 0.0, far)
    put("dmask", np.concatenate([seen[:P, :], seen[P:, P:]], 1))
    inv = np.stack([1.0 / np.minimum(np.arange(1, 17), w) for w in (2, 4, 8, 16)]).reshape(1, 64)
    put("inv", np.tile(inv, (P, 1)))
    pos, kpos = META + np.arange(S)[:, None], np.arange(L2)[None, :]
    rel = np.where(kpos <= pos, kpos - pos, far)
    mask = np.where(kpos <= pos, 0.0, far)
    put("rel", np.concatenate([rel[:P, :K0], rel[P:, :]], 1))
    put("cmask", np.concatenate([mask[:P, :K0], mask[P:, :]], 1))
    slopes = np.exp2(-np.arange(1, 9, dtype=np.float32)) * 8.0
    put("slope", np.tile(slopes, (P, 1)))
    half = 32
    ang = (np.arange(L2, dtype=np.float32)[None, :]
           * (np.float32(10000.0) ** (-np.arange(half, dtype=np.float32) / half))[:, None]).astype(np.float32)
    put("cos", np.tile(np.cos(ang), (4, 1)))
    put("sin", np.tile(np.sin(ang), (4, 1)))
    r = np.zeros((P, P))
    for b in (0, 64):
        for f in range(half):
            r[b + half + f, b + f] = -1.0
            r[b + f, b + half + f] = 1.0
    put("rot", r)
    return a


def stream_array(v):
    def groups(w):
        k, n = w.shape
        return w.reshape(k // (SLOT_KC * P), SLOT_KC, P, n // COLS, COLS).transpose(3, 0, 2, 1, 4)

    w_in, w2 = v["w_in"].reshape(D, -1), v["w_in_2"].reshape(D, -1)
    cuts = np.cumsum([0, D, D, D, D, D, H, H, D // 2, D // 2, D, D])
    q, k, vv, o, z, _, _, u, zb, ga, gb = (groups(w_in[:, a:b]) if b - a >= COLS else None
                                           for a, b in zip(cuts, cuts[1:]))
    pa, pb = groups(v["w_proj_mlstm"].reshape(D, D)), groups(v["w_proj_pool"].reshape(D // 2, D))
    wo = groups(v["w_out"].reshape(D, D))
    aq, ak, av, ag = (groups(w2[:, i * 1024:(i + 1) * 1024]) for i in range(4))
    cq, bg = groups(w2[:, 4096:4608]), groups(w2[:, 4928:5952])
    kr = w2[:, 4864:4928]
    ckv = groups(np.concatenate([w2[:, 4608:4864], kr, kr, np.zeros((D, 128), w2.dtype)], 1))
    uq = v["w_uq_2"].reshape(512, H, 192)
    uqn, uqr = groups(uq[:, :, :P].reshape(512, 1024)), groups(uq[:, :, P:].reshape(512, 512))
    ukv = v["w_ukv_2"].reshape(256, H, 2, P)
    uk, uv = groups(ukv[:, :, 0].reshape(256, 1024)), groups(ukv[:, :, 1].reshape(256, 1024))
    w2o = groups(v["w_out_2"].reshape(4, D // 4, D)[list(OUT_ORDER)].reshape(D, D))
    order = [*q, *k, *vv]
    for i in range(4):
        order += [o[i], z[i]]
    for i in range(2):
        order += [u[i], zb[i]]
    for i in range(4):
        order += [ga[i], pa[i], gb[i], pb[i]]
    order += [*wo, *cq, *ckv, *ak, *av, *aq, *uqn, *uqr, *uk, *uv, *ag, *bg, *w2o]
    return np.concatenate(order)


def kernel(**v):
    from contextlib import ExitStack

    import concourse.bacc as bacc
    from concourse.bass_utils import run_bass_kernel_spmd

    v = {name: np.asarray(a) for name, a in v.items()}
    w_in = v["w_in"].reshape(D, -1)
    arrays = {
        "x": v["x"].reshape(S, D),
        "meta": v["meta_tokens_2"],
        "w_stream": stream_array(v),
        "w_gates": gates_array(w_in[:, 5 * D:5 * D + 2 * H]),
        "pool_w": np.ascontiguousarray(v["pool_w"].reshape(4, 2, P, HD).transpose(2, 0, 1, 3).reshape(P, 8, HD)),
        "small": small_array(v),
        "const": const_array(),
        "post_w": np.tile(v["norm_post_w"].reshape(1, D), (P, 1)),
        "final_w": np.tile(v["final_norm_w_2"].reshape(1, D), (P, 1)),
    }
    nc = bacc.Bacc("TRN2", target_bir_lowering=False, num_devices=1)
    args = [nc.dram_tensor(f"in_{name}", a.shape, mybir.dt.from_np(a.dtype), kind="ExternalInput").ap()
            for name, a in arrays.items()]
    out = nc.dram_tensor("out", (S, D), F32, kind="ExternalOutput").ap()
    with ExitStack() as ctx:
        build_program(nc, ctx, *args, out)
    r = run_bass_kernel_spmd(nc, [{f"in_{name}": a for name, a in arrays.items()}], core_ids=[0])
    return r.results[0]["out"].reshape(1, S, D)
```

```python
import math

import numpy as np

import concourse.bass as bass
from concourse import mybir

F32 = mybir.dt.float32
F32R = mybir.dt.float32r
ACT = mybir.ActivationFunctionType
ALU = mybir.AluOpType
AX = mybir.AxisListType

P = 128
D = 2048
S = 256
META = 16
L2 = S + META
KC = D // P
TOK = S // P
H = 8
HD = D // H
VW = HD + 1
EPS = 1e-6
LAM0 = 0.8 - 0.6 * math.exp(-0.3 * 0)
MLA_SCALE = (128 + 64) ** -0.5
COLS = 512
SLOT_KC = 2
SLOT = SLOT_KC * COLS
RING = 4
LEAD = 3
GROUP = KC // SLOT_KC

STAGES = (
    ("QK", ("qk", "qk"), 4),
    ("V", ("v", "v"), 2),
    ("OZ", ("o", "z"), 4),
    ("UZ", ("u", "zb"), 2),
    ("MG", ("ga", "pa", "gb", "pb"), 4),
    ("WO", ("wo", "wo"), 2),
    ("CKQ", ("cq", "ckv"), 1),
    ("AK", ("ak", "ak"), 1),
    ("AV", ("av", "av"), 1),
    ("AQ", ("aq", "aq"), 1),
    ("UQ", ("uq", "uq", "ur"), 1),
    ("UKV", ("uk", "uk", "uv", "uv"), 1),
    ("G", ("g",), 4),
    ("W2", ("w2", "w2"), 2),
)
N_SLOTS = {"pb": 4, "uq": 2, "ur": 2, "uk": 1, "uv": 1}


def slots_of(kind):
    return N_SLOTS.get(kind, GROUP)


def first_slots():
    at, out = 0, {}
    for name, kinds, times in STAGES:
        out[name] = at
        at += times * sum(map(slots_of, kinds))
    return out, at


FIRST, SLOTS = first_slots()
GATE_W = 32 + H
OUT_ORDER = (0, 2, 1, 3)
HIGH_AT = (("g", 0), ("g", 7), ("w2", 1), ("w2", 3))
LOW_AT = (("g", 1), ("w2", 0), ("w2", 2), ("w2", 4))


def slot_turn(n, r):
    return n // RING if isinstance(n, int) else (n - r) // RING


def align(n):
    return n + -n % 32


def packed(parts):
    at, out = 0, {}
    for name, n in parts:
        out[name] = (at, at + n)
        at += n
    return out, at


SMALL, SMALL_W = packed((
    ("norm_pre", 16), ("conv_w", 128), ("conv_b", 32), ("mnorm", 16), ("pscale", 8), ("attn_norm", 16),
    ("qnorm", 4), ("kvnorm", 2), ("subln", 1), ("ibias", 1), ("fbias", 1), ("lambda", 256), ("half", 4), ("ident", 128)))
K0 = 144
KEYS = K0 + L2
CONST, CONST_W = packed((
    ("ones", 128), ("dmask", 384), ("inv", 64), ("rel", KEYS), ("cmask", KEYS),
    ("slope", 8), ("cos", L2), ("sin", L2), ("rot", 128)))


def build_program(nc, ctx, x, meta, w_stream, w_gates, pool_w, small_in, const_in, post_w, final_w, out):
    x1_dram = nc.dram_tensor("x1_kept", (P, TOK, D), F32, kind="Internal").ap()

    BASE = 16512
    R_X, R_C, R_Y, R_Z, R_V, R_T = 49152, 83968, 116736, 149504, 165888, 182336
    KB4 = 4096

    def sb(name, shape, dt, offset):
        return nc.alloc_sbuf_tensor_at(name, shape, dt, offset=BASE + offset)

    raw = [sb(f"raw{r}", [P, SLOT_KC, COLS], F32, r * KB4) for r in range(RING)]
    wh = [sb(f"wh{r}", [P, SLOT_KC, COLS], F32R, (RING + r) * KB4) for r in range(RING)]
    wl = [sb(f"wl{r}", [P, SLOT_KC, COLS], F32R, (2 * RING + r) * KB4) for r in range(RING)]
    xh = sb("xh", [P, KC, S], F32R, R_X)
    xl = sb("xl", [P, KC, S], F32R, R_X + 16384)
    qk = sb("qk", [P, 2 * KC, S], F32, R_C)
    yh = sb("yh", [P, KC, S], F32R, R_Y)
    yl = sb("yl", [P, KC, S], F32R, R_Y + 16384)
    xn = sb("xn", [P, TOK, D], F32, R_Y)
    xsq = sb("xsq", [P, TOK, D], F32, R_C)
    zh = sb("zh", [P, KC // 2, S], F32R, R_Z)
    zl = sb("zl", [P, KC // 2, S], F32R, R_Z + 8192)
    vn = sb("vn", [P, TOK, H * VW], F32, R_V)
    kst = sb("kst", [P, 2, S], F32, R_Z)
    darg = sb("darg", [P, 384], F32, R_Z + 2048)
    dmat = sb("dmat", [P, 384], F32, R_Z + 3584)
    pt = sb("pt", [P, 384], F32, R_Z + 5120)
    hn = sb("hn", [P, TOK, HD], F32, R_Z + 6656)
    mrow = sb("mrow", [H, S], F32, R_Z + 8704)
    rows = sb("rows", [H, 6, S], F32, R_Z + 9728)
    wg = sb("wg", [P, KC, GATE_W], F32, R_Z)
    wgh = sb("wgh", [P, KC, GATE_W], F32R, R_Z + 4 * KC * GATE_W)
    wgl = sb("wgl", [P, KC, GATE_W], F32R, R_Z + 8 * KC * GATE_W)
    mh = sb("mh", [P, KC, S], F32R, R_C)
    ml = sb("ml", [P, KC, S], F32R, R_C + 16384)
    upad = sb("upad", [P, 4, META + S], F32, R_C)
    wa = sb("wa", [P, 4, META + S], F32, R_C + 4352)
    wb = sb("wb", [P, 4, META + S], F32, R_C + 8704)
    pooled = sb("pooled", [P, 4, S], F32, R_C + 13056)
    poolw = sb("poolw", [P, 8, HD], F32, R_C + 17152)
    work = [sb(f"work{b}", [P, 4, S], F32, R_T + b * 4352) for b in range(4)]
    T2 = R_T + 4 * 4352
    small = sb("small", [P, SMALL_W], F32, T2)
    T3 = T2 + align(4 * SMALL_W)
    const = sb("const", [P, CONST_W], F32, T3)
    T4 = T3 + align(4 * CONST_W)
    cqn = sb("cqn", [P, TOK, COLS], F32, R_T)
    diag = sb("diag", [P, TOK, P], F32, R_T + 2 * 4352)
    sqs = sb("sqs", [P, COLS], F32, R_T + 4352)
    sqk = sb("sqk", [P, 2, L2], F32, R_T + 4352)
    diagk = sb("diagk", [P, L2], F32, R_T + 2 * 4352)
    stat = sb("stat", [P, 144], F32, T4)

    x2h = sb("x2h", [P, KC, L2], F32R, R_X)
    x2l = sb("x2l", [P, KC, L2], F32R, R_X + 17408)
    metan = sb("metan", [META, D], F32, R_V)
    metasq = sb("metasq", [META, D], F32, R_T)
    metat = sb("metat", [P, KC, META], F32, R_V + 8192)
    aq = sb("aq", [P, H, S], F32, R_C)
    ak = sb("ak", [P, H, L2], F32, R_C + 8192)
    kn = sb("kn", [P, H, L2], F32, R_C + 16896)
    qp = sb("qp", [P, H // 2, S], F32, R_C + 25600)
    qst = [sb(f"qst{b}", [P, S], F32, R_C + 29696 + 1024 * b) for b in range(3)]
    kpe = sb("kpe", [P, L2], F32, T4 + 576)
    qhalf = [qst[0], small[:, slice(*SMALL["lambda"])]]
    avn = sb("avn", [P, 3, H * P], F32, R_Y)
    vbn = sb("vbn", [P, 3, H * P], F32, R_Y + 12288)
    qn = sb("qn", [P, H, S], F32, R_Y + 24576)
    ckvf = sb("ckvf", [P, 3, L2], F32, R_Z)
    avt = sb("avt", [P, H, L2], F32, R_Z + 4608)
    gates = sb("gates", [P, KC, S], F32, R_Z)
    cqh = sb("cqh", [P, 4, S], F32R, R_V)
    cql = sb("cql", [P, 4, S], F32R, R_V + 4096)
    KVP = 3 * P
    ckh = sb("ckh", [P, 2, KVP], F32R, R_V + 8192)
    ckl = sb("ckl", [P, 2, KVP], F32R, R_V + 8192 + 3072)
    oall = sb("oall", [P, KC, S], F32, R_V)
    W1, W2_, W3 = R_T + 4352, R_T + 2 * 4352, R_T + 3 * 4352
    sbd = sb("sbd", [P, 2, KEYS], F32, W1)
    ond = sb("ond", [P, TOK, P], F32, W1 + 3328)
    wmix = sb("wmix", [P, KEYS], F32, W2_)
    wt = sb("wt", [P, 384], F32, W2_ + 1664)
    wts = sb("wts", [META, S], F32, W2_ + 3200)
    pm = [sb(f"pm{b}", [P, KEYS], F32, W3 + 1664 * b) for b in range(2)]
    onm = sb("onm", [P, TOK, P], F32, W3 + 3328)
    oh = sb("oh", [P, KC, S], F32R, R_V)
    ol = sb("ol", [P, KC, S], F32R, R_Z)
    yn = sb("yn", [P, TOK, D], F32, R_C)
    finalw = sb("finalw", [P, D], F32, R_C + 16384)
    x1r = sb("x1r", [P, TOK, D], F32, R_Y)

    ps = nc.alloc_psum_tensor("ps", [P, 8, 512], F32)

    def sm(name, a=0, n=None):
        lo, hi = SMALL[name]
        return small[:, lo + a:lo + a + (n or hi - lo - a)]

    def cn(name, a=0, n=None, p=P):
        lo, hi = CONST[name]
        return const[0:p, lo + a:lo + a + (n or hi - lo - a)]

    ident = sm("ident")

    def spread(ap, n):
        return ap.unsqueeze(2).to_broadcast([ap.shape[0], ap.shape[1], n])

    on = sb("on", [P, TOK, D], F32, R_Z)
    postw = sb("postw", [P, D], F32, R_X)
    xr = sb("xr", [P, TOK, D], F32, R_Y)

    sems = {}

    def sem(name):
        if name not in sems:
            sems[name] = ctx.enter_context(nc.semaphore(name))
        return sems[name]

    raw_in = [sem(f"raw_in{r}") for r in range(RING)]
    wh_done = sem("wh_done")
    split_done = sem("split_done")
    slots_done = sem("slots_done")
    s_tile = sem("first_tile_summed")
    psum_free = [sem("psum_free0"), sem("psum_free1")]

    def wait(eng, s, v):
        if not isinstance(v, int) or v > 0:
            eng.wait_ge(s, v)

    def group_numbers():
        at, outp = 0, {}
        for name, kinds, times in STAGES:
            outp[name] = at
            at += times * len(kinds)
        return outp

    FIRST_G = group_numbers()

    def pe_group(pe, n, frees, out_at, moving, tiles, tokens, ring=0, kcs=KC, cols=COLS, before=None,
                 chunk=lambda kc: kc, first_tile_early=False):
        hi, lo = moving
        steps = [(k, range(len(tiles)) if tiles else [0]) for k in range(kcs // SLOT_KC)]
        if first_tile_early:
            steps = steps[:-RING] + [(k, [m]) for m in range(len(tiles)) for k, _ in steps[-RING:]]
        for k, turn_of in steps:
            if turn_of[0] == 0:
                if before:
                    before(k)
                wait(pe, split_done, n + k + 1)
            r = (ring + k) % RING

            def free(c, at):
                if k == 0 and c == 0:
                    for s, v, o in frees:
                        if o == at:
                            wait(pe, s, v)

            for c in range(SLOT_KC):
                kc = k * SLOT_KC + c
                a, z = kc == 0, kc == kcs - 1
                kc = chunk(kc)
                if tiles:
                    for m in turn_of:
                        o, t = out_at(m), tiles[m]
                        free(c, m)
                        pe.matmul(o, hi[:, kc, t], wh[r][:, c, 0:cols], start=a, stop=False)
                        pe.matmul(o, hi[:, kc, t], wl[r][:, c, 0:cols], start=False, stop=False)
                        last = pe.matmul(o, lo[:, kc, t], wh[r][:, c, 0:cols], start=False, stop=z)
                else:
                    two = tokens.stop - tokens.start <= S
                    for j in range(cols // P):
                        f = slice(j * P, (j + 1) * P)
                        st = a and (j % 2 == 0 or not two)
                        free(c, j)
                        pe.matmul(out_at(j), wh[r][:, c, f], hi[:, kc, tokens], start=st, stop=False,
                                  skip_group_check=True)
                        pe.matmul(out_at(j), wh[r][:, c, f], lo[:, kc, tokens], start=False, stop=False,
                                  skip_group_check=True)
                        last = pe.matmul(out_at(j), wl[r][:, c, f], hi[:, kc, tokens], start=False, stop=z,
                                         skip_group_check=True)
            if not tiles or turn_of[-1] == len(tiles) - 1:
                last.then_inc(slots_done, 1)
            elif k == kcs // SLOT_KC - 1:
                last.then_inc(s_tile, 1)

    def half_bank(parity):
        return lambda j: ps[:, 2 * parity + j // 2, (j % 2) * S:(j % 2) * S + S]

    def whole_bank(first, width=COLS):
        return lambda m: ps[:, first + m, 0:width]

    def banks(parity):
        return ps[:, 2 * parity:2 * parity + 2, :].rearrange("p b (j s) -> p (b j) s", j=2)

    s_x, s_small, s_const, s_wg = [sem("x_in0"), sem("x_in1")], sem("small_in"), sem("const_in"), sem("wg_in")
    s_x_squares, s_x_mean, s_rstd, s_x_normed = sem("x_squares"), sem("x_mean"), sem("x_rstd"), sem("x_normed")
    s_x_turned, s_x_high, s_x_low = sem("x_turned"), sem("x_high"), sem("x_low")
    s_wgh, s_wgl, s_gate_sums = sem("gate_w_high"), sem("gate_w_low"), sem("gate_sums")
    s_gate_rows = sem("gate_rows")
    s_gate_log, s_gate_scanned, s_gate_bound = sem("gate_log"), sem("gate_scanned"), sem("gate_bound")
    s_gate_turned, s_gate_columns = sem("gate_turned"), sem("gate_columns")
    s_conv_first, s_conv, s_conv_sigmoid = sem("conv_first"), sem("conv_done"), sem("conv_sigmoid")
    s_qk = sem("qk_done")
    s_head_keys, s_head_scores, s_head_exponent = sem("head_keys"), sem("head_scores"), sem("head_exponent")
    s_head_decay, s_head_weights, s_head_sums = sem("head_decay"), sem("head_weights"), sem("head_sums")
    s_head_denominator, s_head_squares, s_head_mean = sem("head_denominator"), sem("head_squares"), sem("head_mean")
    s_head_rstd, s_head_normed, s_head_turned = sem("head_rstd"), sem("head_normed"), sem("head_turned")
    s_head_kept = sem("head_kept")
    s_z_sigmoid, s_y = sem("z_sigmoid"), sem("y_done")
    s_u_kept, s_pool, s_pool_mixed = sem("u_kept"), sem("pooled"), sem("pool_mixed")
    s_pool_w_in, s_zb_sigmoid, s_yb_done = sem("pool_w_in"), sem("zb_sigmoid"), sem("yb_done")
    s_ga, s_gb, s_merged = sem("ga_sigmoid"), sem("gb_sigmoid"), sem("merged")
    s_out_squares, s_post, s_x_again = sem("out_squares"), sem("post_w_in"), sem("x_again")
    s_out_mean, s_out_rstd, s_x1 = sem("out_mean"), sem("out_rstd"), sem("x1_done")
    s_out = sem("stored")
    s_meta, s_meta_squares, s_meta_mean = sem("meta_in"), sem("meta_squares"), sem("meta_mean")
    s_meta_rstd, s_meta_normed, s_meta_turned = sem("meta_rstd"), sem("meta_normed"), sem("meta_turned")
    s_meta_kept = sem("meta_kept")
    s_xkept, s_x1_squares, s_x1_mean = sem("x1_kept"), sem("x1_squares"), sem("x1_mean")
    s_x1_rstd, s_x1_normed, s_x2_turned = sem("x1_rstd"), sem("x1_normed"), sem("x2_turned")
    s_x2_high, s_x2_low = sem("x2_high"), sem("x2_low")
    s_cks, s_cksum, s_ckm = sem("ckv_squares"), sem("ckv_sums"), sem("ckv_mean")
    s_ckr, s_ckd, s_ckb = sem("ckv_rstd"), sem("ckv_diagonal"), sem("ckv_spread")
    s_krm, s_ckl, s_kpe = sem("kr_rotated"), sem("ckv_low"), sem("kpe_done")
    s_cqs, s_cqm, s_cqr = sem("cq_squares"), sem("cq_mean"), sem("cq_rstd")
    s_cqn, s_cqt, s_cql = sem("cq_normed"), sem("cq_turned"), sem("cq_low")
    s_avt, s_avm, s_avn = sem("av_kept"), sem("av_turned"), sem("av_done")
    s_qpr, s_qpm, s_qp = sem("qp_raw"), sem("qp_rotated"), sem("qp_done")
    s_l1, s_l2, s_lam = sem("lambda_sums"), sem("lambda_exp"), sem("lambda_done")
    s_gsum, s_gs, s_gate = sem("gate_summed"), sem("gate_sigmoid"), sem("gate_done")
    pair = {name: sem("pair_" + name) for name in (
        "queries", "scores_d", "scores_m", "max_d", "exp_d", "mix", "max_m", "exp_m", "turned_d", "kept_d",
        "sums_d", "squares", "mean", "rstd", "scale", "normed_d", "back_d", "out_d", "turned_m", "kept_m",
        "sums_m", "inverse_m", "normed_m", "back_m", "out_m")}
    s_out_gated, s_out_high, s_out_low, s_final_w_in, s_x1_back, s_y_summed, s_y_squares, s_y_mean, s_y_rstd, s_y_scaled = (
        sem("out_gated"), sem("out_high"), sem("out_low"), sem("final_w_in"), sem("x1_back"), sem("y_summed"),
        sem("y_squares"), sem("y_mean"), sem("y_rstd"), sem("y_scaled"))
    s_one, s_pad = sem("vn_ones"), sem("pad_zeroed")

    block = ctx.enter_context(nc.Block())

    @block.sync
    def _(sp):
        sp.dma_start(xn[:, 0, :], x[0:P, :]).then_inc(s_x[0], 16)
        sp.dma_start(small[:, :], small_in).then_inc(s_small, 16)
        sp.dma_start(xn[:, 1, :], x[P:S, :]).then_inc(s_x[1], 16)
        for n in range(RING):
            sp.dma_start(raw[n][:, :, :], w_stream[n]).then_inc(raw_in[n], 16)
        sp.dma_start(wg[:, :, :], w_gates).then_inc(s_wg, 16)
        sp.dma_start(const[:, :], const_in).then_inc(s_const, 16)
        with sp.Fori(1, SLOTS // RING) as i:
            for r in range(RING):
                sp.wait_ge(split_done, i * RING + (r - RING + 1))
                sp.dma_start(raw[r][:, :, :], w_stream[bass.ds(i * RING + r, 1), :, :, :].rearrange(
                    "o p c n -> p (o c) n")).then_inc(raw_in[r], 16)
        for n in range(SLOTS - SLOTS % RING, SLOTS):
            sp.wait_ge(split_done, n - RING + 1)
            sp.dma_start(raw[n % RING][:, :, :], w_stream[n]).then_inc(raw_in[n % RING], 16)

        for c in range(4):
            m, q = c // 2, c % 2
            sp.wait_ge(s_y_scaled, c + 1)
            sp.dma_start(out[m * P:(m + 1) * P, q * 1024:(q + 1) * 1024], yn[:, m, q * 1024:(q + 1) * 1024]).then_inc(
                s_out, 16)
        sp.wait_ge(s_xkept, 16)
        sp.wait_ge(s_out, 4 * 16)

    @block.tensor
    def _(pe):
        def turn(o, i, n=P):
            return pe.transpose(o, i, ident[0:n, 0:n])

        def by_feature(rows_, made, s, parts):
            for m, b in parts:
                pe.wait_ge(made, m + 1)
                for c in range(4 * b, 4 * b + 4):
                    last = pe.matmul(ps[:, c // 2, (c % 2) * S + m * P:(c % 2) * S + (m + 1) * P],
                                     rows_[:, m, c * P:(c + 1) * P], diag[:, m, :], start=True, stop=True)
                if m == TOK - 1:
                    last.then_inc(s, 1)

        last_block = [(m, 3) for m in range(TOK)]
        by_feature(xn, s_x_normed, s_x_turned, [(m, b) for m in range(TOK) for b in range(3)])

        def groups(name, i, moving, token_kinds=(), before=None):
            kinds = dict((a, b) for a, b, _ in STAGES)[name]
            per = sum(map(slots_of, kinds))
            off = 0
            in_loop = not isinstance(i, int)
            for j, kind in enumerate(kinds):
                by_token = kind in token_kinds
                pe_group(pe, FIRST[name] + i * per + off,
                         [(psum_free[j % 2], FIRST_G[name] // 2 + i * (len(kinds) // 2) + j // 2, 0)],
                         whole_bank(2 * (j % 2)) if by_token else half_bank(j % 2), moving[kind],
                         [slice(m * P, (m + 1) * P) for m in range(TOK)] if by_token else None, slice(0, S),
                         kcs=slots_of(kind) * SLOT_KC,
                         first_tile_early=name == "WO" and not in_loop and (i, j) == (1, 1),
                         before=before and (lambda k, j=j, kind=kind: before(j, kind, k)))
                off += slots_of(kind)

        X, Y, Z = (xh, xl), (yh, yl), (zh, zl)

        def x_there(j, kind, k):
            if j == 0 and k == 1:
                by_feature(xn, s_x_normed, s_x_turned, last_block)
            pe.wait_ge(s_x_low, (k * SLOT_KC + SLOT_KC - 1) // 4 + 1)

        groups("QK", 0, {"qk": X}, before=x_there)
        with pe.Fori(1, 4) as i:
            groups("QK", i, {"qk": X})

        pe.wait_ge(s_wgl, 1)
        for kc in range(KC):
            o = ps[0:GATE_W, 4, 0:S]
            pe.matmul(o, wgh[:, kc, :], xh[:, kc, :], start=kc == 0, stop=False)
            pe.matmul(o, wgl[:, kc, :], xh[:, kc, :], start=False, stop=False)
            last = pe.matmul(o, wgh[:, kc, :], xl[:, kc, :], start=False, stop=kc == KC - 1)
        last.then_inc(s_gate_sums, 1)

        groups("V", 0, {"v": X}, token_kinds=("v",))
        groups("V", 1, {"v": X}, token_kinds=("v",))
        pe.wait_ge(s_gate_bound, 1)
        for w, row in enumerate((4, 2)):
            for m in range(TOK):
                last = turn(ps[:, 6, 16 * w + 8 * m:16 * w + 8 * m + 8], rows[:, row, m * P:(m + 1) * P], H)
        last.then_inc(s_gate_turned, 1)

        def head(i, j, k):
            h = i * 2 + j
            if k == 0:
                pe.wait_ge(s_head_keys, h * 2 + 2)
                pe.wait_ge(s_head_kept, h + 1)
                pe.matmul(ps[:, 4, 0:S], cn("ones", p=H), mrow[:, :], start=True, stop=True)
                for st in range(TOK):
                    w = S - st * P
                    for dt in range(2):
                        last = pe.matmul(ps[:, 5, st * S:st * S + w], kst[:, dt, st * P:(st + 1) * P],
                                         qk[:, bass.ds(h * 2 + dt, 1), st * P:S].rearrange("p o s -> p (o s)"),
                                         start=dt == 0, stop=dt == 1)
                last.then_inc(s_head_scores, 1)
            if k == 3:
                pe.wait_ge(s_head_weights, h + 1)
                for t, st in ((0, 0), (1, 0), (1, 1)):
                    lhs = pt[:, t * P:(t + 1) * P] if st == 0 else pt[:, S:S + P]
                    last = pe.matmul(ps[:, 6 + t, 0:VW], lhs, vn[:, st, bass.ds(h * VW, VW)],
                                     start=st == 0, stop=st == t)
                last.then_inc(s_head_sums, 1)
            if k == 7:
                pe.wait_ge(s_head_normed, h + 1)
                for dt in range(2):
                    for m in range(TOK):
                        last = turn(ps[:, 4, dt * S + m * P:dt * S + (m + 1) * P], hn[:, m, dt * P:(dt + 1) * P])
                last.then_inc(s_head_turned, 1)

        pe.wait_ge(s_one, 1)
        pe.wait_ge(s_const, 16)
        with pe.Fori(0, 4) as i:
            groups("OZ", i, {"o": X, "z": X}, before=lambda j, kind, k: head(i, j, k))

        def mix(i, j, k):
            if j == 1 and k == 6:
                pe.wait_ge(s_pool, i + 1)
                pe.wait_ge(s_pool_w_in, 16)
                wait(pe, s_yb_done, i)
                for jj in range(4):
                    for cc in range(2):
                        g = jj // 2
                        last = pe.matmul(ps[:, 4 + g, (jj % 2) * S:(jj % 2) * S + S],
                                         poolw[:, (2 * i + g) * 2 + cc, (jj % 2) * P:(jj % 2) * P + P],
                                         pooled[:, 2 * g + cc, :], start=cc == 0, stop=cc == 1)
                last.then_inc(s_pool_mixed, 1)

        for i in range(2):
            groups("UZ", i, {"u": X, "zb": X}, before=lambda j, kind, k: mix(i, j, k))

        def projected(j, kind, k):
            if kind == "pa" and k == 0:
                pe.wait_ge(s_y, 4)
            if kind == "pb" and k == 0:
                pe.wait_ge(s_yb_done, 2)

        with pe.Fori(0, 4) as i:
            groups("MG", i, {"ga": X, "pa": Y, "gb": X, "pb": Z}, before=projected)

        def merged_there(i, j, k):
            pe.wait_ge(s_merged, (k * SLOT_KC + SLOT_KC - 1) // 4 + 1)
            if i == 1 and j == 0 and k == 2:
                pe.wait_ge(s_meta_normed, 1)
                for c in range(KC):
                    last = turn(ps[:, 6, c * META:(c + 1) * META], metan[:, c * P:(c + 1) * P], META)
                last.then_inc(s_meta_turned, 1)

        for i in range(2):
            groups("WO", i, {"wo": (mh, ml)}, token_kinds=("wo",),
                   before=lambda j, kind, k: merged_there(i, j, k))

        uses = [FIRST_G["CKQ"] // 2, FIRST_G["CKQ"] // 2]
        X2 = (x2h, x2l)
        xtok = [slice(META, META + P), slice(META + P, L2)]
        pe.wait_ge(psum_free[0], uses[0])
        pe.wait_ge(s_meta_kept, 1)
        by_feature(xr, s_x1_normed, s_x2_turned, [(0, 0)])
        pe.wait_ge(psum_free[1], uses[1])
        by_feature(xr, s_x1_normed, s_x2_turned, [(m, b) for b in range(3) for m in range(TOK)][1:])

        def x2_there(k):
            if k == 1:
                by_feature(xr, s_x1_normed, s_x2_turned, last_block)
            pe.wait_ge(s_x2_low, (k * SLOT_KC + SLOT_KC - 1) // 4 + 1)

        def both():
            return [(psum_free[0], uses[0], 0), (psum_free[1], uses[1], 2)]

        def used(*parities):
            for parity in parities:
                uses[parity] += 1

        n = FIRST["CKQ"]
        pe_group(pe, n, [(psum_free[0], uses[0], 0)], whole_bank(0), X2, xtok, None, before=x2_there)
        used(0)
        pe_group(pe, n + GROUP, [(psum_free[1], uses[1], 0)], whole_bank(2, L2), X2, None, slice(0, L2), cols=384)
        used(1)

        def second(stage, j, k):
            if stage == "AK" and j == 0 and k == 2:
                pe.wait_ge(s_cks, 1)
                for m, t in enumerate((0, P, L2 - P)):
                    for c in range(2):
                        last = pe.matmul(ps[:, 5, m:m + 1], sqk[:, c, t:t + P], cn("ones", 0, 1), start=c == 0,
                                         stop=c == 1)
                last.then_inc(s_cksum, 1)
            if stage == "AK" and j == 0 and k == 7:
                pe.wait_ge(s_ckd, 1)
                pe.matmul(ps[:, 6, 0:L2], cn("ones"), diagk[:, :], start=True, stop=True).then_inc(s_ckb, 1)
            if stage == "AV" and j == 0 and k == 2:
                pe.wait_ge(s_ckl, 1)
                pe.matmul(ps[:, 7, 0:L2], cn("rot"), ckvf[:, 2, :], start=True, stop=True).then_inc(s_krm, 1)
                pe.wait_ge(s_cqn, 1)
                for c in range(4):
                    for m in range(TOK):
                        last = turn(ps[:, 5 + c // 2, (c % 2) * S + m * P:(c % 2) * S + (m + 1) * P],
                                    cqn[:, m, c * P:(c + 1) * P])
                last.then_inc(s_cqt, 1)
            if stage == "AQ" and k == 3:
                pe.wait_ge(s_avt, j + 1)
                pe.wait_ge(s_cql, 1)
                pe.wait_ge(s_kpe, 1)
                wait(pe, s_avn, j)
                for kt in range(3):
                    w = min(P, L2 - kt * P)
                    for h in range(4):
                        last = turn(ps[0:w, 4 + kt, h * P:(h + 1) * P], avt[:, 4 * j + h, kt * P:kt * P + w])
                last.then_inc(s_avm, 1)

        for stage in ("AK", "AV"):
            for j in range(2):
                pe_group(pe, FIRST[stage] + j * GROUP, both(), whole_bank(0, L2), X2, None, slice(0, L2),
                         before=lambda k: second(stage, j, k))
                used(0, 1)
        for j in range(2):
            pe_group(pe, FIRST["AQ"] + j * GROUP, [(psum_free[j], uses[j], 0)], half_bank(j), X2, None,
                     slice(META, L2), before=lambda k: second("AQ", j, k))
            used(j)
        n = FIRST["UQ"]
        for j in range(3):
            pe_group(pe, n, [(psum_free[j % 2], uses[j % 2], 0)], half_bank(j % 2), (cqh, cql), None, slice(0, S),
                     kcs=4, ring=n % RING)
            used(j % 2)
            n += 2
        n = FIRST["UKV"]
        for j in range(2):
            pe_group(pe, n, both(), whole_bank(0, L2), (ckh, ckl), None, slice(0, L2), kcs=2, ring=n % RING)
            used(0, 1)
            n += 1
            if j == 0:
                pe.wait_ge(s_qpr, 1)
                pe.wait_ge(s_avn, 2)
                for t in range(4):
                    last = pe.matmul(ps[:, 4 + t // 2, (t % 2) * S:(t % 2) * S + S], cn("rot"), work[1][:, t, :],
                                     start=True, stop=True)
                last.then_inc(s_qpm, 1)
        for j in range(2):
            pe_group(pe, n, both(), whole_bank(0), (ckh, ckl), [slice(t * P, (t + 1) * P) for t in range(3)], None,
                     kcs=2, ring=n % RING)
            used(0, 1)
            n += 1

        def scores(p, odd):
            pe.wait_ge(pair["queries"], p * 4 + 4)
            for c in range(2):
                for t, (lo, w) in enumerate(((0, K0), (K0, L2))):
                    last = pe.matmul(ps[:, 2 + c, lo:lo + w], qhalf[c][:, t * P:(t + 1) * P],
                                     ak[:, bass.ds(p, 1), 0:w].rearrange("p o s -> p (o s)"), start=True, stop=True)
            last.then_inc(pair["scores_d"], 1)
            r = slice(64 * odd, 64 * odd + 64)
            for t, (lo, w) in enumerate(((0, K0), (K0, L2))):
                pe.matmul(ps[:, 4, lo:lo + w], qst[1][:, t * P:(t + 1) * P],
                          kn[:, bass.ds(p, 1), 0:w].rearrange("p o s -> p (o s)"), start=True, stop=False)
                last = pe.matmul(ps[:, 4, lo:lo + w], qst[2][r, t * P:(t + 1) * P], kpe[r, 0:w],
                                 start=False, stop=True)
            last.then_inc(pair["scores_m"], 1)

        def turned(w, s):
            for at, lo in ((0, 0), (P, K0), (2 * P, K0 + P)):
                turn(ps[:, 5, at:at + P], w[:, lo:lo + P])
            for at, lo in ((0, P), (P, K0 + 2 * P)):
                last = turn(ps[0:META, 6, at:at + P], w[:, lo:lo + META])
            last.then_inc(s, 1)

        def weighted(bank, v, h, s):
            hc = bass.ds(h * P, P)
            pe.matmul(ps[:, bank, 0:P], wt[:, 0:P], v[:, 0, hc], start=True, stop=False)
            pe.matmul(ps[:, bank, 0:P], wts[:, 0:P], v[0:META, 1, hc], start=False, stop=True)
            pe.matmul(ps[:, bank, P:2 * P], wt[:, P:2 * P], v[:, 0, hc], start=True, stop=False)
            pe.matmul(ps[:, bank, P:2 * P], wt[:, 2 * P:3 * P], v[:, 1, hc], start=False, stop=False)
            pe.matmul(ps[:, bank, P:2 * P], wts[:, P:2 * P], v[0:META, 2, hc], start=False, stop=True).then_inc(s, 1)

        def back(bank, o, s):
            for m in range(TOK):
                last = turn(ps[:, bank, m * P:(m + 1) * P], o[:, m, :])
            last.then_inc(s, 1)

        def quarter(p, k, odd):
            first = p if isinstance(p, int) else 2
            here = not isinstance(p, int) or p < H
            if k == 0:
                if first >= 1:
                    pe.wait_ge(pair["kept_m"], p)
                    weighted(6, vbn, p - 1, pair["sums_m"])
                if here:
                    if first < 1:
                        pe.wait_ge(s_qp, 1)
                    else:
                        pe.wait_ge(pair["max_m"], p)
                    scores(p, odd)
            if k == 1 and first >= 1:
                pe.wait_ge(pair["normed_m"], p)
                back(6, onm, pair["back_m"])
                pe.wait_ge(pair["normed_d"], p)
                back(7, ond, pair["back_d"])
            if k == 2 and here:
                pe.wait_ge(pair["mix"], p + 1)
                if first >= 1:
                    pe.wait_ge(pair["out_m"], p)
                turned(wmix, pair["turned_d"])
            if k == 3 and here:
                pe.wait_ge(pair["kept_d"], p + 1)
                if first >= 1:
                    pe.wait_ge(pair["out_d"], p)
                weighted(7, avn, p, pair["sums_d"])
                pe.wait_ge(pair["exp_m"], p + 1)
                turned(pm[odd], pair["turned_m"])

        def gate_group(q):
            pe_group(pe, FIRST["G"] + q * GROUP, [(s_gsum, q, 0)] if not isinstance(q, int) or q else [],
                     half_bank(0), X2, None, slice(META, L2), ring=FIRST["G"] % RING,
                     before=lambda k: quarter(q * 2 + k // 4, k % 4, k // 4))

        pe.wait_ge(psum_free[0], uses[0])
        pe.wait_ge(psum_free[1], uses[1])
        gate_group(0)
        with pe.Fori(1, 3) as q:
            gate_group(q)
        gate_group(3)

        for j in range(4):
            def out_there(k):
                if j == 0:
                    if k < 2:
                        quarter(H, k, 0)
                    pe.wait_ge(s_out_low, k // 2 + 1)
            left = (pair["max_m"], H), (s_gsum, 4), (s_y_summed, 2), (s_y_summed, 4)
            pe_group(pe, FIRST["W2"] + j * GROUP, [(*left[j], 0)],
                     whole_bank(2 * (1 - j % 2)), (oh, ol), [slice(0, P), slice(P, S)], None,
                     ring=FIRST["W2"] % RING, before=out_there, first_tile_early=j == 3,
                     chunk=lambda kc: OUT_ORDER[kc // 4] * 4 + kc % 4)

    def run(eng, split, evac, attend, attend_late, breaks):
        prev = None
        for at, (name, kinds, times) in enumerate(STAGES):
            if name in breaks:
                breaks[name]()
                prev = None
            end = FIRST[STAGES[at + 1][0]] if at + 1 < len(STAGES) and STAGES[at + 1][0] in breaks else SLOTS
            per = sum(map(slots_of, kinds))
            n0 = FIRST[name]

            def body(i, prev):
                off = 0
                for j, kind in enumerate(kinds):
                    here = n0 + i * per + off
                    for k in range(slots_of(kind)):
                        late = prev and prev[0] == "g" and (k > 0 or kind == "w2")
                        if prev and k == 0 and not late:
                            evac(prev[0], k, prev[1], prev[2], here)
                        attend(kind, k, i, j)
                        if prev and k > 0 and not late:
                            evac(prev[0], k, prev[1], prev[2], here)
                        if not isinstance(i, int) or here + k + LEAD < end:
                            split(here + k + LEAD, (n0 + off + k + LEAD) % RING)
                        if late:
                            evac(prev[0], k, prev[1], prev[2], here)
                        attend_late(kind, k, i, j)
                    prev = (kind, i, j)
                    off += slots_of(kind)
                return prev

            prev = body(0, prev)
            if times > 2:
                last = times - (name == "G")
                with eng.Fori(1, last) as i:
                    body(i, (kinds[-1], i - 1, len(kinds) - 1))
                if last < times:
                    body(last, (kinds[-1], last - 1, len(kinds) - 1))
            elif times == 2:
                body(1, prev)
            prev = (kinds[-1], times - 1, len(kinds) - 1)

    @block.scalar
    def _(act):
        def drain():
            act.drain()

        def split(n, r):
            act.wait_ge(raw_in[r], 16 * slot_turn(n, r) + 16)
            wait(act, slots_done, n - RING + 1)
            act.activation(wh[r][:, :, :], raw[r][:, :, :], ACT.Copy).then_inc(wh_done, 1)

        act.sem_inc(s_head_kept, 1)
        for m in range(TOK):
            act.wait_ge(s_x[m], 16)
            act.activation(xsq[:, m, :], xn[:, m, :], ACT.Square, accum_out=stat[:, m:m + 1]).then_inc(s_x_squares, 1)
        split(0, 0)

        def high_parts(hi, b, name, s):
            for j in range(4):
                c = 4 * b + j
                last = act.activation(hi[:, c, :], ps[:, c // 2, (c % 2) * S:(c % 2) * S + S], ACT.Copy,
                                      scale=sm(name, c, 1))
            last.then_inc(s, 1)

        for b in range(4):
            act.wait_ge(s_x_turned, b + 1)
            high_parts(xh, b, "norm_pre", s_x_high)
            if b + 1 < LEAD:
                split(b + 1, b + 1)

        def out_squares(q, m):
            act.activation(ps[:, 4 + m, :], ps[:, 2 * (q % 2) + m, :], ACT.Square,
                           accum_out=stat[:, 12 + 4 * m + q:13 + 4 * m + q])
            act.drain()

        def y_squares(q, m):
            act.wait_ge(s_y_summed, 2 * q + m + 1)
            act.activation(sqs[:, :], yn[:, m, q * COLS:(q + 1) * COLS], ACT.Square,
                           accum_out=stat[:, 12 + 4 * m + q:13 + 4 * m + q])
            act.drain().then_inc(s_y_squares, 1)

        def evac(kind, k, i, j, done):
            if kind == "qk":
                q = i * 2 + j
                if k == 0:
                    act.wait_ge(slots_done, done)
                    wait(act, s_qk, q)
                    for jj in range(4):
                        last = act.activation(
                            work[0][:, jj, :], banks(j)[:, jj, :], ACT.Identity,
                            bias=small[:, bass.ds(SMALL["conv_b"][0] + q * 4 + jj, 1)],
                            scale=small[:, bass.ds(SMALL["conv_w"][0] + q * 16 + 4 * jj + 3, 1)])
                    last.then_inc(s_conv_first, 1)
                if k == 3:
                    act.wait_ge(s_conv, q + 1)
                    act.activation(work[1][:, :, :], work[0][:, :, :], ACT.Sigmoid).then_inc(s_conv_sigmoid, 1)
            if kind == "v" and k == 0:
                act.wait_ge(slots_done, done)
                q = i * 2 + j
                for m in range(TOK):
                    last = act.activation(
                        vn[:, m, 2 * q * VW:2 * (q + 1) * VW].rearrange("p (h d) -> p h d", h=2)[:, :, 0:HD],
                        ps[:, 2 * j + m, :].rearrange("p (h d) -> p h d", h=2), ACT.Copy)
                last.then_inc(psum_free[j], 1)
            if kind == "o" and k == 0:
                act.wait_ge(slots_done, done)
                wait(act, s_y, i)
                if isinstance(i, int):
                    act.wait_ge(s_qk, 8)
                act.activation(work[0][:, :, :], banks(0), ACT.Sigmoid).then_inc(psum_free[0], 1)
            if kind == "z" and k == 0:
                act.wait_ge(slots_done, done)
                act.activation(work[1][:, :, :], banks(1), ACT.Sigmoid).then_inc(s_z_sigmoid, 1)
            if kind == "u" and k == 0:
                act.wait_ge(slots_done, done)
                wait(act, s_pool, i)
                act.wait_ge(s_pad, 1)
                act.activation(upad[:, :, META:META + S], banks(0), ACT.Copy).then_inc(s_u_kept, 1)
                act.drain().then_inc(psum_free[0], 1)
            if kind == "zb" and k == 0:
                act.wait_ge(slots_done, done)
                act.wait_ge(s_y, 4)
                wait(act, s_yb_done, i)
                act.activation(work[1][:, :, :], banks(1), ACT.Sigmoid).then_inc(s_zb_sigmoid, 1)
            if kind == "ga" and k == 0:
                act.wait_ge(slots_done, done)
                wait(act, s_merged, i)
                if isinstance(i, int):
                    act.wait_ge(s_yb_done, 2)
                act.activation(work[0][:, :, :], banks(0), ACT.Sigmoid).then_inc(s_ga, 1)
                act.drain().then_inc(psum_free[0], 1)
            if kind == "gb" and k == 0:
                act.wait_ge(slots_done, done)
                act.activation(work[1][:, :, :], banks(0), ACT.Sigmoid).then_inc(s_gb, 1)
                act.drain().then_inc(psum_free[0], 1)
            if kind == "wo" and k == 0:
                act.wait_ge(slots_done, done)
                act.wait_ge(s_merged, 4)
                for m in range(TOK):
                    out_squares(i * 2 + j, m)
                act.drain().then_inc(s_out_squares, 1)

            if kind == "ckv" and k == 0:
                act.wait_ge(slots_done, done)
                act.activation(ckvf[:, :, :], ps[:, 2:5, 0:L2], ACT.Copy)
                act.drain().then_inc(psum_free[1], 1)
                act.activation(sqk[:, :, :], ckvf[:, 0:2, :], ACT.Square).then_inc(s_cks, 1)
            if kind == "cq" and k == 0:
                act.wait_ge(slots_done, done)
                act.activation(cqn[:, :, :], ps[:, 0:2, :], ACT.Copy)
                act.drain().then_inc(psum_free[0], 1)
                for m in range(TOK):
                    act.activation(sqs[:, :], cqn[:, m, :], ACT.Square, accum_out=stat[:, 36 + m:37 + m])
                    drain()
                act.drain().then_inc(s_cqs, 1)
            if kind in ("ak", "av", "uk") and k == 0:
                act.wait_ge(slots_done, done)
                to = {"ak": ak, "av": avt, "uk": kn}[kind]
                for b in range(2):
                    act.activation(to[:, 4 * j + 2 * b:4 * j + 2 * b + 2, :], ps[:, 2 * b:2 * b + 2, 0:L2], ACT.Copy)
                    act.drain().then_inc(psum_free[b], 1)
                if kind == "av":
                    act.sem_inc(s_avt, 1)
            if kind in ("aq", "uq") and k == 0:
                act.wait_ge(slots_done, done)
                to = aq if kind == "aq" else qn
                act.activation(to[:, 4 * j:4 * j + 4, :], banks(j), ACT.Copy).then_inc(psum_free[j], 1)
            if kind == "ur" and k == 0:
                act.wait_ge(slots_done, done)
                act.activation(work[1][:, :, :], banks(0), ACT.Copy)
                act.drain().then_inc(psum_free[0], 1)
                act.sem_inc(s_qpr, 1)
            if kind == "uv" and k == 0:
                act.wait_ge(slots_done, done)
                c = slice((j - 2) * COLS, (j - 1) * COLS)
                act.activation(vbn[:, 0:2, c], ps[:, 0:2, :], ACT.Copy)
                act.drain().then_inc(psum_free[0], 1)
                act.activation(vbn[0:META, 2, c], ps[0:META, 2, :], ACT.Copy)
                act.drain().then_inc(psum_free[1], 1)
            if kind == "g" and k == (1 if isinstance(i, int) and i == 3 else 3):
                act.wait_ge(s_gsum, i + 1)
                wait(act, s_gate, i)
                act.activation(work[0][:, :, :], gates[:, bass.ds(i * 4, 4), :], ACT.Sigmoid).then_inc(s_gs, 1)
            if kind == "w2" and k == 1:
                for m in range(TOK):
                    y_squares(i * 2 + j, m)

        def exps(parts, p, s):
            for x_, bias, total, scale in parts:
                act.activation(x_, x_, ACT.Exp, bias=bias, scale=scale, accum_out=total)
            act.drain().then_inc(s, 1)

        def quarter(p, k, odd, late):
            first = p if isinstance(p, int) else 2
            here = not isinstance(p, int) or p < H
            b, b1 = 64 + 40 * odd, 64 + 40 * (1 - odd)

            def keep(s, t):
                act.wait_ge(t, p + 1)
                act.activation(wt[:, :], ps[:, 5, 0:384], ACT.Copy)
                act.activation(wts[:, :], ps[0:META, 6, 0:S], ACT.Copy)
                act.drain().then_inc(s, 1)

            if k == 0:
                if first >= 1 and not late:
                    act.wait_ge(pair["scale"], p)
                    for m in range(TOK):
                        act.activation(ond[:, m, :], ps[:, 7, m * P:(m + 1) * P], ACT.Copy,
                                       scale=stat[:, b1 + 24 + m:b1 + 25 + m])
                    act.drain().then_inc(pair["normed_d"], 1)
                    act.wait_ge(pair["sums_m"], p)
                    act.wait_ge(pair["inverse_m"], p)
                    for m in range(TOK):
                        act.activation(onm[:, m, :], ps[:, 6, m * P:(m + 1) * P], ACT.Copy,
                                       scale=stat[:, b1 + 32 + m:b1 + 33 + m])
                    act.drain().then_inc(pair["normed_m"], 1)
                if here and late:
                    act.wait_ge(pair["max_d"], p + 1)
                    exps([(sbd[:, c, lo:lo + w], stat[:, b + 4 + 2 * t + c:b + 5 + 2 * t + c],
                           stat[:, b + 8 + 2 * t + c:b + 9 + 2 * t + c], 0.125)
                          for t, (lo, w) in enumerate(((0, K0), (K0, L2))) for c in range(2)], p, pair["exp_d"])
            if k == 2 and here and late:
                act.wait_ge(pair["max_m"], p + 1)
                exps([(pm[odd][:, lo:lo + w], stat[:, b + 28 + t:b + 29 + t], stat[:, b + 30 + t:b + 31 + t],
                       MLA_SCALE) for t, (lo, w) in enumerate(((0, K0), (K0, L2)))], p, pair["exp_m"])
            if k == 2 and here and not late:
                if first >= 1:
                    act.wait_ge(pair["sums_m"], p)
                keep(pair["kept_d"], pair["turned_d"])
            if k == 3 and here and not late:
                act.wait_ge(pair["sums_d"], p + 1)
                if first >= 1:
                    act.wait_ge(pair["back_d"], p)
                for m in range(TOK):
                    act.activation(ond[:, m, :], ps[:, 7, m * P:(m + 1) * P], ACT.Square,
                                   scale=stat[:, b + 12 + 2 * m:b + 13 + 2 * m],
                                   accum_out=stat[:, b + 18 + m:b + 19 + m])
                act.drain().then_inc(pair["squares"], 1)
                keep(pair["kept_m"], pair["turned_m"])

        def attend(kind, k, i, j):
            if kind == "wo" and i == 0 and j == 0 and k == 4:
                act.wait_ge(s_meta, 16)
                act.wait_ge(s_merged, 4)
                act.activation(metasq[:, :], metan[:, :], ACT.Square, accum_out=stat[0:META, 24:25])
                act.drain().then_inc(s_meta_squares, 1)
            if kind == "ak" and j == 0 and k == 3:
                act.wait_ge(s_l1, 1)
                act.activation(stat[:, 40:42], stat[:, 40:42], ACT.Exp).then_inc(s_l2, 1)
            if kind == "g":
                quarter(i * 2 + k // 4, k % 4, k // 4, False)
            if kind == "w2" and i == 0 and j == 0 and k < 2:
                quarter(H, k, 0, False)
            if kind == "qk" and isinstance(i, int) and j == 0 and k == 4:
                act.wait_ge(s_wg, 16)
                act.activation(wgh[:, :, :], wg[:, :, :], ACT.Copy).then_inc(s_wgh, 1)
            if kind == "v" and i == 1 and j == 0 and k == 2:
                act.wait_ge(s_gate_rows, 1)
                act.activation(rows[:, 0, :], rows[:, 0, :], ACT.Identity, bias=sm("ibias")[0:H, :])
                act.activation(rows[:, 1, :], rows[:, 5, :], ACT.Abs, bias=sm("fbias")[0:H, :])
                drain()
                act.activation(rows[:, 1, :], rows[:, 1, :], ACT.Exp, scale=-1.0)
                drain()
                act.activation(rows[:, 1, :], rows[:, 1, :], ACT.Ln, bias=1.0).then_inc(s_gate_log, 1)
            if kind == "v" and i == 1 and j == 0 and k == 5:
                act.wait_ge(s_gate_scanned, 1)
                act.activation(rows[:, 2, :], rows[:, 2, :], ACT.Exp, scale=-1.0).then_inc(s_gate_bound, 1)
            if kind in ("o", "z"):
                h = i * 2 + j
                if k == 1:
                    act.wait_ge(s_head_exponent, h + 1)
                    act.activation(dmat[:, :], darg[:, :], ACT.Exp).then_inc(s_head_decay, 1)
                if k == 4:
                    act.wait_ge(s_head_denominator, h + 1)
                    for m in range(TOK):
                        last = act.activation(ps[:, 5, m * S:m * S + S], ps[:, 6 + m, 0:HD], ACT.Square,
                                              scale=stat[:, 2 + m:3 + m], accum_out=stat[:, 4 + m:5 + m])
                    act.drain().then_inc(s_head_squares, 1)
                if k == 7:
                    act.wait_ge(s_head_turned, h + 1)
                    wait(act, s_y, i)
                    act.activation(work[3][:, 2 * j:2 * j + 2, :],
                                   ps[:, 4, :].rearrange("p (a s) -> p a s", a=2), ACT.Copy).then_inc(s_head_kept, 1)

        def between():
            def x1_squares(c):
                m, q = c // 2, slice(c % 2 * 1024, c % 2 * 1024 + 1024)
                act.wait_ge(s_x1, c + 1)
                act.activation(work[0][:, :, :].rearrange("p a s -> p (a s)"), xr[:, m, q], ACT.Square,
                               scale=D ** -0.5, accum_out=stat[:, 44 + c:45 + c])
                act.drain().then_inc(s_x1_squares, 1)

            n = FIRST["CKQ"]
            act.wait_ge(s_tile, 1)
            out_squares(3, 0)
            act.drain().then_inc(s_out_squares, 1)
            x1_squares(0)
            x1_squares(1)
            act.wait_ge(slots_done, n)
            out_squares(3, 1)
            act.drain().then_inc(s_out_squares, 1)
            split(n, n % RING)
            split(n + 1, (n + 1) % RING)
            x1_squares(2)
            x1_squares(3)
            split(n + 2, (n + 2) % RING)
            for b in range(4):
                act.wait_ge(s_x2_turned, b + 1)
                high_parts(x2h[:, :, META:L2], b, "attn_norm", s_x2_high)

        def attend_late(kind, k, i, j):
            if kind == "g":
                quarter(i * 2 + k // 4, k % 4, k // 4, True)
            if kind == "w2" and i == 0 and j == 0 and k < 2:
                quarter(H, k, 0, True)
            if kind == "g" and isinstance(i, int) and i == 3 or kind == "w2" and i == 0 and j == 0:
                for turn, b in enumerate(OUT_ORDER):
                    if (kind, k) == HIGH_AT[turn]:
                        act.wait_ge(s_out_gated, turn + 1)
                        act.activation(oh[:, 4 * b:4 * b + 4, :], gates[:, 4 * b:4 * b + 4, :], ACT.Copy).then_inc(
                            s_out_high, 1)

        run(act, split, evac, attend, attend_late, {"CKQ": between})
        for m in range(TOK):
            y_squares(3, m)

    @block.vector
    def _(dve):
        tt, ts, stt = dve.tensor_tensor, dve.tensor_scalar, dve.scalar_tensor_tensor

        def drain():
            dve.drain()

        def split(n, r):
            dve.wait_ge(wh_done, n + 1)
            tt(wl[r][:, :, :], raw[r][:, :, :], wh[r][:, :, :].bitcast(F32), ALU.subtract).then_inc(split_done, 1)

        for m in range(TOK):
            dve.wait_ge(s_x_squares, m + 1)
            ts(stat[:, m:m + 1], stat[:, m:m + 1], 1.0 / D, EPS, ALU.mult, ALU.add).then_inc(s_x_mean, 1)
            dve.wait_ge(s_rstd, m + 1)
            ts(diag[:, m, :], ident, stat[:, 2 + m:3 + m], None, ALU.mult).then_inc(s_x_normed, 1)
        split(0, 0)

        def low_parts(lo, hi, b, name, s):
            for j in range(4):
                c = 4 * b + j
                last = stt(out=lo[:, c, :], in0=ps[:, c // 2, (c % 2) * S:(c % 2) * S + S], scalar=sm(name, c, 1),
                           in1=hi[:, c, :].bitcast(F32), op0=ALU.mult, op1=ALU.subtract)
            last.then_inc(s, 1)

        for b in range(4):
            dve.wait_ge(s_x_high, b + 1)
            low_parts(xl, xh, b, "norm_pre", s_x_low)
            if b + 1 < LEAD:
                split(b + 1, b + 1)

        def split_high_low(hi, lo, src, s):
            dve.tensor_copy(hi, src)
            drain()
            tt(lo, src, hi.bitcast(F32), ALU.subtract).then_inc(s, 1)

        def y_sum(q, m):
            c = slice(q * COLS, (q + 1) * COLS)
            tt(yn[:, m, c], ps[:, 2 * (1 - q % 2) + m, :], x1r[:, m, c], ALU.add).then_inc(s_y_summed, 1)

        def evac(kind, k, i, j, done):
            if kind == "qk":
                q = i * 2 + j
                if k < 3:
                    if k == 0:
                        dve.wait_ge(s_conv_first, q + 1)
                    sh = k + 1
                    for jj in range(4):
                        last = stt(out=work[0][:, jj, sh:S], in0=banks(j)[:, jj, 0:S - sh],
                                   scalar=small[:, bass.ds(SMALL["conv_w"][0] + q * 16 + 4 * jj + 3 - sh, 1)],
                                   in1=work[0][:, jj, sh:S], op0=ALU.mult, op1=ALU.add)
                    if k == 2:
                        last.then_inc(psum_free[j], 1)
                        dve.drain().then_inc(s_conv, 1)
                    else:
                        drain()
                if k == 4:
                    dve.wait_ge(s_conv_sigmoid, q + 1)
                    tt(qk[:, bass.ds(q * 4, 4), :], work[0][:, :, :], work[1][:, :, :], ALU.mult).then_inc(s_qk, 1)
            if kind == "z":
                t = work[2]
                if k == 1:
                    dve.wait_ge(s_z_sigmoid, i + 1)
                    tt(t[:, :, :], banks(1), work[1][:, :, :], ALU.mult).then_inc(psum_free[1], 1)
                    drain()
                if k == 2:
                    for jj in range(4):
                        stt(out=t[:, jj, :], in0=work[0][:, jj, :],
                            scalar=small[:, bass.ds(SMALL["mnorm"][0] + i * 4 + jj, 1)],
                            in1=t[:, jj, :], op0=ALU.mult, op1=ALU.mult)
                    drain()
                if k == 3:
                    dve.wait_ge(s_head_kept, i * 2 + 3)
                    tt(t[:, :, :], t[:, :, :], work[3][:, :, :], ALU.mult)
                    drain()
                if k == 4:
                    split_high_low(yh[:, bass.ds(i * 4, 4), :], yl[:, bass.ds(i * 4, 4), :], t[:, :, :], s_y)
                    drain()
            if kind == "u":
                u = upad
                if k == 0:
                    dve.wait_ge(s_u_kept, i + 1)
                    tt(wa[:, :, 1:], u[:, :, 1:], u[:, :, :-1], ALU.add)
                    drain()
                if k == 1:
                    tt(wb[:, 2 - 2 * i:, 3:], wa[:, 2 - 2 * i:, 3:], wa[:, 2 - 2 * i:, 1:-2], ALU.add)
                    drain()
                if k == 2 and i == 1:
                    tt(wa[:, :, 7:], wb[:, :, 7:], wb[:, :, 3:-4], ALU.add)
                    drain()
                    tt(wb[:, 2:, 15:], wa[:, 2:, 15:], wa[:, 2:, 7:-8], ALU.add)
                    drain()
                if k == 3:
                    for gg, win in enumerate((wa, wb)):
                        f = slice(2 * gg, 2 * gg + 2)
                        stt(out=pooled[:, f, :], in0=win[:, f, META:], scalar=1.0 / 2 ** (2 * i + gg + 1),
                            in1=u[:, f, META:], op0=ALU.mult, op1=ALU.subtract)
                        inv = cn("inv", 16 * (2 * i + gg), 16).unsqueeze(1).to_broadcast([P, 2, 16])
                        tt(work[3][:, f, 0:16], win[:, f, META:META + 16], inv, ALU.mult)
                    drain()
                    tt(pooled[:, :, 0:16], work[3][:, :, 0:16], u[:, :, META:META + 16], ALU.subtract).then_inc(
                        s_pool, 1)
                    drain()
            if kind == "zb":
                t = work[2]
                if k == 1:
                    dve.wait_ge(s_zb_sigmoid, i + 1)
                    tt(t[:, :, :], banks(1), work[1][:, :, :], ALU.mult).then_inc(psum_free[1], 1)
                    drain()
                if k == 2:
                    dve.wait_ge(s_pool_mixed, i + 1)
                    for jj in range(4):
                        stt(out=t[:, jj, :], in0=ps[:, 4 + jj // 2, (jj % 2) * S:(jj % 2) * S + S],
                            scalar=sm("pscale", 4 * i + jj, 1), in1=t[:, jj, :], op0=ALU.mult, op1=ALU.mult)
                    drain()
                if k == 3:
                    split_high_low(zh[:, 4 * i:4 * i + 4, :], zl[:, 4 * i:4 * i + 4, :], t[:, :, :], s_yb_done)
                    drain()
            if kind == "pa" and k == 0:
                dve.wait_ge(slots_done, done)
                dve.wait_ge(s_ga, i + 1)
                tt(work[2][:, :, :], banks(1), work[0][:, :, :], ALU.mult).then_inc(psum_free[1], 1)
            if kind == "pb":
                if k == 0:
                    dve.wait_ge(slots_done, done)
                    dve.wait_ge(s_gb, i + 1)
                    tt(work[3][:, :, :], banks(1), work[1][:, :, :], ALU.mult).then_inc(psum_free[1], 1)
                    drain()
                if k == 1:
                    tt(work[2][:, :, :], work[2][:, :, :], work[3][:, :, :], ALU.add)
                    drain()
                if k == 2:
                    split_high_low(mh[:, bass.ds(i * 4, 4), :], ml[:, bass.ds(i * 4, 4), :], work[2][:, :, :], s_merged)
                    drain()
            if kind == "wo" and k == 1:
                q = i * 2 + j
                dve.wait_ge(s_out_squares, q + 1)
                dve.wait_ge(s_post, 16)
                c = slice(q * COLS, (q + 1) * COLS)
                tt(on[:, :, c], ps[:, 2 * j:2 * j + 2, :],
                   postw[:, c].unsqueeze(1).to_broadcast([P, TOK, COLS]), ALU.mult).then_inc(psum_free[j], 1)

            if kind == "cq":
                if k == 2:
                    dve.wait_ge(s_cqs, 1)
                    ts(stat[:, 36:38], stat[:, 36:38], 1.0 / COLS, EPS, ALU.mult, ALU.add).then_inc(s_cqm, 1)
                if k == 4:
                    dve.wait_ge(s_cqr, 1)
                    for m in range(TOK):
                        ts(cqn[:, m, :], cqn[:, m, :], stat[:, 38 + m:39 + m], None, ALU.mult)
                    dve.drain().then_inc(s_cqn, 1)
            if kind == "g" and k == 0:
                dve.wait_ge(slots_done, done)
                dve.tensor_copy(gates[:, bass.ds(i * 4, 4), :], banks(0)).then_inc(s_gsum, 1)
            if kind == "g" and k == (2 if isinstance(i, int) and i == 3 else 4):
                dve.wait_ge(s_gs, i + 1)
                g = gates[:, bass.ds(i * 4, 4), :]
                tt(g, g, work[0][:, :, :], ALU.mult).then_inc(s_gate, 1)
                drain()
            if kind == "w2" and k == 0:
                dve.wait_ge(slots_done, done)
                dve.wait_ge(s_x1_back, 16)
                for m in range(TOK):
                    y_sum(i * 2 + j, m)

        def quarter(p, k, odd, late):
            first = p if isinstance(p, int) else 2
            here = not isinstance(p, int) or p < H
            b, b1 = 64 + 40 * odd, 64 + 40 * (1 - odd)
            segs = ((0, K0), (K0, L2))
            if k == 0 and not late:
                if first >= 1:
                    dve.wait_ge(pair["rstd"], p)
                    tt(stat[:, b1 + 24:b1 + 26], stat[:, b1 + 12:b1 + 16].rearrange("p (t c) -> p t c", c=2)[:, :, 0],
                       stat[:, b1 + 22:b1 + 24], ALU.mult).then_inc(pair["scale"], 1)
                if here:
                    dve.wait_ge(pair["scores_d"], p + 1)
                    for c in range(2):
                        stt(out=sbd[:, c, :], in0=cn("rel"), scalar=const[:, bass.ds(CONST["slope"][0] + p, 1)],
                            in1=ps[:, 2 + c, 0:KEYS], op0=ALU.mult, op1=ALU.add)
                    drain()
                    for t, (lo, w) in enumerate(segs):
                        dve.tensor_reduce(stat[:, b + 2 * t:b + 2 * t + 2], sbd[:, :, lo:lo + w], AX.X, ALU.max)
                    drain()
                    ts(stat[:, b + 4:b + 8], stat[:, b:b + 4], -0.125, None, ALU.mult).then_inc(pair["max_d"], 1)
            if k == 1 and not late:
                if here:
                    dve.wait_ge(pair["exp_d"], p + 1)
                    dve.reciprocal(stat[:, b + 12:b + 16], stat[:, b + 8:b + 12])
                    drain()
                    pairs = stat[:, b + 8:b + 16].rearrange("p (a t c) -> p a t c", a=2, t=2)
                    stt(out=stat[:, b + 16:b + 18], in0=pairs[:, 1, :, 1], scalar=stat[:, 42:43],
                        in1=pairs[:, 0, :, 0], op0=ALU.mult, op1=ALU.mult)
                    drain()
                    for t, (lo, w) in enumerate(segs):
                        stt(out=wmix[:, lo:lo + w], in0=sbd[:, 1, lo:lo + w], scalar=stat[:, b + 16 + t:b + 17 + t],
                            in1=sbd[:, 0, lo:lo + w], op0=ALU.mult, op1=ALU.add)
                    dve.drain().then_inc(pair["mix"], 1)
                if first >= 1:
                    dve.wait_ge(pair["back_m"], p)
                    dve.tensor_copy(oall[:, bass.ds(p + H - 1, 1), :].rearrange("p o s -> p (o s)"),
                                    ps[:, 6, 0:S]).then_inc(pair["out_m"], 1)
                    dve.wait_ge(pair["back_d"], p)
                    ts(oall[:, bass.ds(p - 1, 1), :].rearrange("p o s -> p (o s)"), ps[:, 7, 0:S], sm("subln"), 0.8,
                       ALU.mult, ALU.mult).then_inc(pair["out_d"], 1)
            if k == 1 and late:
                if here:
                    dve.wait_ge(pair["scores_m"], p + 1)
                    tt(pm[odd][:, :], ps[:, 4, 0:KEYS], cn("cmask"), ALU.add)
                    drain()
                    for t, (lo, w) in enumerate(segs):
                        dve.tensor_reduce(stat[:, b + 26 + t:b + 27 + t], pm[odd][:, lo:lo + w], AX.X, ALU.max)
                    drain()
                    ts(stat[:, b + 28:b + 30], stat[:, b + 26:b + 28], -MLA_SCALE, None, ALU.mult).then_inc(
                        pair["max_m"], 1)
            if k == 3 and here and not late:
                dve.wait_ge(pair["exp_m"], p + 1)
                dve.reciprocal(stat[:, b + 32:b + 34], stat[:, b + 30:b + 32]).then_inc(pair["inverse_m"], 1)
                dve.wait_ge(pair["squares"], p + 1)
                ts(stat[:, b + 20:b + 22], stat[:, b + 18:b + 20], 1.0 / P, EPS, ALU.mult, ALU.add).then_inc(
                    pair["mean"], 1)

        def attend(kind, k, i, j):
            if kind == "wo" and j == 0:
                if i == 0 and k == 6:
                    dve.wait_ge(s_meta_squares, 1)
                    ts(stat[0:META, 24:25], stat[0:META, 24:25], 1.0 / D, EPS, ALU.mult, ALU.add).then_inc(s_meta_mean, 1)
                if i == 1 and k == 0:
                    dve.wait_ge(s_meta_rstd, 1)
                    ts(metan[:, :], metan[:, :], stat[0:META, 25:26], None, ALU.mult).then_inc(s_meta_normed, 1)
                if i == 1 and k == 5:
                    dve.wait_ge(s_meta_turned, 1)
                    tt(metat[:, :, :], ps[:, 6, 0:S].rearrange("p (c s) -> p c s", c=KC), spread(sm("attn_norm"), META),
                       ALU.mult).then_inc(s_meta_kept, 1)
            if kind == "ak" and j == 0 and k == 1:
                lp = sm("lambda").rearrange("p (a b d) -> p a b d", a=2, b=2)
                lt = work[3][:, 3, 0:128].rearrange("p (a d) -> p a d", a=2)
                tt(lt, lp[:, :, 0, :], lp[:, :, 1, :], ALU.mult)
                drain()
                dve.tensor_reduce(stat[:, 40:42], lt, AX.X, ALU.add).then_inc(s_l1, 1)
            if kind == "ak" and j == 0 and k == 7:
                dve.wait_ge(s_l2, 1)
                tt(stat[:, 42:43], stat[:, 41:42], stat[:, 40:41], ALU.subtract)
                drain()
                ts(stat[:, 42:43], stat[:, 42:43], -LAM0, None, ALU.add).then_inc(s_lam, 1)
            if kind == "ak" and j == 0 and k == 3:
                dve.wait_ge(s_cksum, 1)
                ts(stat[:, 30:33], ps[:, 5, 0:3], 1.0 / S, EPS, ALU.mult, ALU.add).then_inc(s_ckm, 1)
            if kind == "ak" and j == 0 and k == 5:
                dve.wait_ge(s_ckr, 1)
                for m, (t, w) in enumerate(((0, P), (P, P), (2 * P, META))):
                    ts(diagk[:, t:t + w], ident[:, P - w:P], stat[:, 33 + m:34 + m], None, ALU.mult)
                dve.drain().then_inc(s_ckd, 1)
            if kind == "ak" and j == 1 and k == 1:
                dve.wait_ge(s_ckb, 1)
                f = [work[2 + c][:, 0:2, :].rearrange("p a s -> p (a s)")[:, 0:L2] for c in range(2)]
                for c in range(2):
                    stt(out=f[c], in0=ckvf[:, c, :], scalar=sm("kvnorm", c, 1), in1=ps[:, 6, 0:L2],
                        op0=ALU.mult, op1=ALU.mult)
                drain()
                for c in range(2):
                    dve.tensor_copy(ckh[:, c, 0:L2], f[c])
                    for t in (ckh, ckl):
                        ts(t[:, c, L2:KVP], ident[:, 0:KVP - L2], 0.0, None, ALU.mult)
                drain()
                for c in range(2):
                    tt(ckl[:, c, 0:L2], f[c], ckh[:, c, 0:L2].bitcast(F32), ALU.subtract)
                dve.drain().then_inc(s_ckl, 1)
            if kind == "av" and j == 0 and k == 5:
                dve.wait_ge(s_krm, 1)
                f = work[2][:, 0:2, :].rearrange("p a s -> p (a s)")[:, 0:L2]
                tt(f, ps[:, 7, 0:L2], cn("sin"), ALU.mult)
                tt(kpe[:, :], ckvf[:, 2, :], cn("cos"), ALU.mult)
                drain()
                tt(kpe[:, :], kpe[:, :], f, ALU.add).then_inc(s_kpe, 1)
                drain()
            if kind == "av" and j == 0 and k == 6:
                dve.wait_ge(s_cqt, 1)
                tt(work[2][:, :, :], ps[:, 5:7, :].rearrange("p b (j s) -> p (b j) s", j=2), spread(sm("qnorm"), S),
                   ALU.mult)
                drain()
                split_high_low(cqh[:, :, :], cql[:, :, :], work[2][:, :, :], s_cql)
            if kind == "aq" and k == 5:
                dve.wait_ge(s_avm, j + 1)
                if j == 0:
                    dve.wait_ge(s_xkept, 16)
                c = slice(j * COLS, (j + 1) * COLS)
                dve.tensor_copy(avn[:, 0:2, c], ps[:, 4:6, :])
                dve.tensor_copy(avn[0:META, 2, c], ps[0:META, 6, :])
                dve.drain().then_inc(s_avn, 1)
            if kind == "uk" and j == 1 and k == 0:
                dve.wait_ge(s_qpm, 1)
                wide = [P, 4, S]
                tt(work[2][:, :, :], ps[:, 4:6, :].rearrange("p b (j s) -> p (b j) s", j=2),
                   cn("sin", META, S).unsqueeze(1).to_broadcast(wide), ALU.mult)
                tt(qp[:, :, :], work[1][:, :, :], cn("cos", META, S).unsqueeze(1).to_broadcast(wide), ALU.mult)
                drain()
                tt(qp[:, :, :], qp[:, :, :], work[2][:, :, :], ALU.add).then_inc(s_qp, 1)
            if kind == "g":
                quarter(i * 2 + k // 4, k % 4, k // 4, False)
            if kind == "w2" and i == 0 and j == 0 and k < 2:
                quarter(H, k, 0, False)
            if kind == "g" and isinstance(i, int) and i == 3 or kind == "w2" and i == 0 and j == 0:
                for turn, b in enumerate(OUT_ORDER):
                    if (kind, k) == LOW_AT[turn]:
                        c = slice(4 * b, 4 * b + 4)
                        dve.wait_ge(s_out_high, turn + 1)
                        tt(ol[:, c, :], gates[:, c, :], oh[:, c, :].bitcast(F32), ALU.subtract).then_inc(s_out_low, 1)
            if kind == "qk" and isinstance(i, int) and j == 0 and k == 5:
                dve.wait_ge(s_wgh, 1)
                tt(wgl[:, :, :], wg[:, :, :], wgh[:, :, :].bitcast(F32), ALU.subtract).then_inc(s_wgl, 1)
            if kind == "v" and i == 0 and j == 0 and k == 2:
                dve.wait_ge(s_gate_sums, 1)
                dve.tensor_copy(rows[:, 0, :], ps[0:H, 4, 0:S])
                dve.tensor_copy(rows[:, 5, :], ps[32:GATE_W, 4, 0:S])
                dve.drain().then_inc(s_gate_rows, 1)
            if kind == "v" and i == 1 and j == 0 and k == 3:
                dve.wait_ge(s_gate_log, 1)
                ts(rows[:, 2, :], rows[:, 5, :], sm("fbias")[0:H, :], 0.0, ALU.add, ALU.min)
                drain()
                dve.memset(rows[:, 5, :], 0.0)
                drain()
                tt(rows[:, 2, :], rows[:, 2, :], rows[:, 1, :], ALU.subtract)
                drain()
                dve.tensor_tensor_scan(rows[:, 3, :], rows[:, 5, :], rows[:, 2, :], 0.0, ALU.add, ALU.add)
                drain()
                tt(rows[:, 4, :], rows[:, 0, :], rows[:, 3, :], ALU.subtract)
                drain()
                dve.tensor_tensor_scan(rows[:, 1, :], rows[:, 5, :], rows[:, 4, :], 0.0, ALU.add, ALU.max)
                drain()
                tt(rows[:, 2, :], rows[:, 3, :], rows[:, 1, :], ALU.add)
                ts(rows[:, 0, :], rows[:, 1, :], -1.0, None, ALU.mult)
                dve.drain().then_inc(s_gate_scanned, 1)
            if kind == "o" and isinstance(i, int) and k == 0:
                dve.wait_ge(s_gate_turned, 1)
                dve.tensor_copy(stat[:, 32:64], ps[:, 6, 0:32]).then_inc(s_gate_columns, 1)
                drain()
            if kind in ("o", "z"):
                h = i * 2 + j
                if k == 1:
                    dve.wait_ge(s_head_scores, h + 1)
                    for st in range(TOK):
                        w = S - st * P
                        stt(out=darg[:, st * S:st * S + w], in0=ps[:, 4, st * P:S],
                            scalar=stat[:, bass.ds(h + 32 + 8 * st, 1)], in1=cn("dmask", st * S, w),
                            op0=ALU.add, op1=ALU.min)
                    dve.drain().then_inc(s_head_exponent, 1)
                if k == 2:
                    dve.wait_ge(s_head_decay, h + 1)
                    stt(out=pt[:, :], in0=ps[:, 5, 0:384], scalar=HD ** -0.5, in1=dmat[:, :],
                        op0=ALU.mult, op1=ALU.mult).then_inc(s_head_weights, 1)
                if k == 4:
                    dve.wait_ge(s_head_sums, h + 1)
                    for m in range(TOK):
                        stt(out=stat[:, m:m + 1], in0=ps[:, 6 + m, HD:VW], scalar=-1.0,
                            in1=stat[:, bass.ds(h + 48 + 8 * m, 1)], op0=ALU.mult, op1=ALU.max)
                    drain()
                    tt(stat[:, 0:2].unsqueeze(2), stat[:, 0:2].unsqueeze(2), ps[:, 6:8, HD:VW], ALU.max)
                    drain()
                    dve.reciprocal(stat[:, 2:4], stat[:, 0:2]).then_inc(s_head_denominator, 1)
                if k == 5:
                    dve.wait_ge(s_head_squares, h + 1)
                    ts(stat[:, 6:8], stat[:, 4:6], 1.0 / HD, EPS, ALU.mult, ALU.add).then_inc(s_head_mean, 1)
                if k == 6:
                    dve.wait_ge(s_head_rstd, h + 1)
                    tt(stat[:, 10:12], stat[:, 2:4], stat[:, 8:10], ALU.mult)
                    drain()
                    for m in range(TOK):
                        ts(hn[:, m, :], ps[:, 6 + m, 0:HD], stat[:, 10 + m:11 + m], None, ALU.mult)
                    dve.drain().then_inc(s_head_normed, 1)

        def row_mean(m, s):
            dve.tensor_reduce(stat[:, 20 + m:21 + m], stat[:, 12 + 4 * m:16 + 4 * m], AX.X, ALU.add)
            drain()
            ts(stat[:, 20 + m:21 + m], stat[:, 20 + m:21 + m], 1.0 / D, EPS, ALU.mult, ALU.add).then_inc(s, 1)

        def between():
            c3 = slice(3 * COLS, D)

            def mean(m):
                dve.wait_ge(s_out_squares, 4 + m)
                row_mean(m, s_out_mean)
                tt(on[:, m, c3], ps[:, 2 + m, :], postw[:, c3], ALU.mult)
                if m == 1:
                    dve.drain().then_inc(psum_free[1], 1)
                else:
                    drain()

            def x1_rows(m):
                dve.wait_ge(s_out_rstd, m + 1)
                for q in (slice(0, D // 2), slice(D // 2, D)):
                    stt(out=xr[:, m, q], in0=on[:, m, q], scalar=stat[:, 22 + m:23 + m], in1=xr[:, m, q],
                        op0=ALU.mult, op1=ALU.add).then_inc(s_x1, 1)

            def x1_scale(m):
                dve.wait_ge(s_x1_squares, 2 * m + 2)
                ts(stat[:, 26 + m:27 + m], stat[:, 44 + 2 * m:45 + 2 * m], stat[:, 45 + 2 * m:46 + 2 * m], EPS,
                   ALU.add, ALU.add).then_inc(s_x1_mean, 1)
                dve.wait_ge(s_x1_rstd, m + 1)
                ts(diag[:, m, :], ident, stat[:, 28 + m:29 + m], None, ALU.mult).then_inc(s_x1_normed, 1)

            n = FIRST["CKQ"]
            dve.wait_ge(s_x_again, 16)
            mean(0)
            x1_rows(0)
            mean(1)
            x1_scale(0)
            x1_rows(1)
            split(n, n % RING)
            x1_scale(1)
            split(n + 1, (n + 1) % RING)
            split(n + 2, (n + 2) % RING)
            dve.tensor_copy(x2h[:, :, 0:META], metat[:, :, :])
            drain()
            tt(x2l[:, :, 0:META], metat[:, :, :], x2h[:, :, 0:META].bitcast(F32), ALU.subtract)
            for b in range(4):
                dve.wait_ge(s_x2_high, b + 1)
                low_parts(x2l[:, :, META:L2], x2h[:, :, META:L2], b, "attn_norm", s_x2_low)

        def attend_late(kind, k, i, j):
            if kind == "g":
                quarter(i * 2 + k // 4, k % 4, k // 4, True)
            if kind == "w2" and i == 0 and j == 0 and k < 2:
                quarter(H, k, 0, True)
            if kind == "g" and isinstance(i, int) and i == 3 or kind == "w2" and i == 0 and j == 0:
                for turn, b in enumerate(OUT_ORDER):
                    c = slice(4 * b, 4 * b + 4)
                    if (kind, k) == HIGH_AT[turn]:
                        drain()
                        tt(gates[:, c, :], gates[:, c, :], oall[:, c, :], ALU.mult).then_inc(s_out_gated, 1)

        run(dve, split, evac, attend, attend_late, {"CKQ": between})

        for m in range(TOK):
            if m == 0:
                dve.wait_ge(s_tile, 2)
            else:
                dve.wait_ge(slots_done, SLOTS)
            y_sum(3, m)
            dve.wait_ge(s_y_squares, 2 * 3 + m + 1)
            row_mean(m, s_y_mean)
            dve.wait_ge(s_y_rstd, m + 1)
            dve.wait_ge(s_final_w_in, 16)
            for q in (slice(0, D // 2), slice(D // 2, D)):
                stt(out=yn[:, m, q], in0=yn[:, m, q], scalar=stat[:, 22 + m:23 + m], in1=finalw[:, q],
                    op0=ALU.mult, op1=ALU.mult).then_inc(s_y_scaled, 1)

    @block.gpsimd
    def _(pool):
        pool.memset(vn[:, :, :].rearrange("p m (h d) -> p m h d", h=H)[:, :, :, HD:VW], 1.0).then_inc(s_one, 1)
        half = sm("half", 0, 2)
        pool.wait_ge(s_small, 16)
        for m in range(TOK):
            pool.wait_ge(s_x_mean, m + 1)
            pool.tensor_tensor(stat[:, 2 + m:3 + m], stat[:, m:m + 1], half[:, 0:1], ALU.pow).then_inc(s_rstd, 1)

        def set_down(h):
            e = small[0:H, bass.ds(SMALL["ident"][0] + h, 1)]
            pool.tensor_tensor(mrow[:, :], rows[:, 0, :], e.to_broadcast([H, S]), ALU.mult).then_inc(s_head_keys, 1)
            pool.tensor_copy(kst[:, :, :], qk[:, bass.ds(h * 2 + KC, 2), :]).then_inc(s_head_keys, 1)

        def rstd(h):
            pool.wait_ge(s_head_mean, h + 1)
            pool.tensor_tensor(stat[:, 8:10], stat[:, 6:8], half, ALU.pow).then_inc(s_head_rstd, 1)

        pool.wait_ge(s_gate_bound, 1)
        pool.wait_ge(s_qk, 8)
        pool.wait_ge(s_const, 16)
        set_down(0)
        with pool.Fori(0, H - 1) as h:
            pool.wait_ge(s_head_scores, h + 1)
            set_down(h + 1)
            rstd(h)
        pool.wait_ge(s_head_scores, H)
        pool.memset(upad[:, :, 0:META], 0.0).then_inc(s_pad, 1)
        pool.dma_start(poolw[:, :, :], pool_w).then_inc(s_pool_w_in, 16)
        rstd(H - 1)
        pool.wait_ge(slots_done, FIRST["WO"])
        pool.dma_start(postw[:, :], post_w).then_inc(s_post, 16)
        pool.dma_start(xr[:, :, :], x.rearrange("(m p) d -> p m d", p=P)).then_inc(s_x_again, 16)
        pool.dma_start(metan[:, :], meta).then_inc(s_meta, 16)
        pool.wait_ge(s_meta_mean, 1)
        pool.tensor_tensor(stat[0:META, 25:26], stat[0:META, 24:25], sm("half", 0, 1)[0:META, :],
                           ALU.pow).then_inc(s_meta_rstd, 1)
        for m in range(TOK):
            pool.wait_ge(s_out_mean, m + 1)
            pool.tensor_tensor(stat[:, 22 + m:23 + m], stat[:, 20 + m:21 + m], half[:, 0:1], ALU.pow).then_inc(s_out_rstd, 1)
        for m in range(TOK):
            pool.wait_ge(s_x1_mean, m + 1)
            pool.tensor_tensor(stat[:, 28 + m:29 + m], stat[:, 26 + m:27 + m], half[:, 0:1], ALU.pow).then_inc(s_x1_rstd, 1)
        pool.wait_ge(s_x1, 4)
        pool.dma_start(x1_dram, xr[:, :, :]).then_inc(s_xkept, 16)
        const3 = sm("half", 0, 3)
        pool.wait_ge(s_cqm, 1)
        pool.tensor_tensor(stat[:, 38:40], stat[:, 36:38], half, ALU.pow).then_inc(s_cqr, 1)
        pool.wait_ge(s_ckm, 1)
        pool.tensor_tensor(stat[:, 33:36], stat[:, 30:33], const3, ALU.pow).then_inc(s_ckr, 1)

        def set_queries(p):
            pool.tensor_copy(qst[1][:, :], qn[:, bass.ds(p, 1), :].rearrange("p o s -> p (o s)")).then_inc(
                pair["queries"], 1)
            pool.drain()
            for b in range(2):
                r = slice(64 * b, 64 * b + 64)
                pool.tensor_copy(qhalf[b][r, :], aq[r, bass.ds(p, 1), :].rearrange("p o s -> p (o s)")).then_inc(
                    pair["queries"], 1)
            pool.drain()

        def set_rotated(t):
            pool.tensor_copy(qst[2][:, :], qp[:, bass.ds(t, 1), :].rearrange("p o s -> p (o s)")).then_inc(
                pair["queries"], 1)

        def pair_rstd(p, odd):
            b = 64 + 40 * odd
            pool.wait_ge(pair["mean"], p + 1)
            pool.tensor_tensor(stat[:, b + 22:b + 24], stat[:, b + 20:b + 22], half, ALU.pow).then_inc(pair["rstd"], 1)

        pool.wait_ge(s_qp, 1)
        pool.memset(qhalf[0][64:P, :], 0.0)
        pool.memset(qhalf[1][0:64, :], 0.0)
        pool.drain()
        set_queries(0)
        set_rotated(0)
        with pool.Fori(0, H // 2 - 1) as q:
            pool.wait_ge(pair["scores_m"], q * 2 + 1)
            set_queries(q * 2 + 1)
            set_rotated(q)
            pair_rstd(q * 2, 0)
            pool.wait_ge(pair["scores_m"], q * 2 + 2)
            set_queries(q * 2 + 2)
            set_rotated(q + 1)
            pair_rstd(q * 2 + 1, 1)
        pool.wait_ge(pair["scores_m"], H - 1)
        set_queries(H - 1)
        set_rotated(H // 2 - 1)
        pair_rstd(H - 2, 0)
        pool.wait_ge(pair["scores_m"], H)
        pool.dma_start(finalw[:, :], final_w).then_inc(s_final_w_in, 16)
        pair_rstd(H - 1, 1)
        pool.wait_ge(pair["sums_m"], H)
        pool.dma_start(x1r[:, :, :], x1_dram).then_inc(s_x1_back, 16)
        for m in range(TOK):
            pool.wait_ge(s_y_mean, m + 1)
            pool.tensor_tensor(stat[:, 22 + m:23 + m], stat[:, 20 + m:21 + m], half[:, 0:1], ALU.pow).then_inc(s_y_rstd, 1)


def small_array(v):
    a = np.zeros((P, SMALL_W), np.float32)

    def put(name, m):
        lo, hi = SMALL[name]
        a[:m.shape[0], lo:hi] = m

    put("norm_pre", v["norm_pre_w"].reshape(KC, P).T)
    put("conv_w", v["qk_conv_w"].reshape(4, 2 * KC, P).transpose(2, 1, 0).reshape(P, 128))
    put("conv_b", v["qk_conv_b"].reshape(2 * KC, P).T)
    put("mnorm", v["mlstm_norm_w"].reshape(KC, P).T)
    put("pscale", v["pool_scale"].reshape(8, P).T)
    put("attn_norm", v["attn_norm_w_2"].reshape(KC, P).T)
    put("qnorm", v["mla_q_norm_w_2"].reshape(4, P).T)
    put("kvnorm", v["mla_kv_norm_w_2"].reshape(2, P).T)
    put("subln", v["diff_subln_w_2"].reshape(1, P).T)
    put("ibias", v["mlstm_i_bias"].reshape(1, H).T)
    put("fbias", v["mlstm_f_bias"].reshape(1, H).T)
    put("ident", np.eye(P))
    put("half", np.full((P, 4), -0.5))
    put("lambda", np.tile(v["diff_lambda_2"].reshape(1, 256), (P, 1)))
    return a


def gates_array(w):
    a = np.zeros((P, KC, GATE_W), np.float32)
    w = w.reshape(KC, P, 2 * H).transpose(1, 0, 2)
    a[:, :, 0:H], a[:, :, 32:GATE_W] = w[:, :, 0:H], w[:, :, H:]
    return a


def const_array():
    a = np.zeros((P, CONST_W), np.float32)

    def put(name, m):
        lo, hi = CONST[name]
        a[:m.shape[0], lo:hi] = m

    far = -1e30
    put("ones", np.ones((P, P)))
    key, tok = np.arange(S)[:, None], np.arange(S)[None, :]
    seen = np.where(key <= tok, 0.0, far)
    put("dmask", np.concatenate([seen[:P, :], seen[P:, P:]], 1))
    inv = np.stack([1.0 / np.minimum(np.arange(1, 17), w) for w in (2, 4, 8, 16)]).reshape(1, 64)
    put("inv", np.tile(inv, (P, 1)))
    pos, kpos = META + np.arange(S)[:, None], np.arange(L2)[None, :]
    rel = np.where(kpos <= pos, kpos - pos, far)
    mask = np.where(kpos <= pos, 0.0, far)
    put("rel", np.concatenate([rel[:P, :K0], rel[P:, :]], 1))
    put("cmask", np.concatenate([mask[:P, :K0], mask[P:, :]], 1))
    slopes = np.exp2(-np.arange(1, 9, dtype=np.float32)) * 8.0
    put("slope", np.tile(slopes, (P, 1)))
    half = 32
    ang = (np.arange(L2, dtype=np.float32)[None, :]
           * (np.float32(10000.0) ** (-np.arange(half, dtype=np.float32) / half))[:, None]).astype(np.float32)
    put("cos", np.tile(np.cos(ang), (4, 1)))
    put("sin", np.tile(np.sin(ang), (4, 1)))
    r = np.zeros((P, P))
    for b in (0, 64):
        for f in range(half):
            r[b + half + f, b + f] = -1.0
            r[b + f, b + half + f] = 1.0
    put("rot", r)
    return a


def stream_array(v):
    def groups(w):
        k, n = w.shape
        return w.reshape(k // (SLOT_KC * P), SLOT_KC, P, n // COLS, COLS).transpose(3, 0, 2, 1, 4)

    w_in, w2 = v["w_in"].reshape(D, -1), v["w_in_2"].reshape(D, -1)
    cuts = np.cumsum([0, D, D, D, D, D, H, H, D // 2, D // 2, D, D])
    q, k, vv, o, z, _, _, u, zb, ga, gb = (groups(w_in[:, a:b]) if b - a >= COLS else None
                                           for a, b in zip(cuts, cuts[1:]))
    pa, pb = groups(v["w_proj_mlstm"].reshape(D, D)), groups(v["w_proj_pool"].reshape(D // 2, D))
    wo = groups(v["w_out"].reshape(D, D))
    aq, ak, av, ag = (groups(w2[:, i * 1024:(i + 1) * 1024]) for i in range(4))
    cq, bg = groups(w2[:, 4096:4608]), groups(w2[:, 4928:5952])
    kr = w2[:, 4864:4928]
    ckv = groups(np.concatenate([w2[:, 4608:4864], kr, kr, np.zeros((D, 128), w2.dtype)], 1))
    uq = v["w_uq_2"].reshape(512, H, 192)
    uqn, uqr = groups(uq[:, :, :P].reshape(512, 1024)), groups(uq[:, :, P:].reshape(512, 512))
    ukv = v["w_ukv_2"].reshape(256, H, 2, P)
    uk, uv = groups(ukv[:, :, 0].reshape(256, 1024)), groups(ukv[:, :, 1].reshape(256, 1024))
    w2o = groups(v["w_out_2"].reshape(4, D // 4, D)[list(OUT_ORDER)].reshape(D, D))
    order = [*q, *k, *vv]
    for i in range(4):
        order += [o[i], z[i]]
    for i in range(2):
        order += [u[i], zb[i]]
    for i in range(4):
        order += [ga[i], pa[i], gb[i], pb[i]]
    order += [*wo, *cq, *ckv, *ak, *av, *aq, *uqn, *uqr, *uk, *uv, *ag, *bg, *w2o]
    return np.concatenate(order)


def kernel(**v):
    from contextlib import ExitStack

    import concourse.bacc as bacc
    from concourse.bass_utils import run_bass_kernel_spmd

    v = {name: np.asarray(a) for name, a in v.items()}
    w_in = v["w_in"].reshape(D, -1)
    arrays = {
        "x": v["x"].reshape(S, D),
        "meta": v["meta_tokens_2"],
        "w_stream": stream_array(v),
        "w_gates": gates_array(w_in[:, 5 * D:5 * D + 2 * H]),
        "pool_w": np.ascontiguousarray(v["pool_w"].reshape(4, 2, P, HD).transpose(2, 0, 1, 3).reshape(P, 8, HD)),
        "small": small_array(v),
        "const": const_array(),
        "post_w": np.tile(v["norm_post_w"].reshape(1, D), (P, 1)),
        "final_w": np.tile(v["final_norm_w_2"].reshape(1, D), (P, 1)),
    }
    nc = bacc.Bacc("TRN2", target_bir_lowering=False, num_devices=1)
    args = [nc.dram_tensor(f"in_{name}", a.shape, mybir.dt.from_np(a.dtype), kind="ExternalInput").ap()
            for name, a in arrays.items()]
    out = nc.dram_tensor("out", (S, D), F32, kind="ExternalOutput").ap()
    with ExitStack() as ctx:
        build_program(nc, ctx, *args, out)
    r = run_bass_kernel_spmd(nc, [{f"in_{name}": a for name, a in arrays.items()}], core_ids=[0])
    return r.results[0]["out"].reshape(1, S, D)
```
